# Optimizing a Trainium2 kernel written in Bass

```python
import math
import jax, jax.numpy as jnp
from jax import lax
import numpy as np

D_MODEL = 1024
BATCH = 1
SEQ = 512
DEPTH = 1

ATTN_HEADS = 8
ATTN_HEAD_DIM = D_MODEL // 16
ATTN_WIDTH = ATTN_HEADS * ATTN_HEAD_DIM
RET_HEADS = 4
RET_HEAD_DIM = D_MODEL // 8
RET_WIDTH = RET_HEADS * RET_HEAD_DIM
MIX_WIDTH = ATTN_WIDTH + RET_WIDTH
N_IN_SLICES = 7
MOBA_BLOCK = 256
MOBA_TOPK = 3
Q_BLOCK = 128
RET_CHUNK = 256
REL_BUCKETS = 32
REL_MAX_DIST = 128
ROPE_BASE = 10000.0
N_GROUPS = 4
EXPERTS_PER_GROUP = 8
N_EXPERTS = N_GROUPS * EXPERTS_PER_GROUP
D_EXPERT = D_MODEL // 2
TOP_K_INNER = 2
ALPHA = (2.0 * DEPTH) ** 0.25
BETA = (8.0 * DEPTH) ** -0.25
LN_EPS = 1e-5

kernel_name = "hymba_moba_retnet_hmoe_deepnorm"

def layer_norm(x, g, b):
    xf = x.astype(jnp.float32)
    mu = jnp.mean(xf, -1, keepdims=True)
    var = jnp.mean(jnp.square(xf - mu), -1, keepdims=True)
    return ((xf - mu) * lax.rsqrt(var + LN_EPS) * g + b).astype(x.dtype)

def rms_norm(x, g):
    xf = x.astype(jnp.float32)
    return (xf * lax.rsqrt(jnp.mean(jnp.square(xf), -1, keepdims=True) + LN_EPS) * g).astype(x.dtype)

def t5_bucket(dist):
    n = jnp.maximum(dist, 0)
    max_exact = REL_BUCKETS // 2
    nf = jnp.maximum(n, 1).astype(jnp.float32)
    large = max_exact + (jnp.log(nf / max_exact) / math.log(REL_MAX_DIST / max_exact)
                         * (REL_BUCKETS - max_exact)).astype(jnp.int32)
    large = jnp.minimum(large, REL_BUCKETS - 1)
    return jnp.where(n < max_exact, n, large)

def rope(t, pos):
    half = t.shape[-1] // 2
    inv = ROPE_BASE ** (-jnp.arange(half, dtype=jnp.float32) / half)
    ang = pos[:, None].astype(jnp.float32) * inv[None, :]
    cos, sin = jnp.cos(ang), jnp.sin(ang)
    tf = t.astype(jnp.float32)
    t1, t2 = tf[..., :half], tf[..., half:]
    return jnp.concatenate([t1 * cos - t2 * sin, t1 * sin + t2 * cos], -1).astype(t.dtype)

def moba_attention(q, k, v, rel_table):
    B, H, S, Dh = q.shape
    L = MOBA_BLOCK
    nb = S // L
    topk = min(MOBA_TOPK, nb)
    scale = Dh ** -0.5
    k_blk = k.reshape(B, H, nb, L, Dh)
    v_blk = v.reshape(B, H, nb, L, Dh)
    k_mean = jnp.mean(k_blk.astype(jnp.float32), axis=3)
    n_chunks = S // Q_BLOCK
    q_chunks = q.reshape(B, H, n_chunks, Q_BLOCK, Dh).transpose(2, 0, 1, 3, 4)
    table_t = rel_table.astype(jnp.float32).T
    head_idx = jnp.arange(H)[None, :, None, None, None]
    gather = jax.vmap(jax.vmap(lambda kb, idx: kb[idx]))

    def one_chunk(args):
        qc, c = args
        q_pos = c * Q_BLOCK + jnp.arange(Q_BLOCK)
        own = (c * Q_BLOCK) // L
        gate = jnp.einsum('bhqd,bhnd->bhqn', qc.astype(jnp.float32), k_mean)
        gate = jnp.where(jnp.arange(nb) < own, gate, -jnp.inf)
        _, sel = lax.top_k(gate, topk)
        sel_valid = sel < own
        k_sel = gather(k_blk, sel)
        v_sel = gather(v_blk, sel)
        s_sel = jnp.einsum('bhqd,bhqtld->bhqtl', qc, k_sel).astype(jnp.float32) * scale
        k_pos_sel = sel[..., None] * L + jnp.arange(L)
        bucket_sel = t5_bucket(q_pos[None, None, :, None, None] - k_pos_sel)
        s_sel = s_sel + table_t[head_idx, bucket_sel]
        s_sel = jnp.where(sel_valid[..., None], s_sel, -jnp.inf)
        start = own * L
        k_own = lax.dynamic_slice_in_dim(k, start, L, axis=2)
        v_own = lax.dynamic_slice_in_dim(v, start, L, axis=2)
        s_own = jnp.einsum('bhqd,bhld->bhql', qc, k_own).astype(jnp.float32) * scale
        dist_own = q_pos[:, None] - (start + jnp.arange(L))[None, :]
        s_own = s_own + table_t[:, t5_bucket(dist_own)][None]
        s_own = jnp.where(dist_own[None, None] >= 0, s_own, -jnp.inf)
        logits = jnp.concatenate([s_sel.reshape(B, H, Q_BLOCK, topk * L), s_own], -1)
        p = jax.nn.softmax(logits, axis=-1)
        p_sel = p[..., :topk * L].reshape(B, H, Q_BLOCK, topk, L).astype(v.dtype)
        p_own = p[..., topk * L:].astype(v.dtype)
        return (jnp.einsum('bhqtl,bhqtld->bhqd', p_sel, v_sel)
                + jnp.einsum('bhql,bhld->bhqd', p_own, v_own))

    out = lax.map(one_chunk, (q_chunks, jnp.arange(n_chunks)))
    return out.transpose(1, 2, 0, 3, 4).reshape(B, H, S, Dh)

def retention_chunkwise(q, k, v):
    B, H, S, Dk = q.shape
    Dv = v.shape[-1]
    C = RET_CHUNK
    n = S // C
    gammas = 1.0 - jnp.exp(jnp.linspace(math.log(1.0 / 32), math.log(1.0 / 512), H, dtype=jnp.float32))
    log_g = jnp.log(gammas)
    idx = jnp.arange(C, dtype=jnp.float32)
    diff = idx[:, None] - idx[None, :]
    decay_inner = jnp.where(diff[None] >= 0, jnp.exp(jnp.maximum(diff, 0.0)[None] * log_g[:, None, None]), 0.0)
    q_decay = jnp.exp((idx[None, :] + 1.0) * log_g[:, None])[None, :, :, None]
    k_decay = jnp.exp((C - 1.0 - idx[None, :]) * log_g[:, None])[None, :, :, None]
    chunk_decay = jnp.exp(C * log_g)[None, :, None, None]

    def to_chunks(t):
        return t.astype(jnp.float32).reshape(B, H, n, C, t.shape[-1]).transpose(2, 0, 1, 3, 4)

    def step(R, xs):
        qi, ki, vi = xs
        s = jnp.einsum('bhqd,bhkd->bhqk', qi, ki) * decay_inner
        inner = jnp.einsum('bhqk,bhkv->bhqv', s, vi)
        cross = jnp.einsum('bhqd,bhdv->bhqv', qi * q_decay, R)
        R = R * chunk_decay + jnp.einsum('bhkd,bhkv->bhdv', ki * k_decay, vi)
        return R, inner + cross

    R0 = jnp.zeros((B, H, Dk, Dv), jnp.float32)
    _, out = lax.scan(step, R0, (to_chunks(q), to_chunks(k), to_chunks(v)))
    return out.transpose(1, 2, 0, 3, 4).reshape(B, H, S, Dv)

def hybrid_mixer(h, w_in, attn_out_gain, rel_table, w_out):
    B, S, _ = h.shape
    proj = jnp.einsum('bsd,de->bse', h, w_in)
    pad = (-S) % MOBA_BLOCK
    proj = jnp.pad(proj, ((0, 0), (0, pad), (0, 0)))
    Sp = S + pad
    aq, ak, av, rq, rk, rv, rg = jnp.split(proj, N_IN_SLICES, axis=-1)

    def heads(t, nh):
        return t.reshape(B, Sp, nh, -1).transpose(0, 2, 1, 3)

    attn = moba_attention(heads(aq, ATTN_HEADS), heads(ak, ATTN_HEADS), heads(av, ATTN_HEADS), rel_table)
    attn = rms_norm(attn.transpose(0, 2, 1, 3).reshape(B, Sp, ATTN_WIDTH), attn_out_gain)
    pos = jnp.arange(Sp)
    rqh = rope(heads(rq, RET_HEADS), pos)
    rkh = rope(heads(rk, RET_HEADS), pos) * (RET_HEAD_DIM ** -0.5)
    ret = retention_chunkwise(rqh, rkh, heads(rv, RET_HEADS))
    mu = jnp.mean(ret, -1, keepdims=True)
    var = jnp.mean(jnp.square(ret - mu), -1, keepdims=True)
    ret = (ret - mu) * lax.rsqrt(var + LN_EPS)
    ret = ret.transpose(0, 2, 1, 3).reshape(B, Sp, RET_WIDTH)
    ret = (jax.nn.silu(rg.astype(jnp.float32)) * ret).astype(h.dtype)
    cat = jnp.concatenate([attn, ret], -1)[:, :S]
    return jnp.einsum('bse,ed->bsd', cat, w_out)

def hierarchical_moe(x2d, w_rg, b_rg, w_re, b_re, w_gu, w_dn):
    T, D = x2d.shape
    g_prob = jax.nn.softmax((x2d @ w_rg).astype(jnp.float32) + b_rg.astype(jnp.float32), axis=-1)
    g_p, g_idx = lax.top_k(g_prob, 1)
    e_logits = ((x2d @ w_re).astype(jnp.float32) + b_re.astype(jnp.float32)).reshape(T, N_GROUPS, EXPERTS_PER_GROUP)
    e_logits = jnp.take_along_axis(e_logits, jnp.broadcast_to(g_idx[:, :, None], (T, 1, EXPERTS_PER_GROUP)), axis=1)[:, 0]
    e_prob = jax.nn.softmax(e_logits, axis=-1)
    e_p, e_idx = lax.top_k(e_prob, TOP_K_INNER)
    e_p = e_p / jnp.sum(e_p, -1, keepdims=True)
    weights = g_p * e_p
    flat_e = (g_idx * EXPERTS_PER_GROUP + e_idx).reshape(-1)
    order = jnp.argsort(flat_e)
    xs = x2d[order // TOP_K_INNER]
    sizes = jnp.bincount(flat_e, length=N_EXPERTS).astype(jnp.int32)
    gu = lax.ragged_dot(xs, w_gu, sizes)
    hid = jax.nn.silu(gu[:, :D_EXPERT]) * gu[:, D_EXPERT:]
    y = lax.ragged_dot(hid, w_dn, sizes)
    y = jnp.zeros_like(y).at[order].set(y).reshape(T, TOP_K_INNER, D)
    return jnp.sum(y * weights[..., None].astype(y.dtype), axis=1)

def setup_inputs(seed: int = 0) -> dict:
    key = jax.random.key(seed)
    ks = jax.random.split(key, 16)
    f32 = jnp.float32
    x = jax.random.normal(ks[0], (BATCH, SEQ, D_MODEL), f32)
    w_in = jax.random.normal(ks[1], (DEPTH, D_MODEL, N_IN_SLICES * ATTN_WIDTH), f32) * D_MODEL ** -0.5
    col = jnp.arange(N_IN_SLICES * ATTN_WIDTH) // ATTN_WIDTH
    v_cols = (col == 2) | (col == 5)
    w_in = w_in * jnp.where(v_cols, BETA, 1.0).astype(f32)
    attn_out_gain = 1.0 + 0.02 * jax.random.normal(ks[2], (DEPTH, ATTN_WIDTH), f32)
    rel_bias_table = 0.5 * jax.random.normal(ks[3], (REL_BUCKETS, ATTN_HEADS), f32)
    w_out = jax.random.normal(ks[4], (DEPTH, MIX_WIDTH, D_MODEL), f32) * MIX_WIDTH ** -0.5 * BETA
    ln1_g = 1.0 + 0.02 * jax.random.normal(ks[5], (DEPTH, D_MODEL), f32)
    ln1_b = 0.02 * jax.random.normal(ks[6], (DEPTH, D_MODEL), f32)
    w_router_group = jax.random.normal(ks[7], (DEPTH, D_MODEL, N_GROUPS), f32) * D_MODEL ** -0.5
    b_router_group = 0.01 * jax.random.normal(ks[8], (DEPTH, N_GROUPS), f32)
    w_router_expert = jax.random.normal(ks[9], (DEPTH, D_MODEL, N_EXPERTS), f32) * D_MODEL ** -0.5
    b_router_expert = 0.01 * jax.random.normal(ks[10], (DEPTH, N_EXPERTS), f32)
    w_gate_up = jax.random.normal(ks[11], (DEPTH, N_EXPERTS, D_MODEL, 2 * D_EXPERT), f32) * D_MODEL ** -0.5 * BETA
    w_down = jax.random.normal(ks[12], (DEPTH, N_EXPERTS, D_EXPERT, D_MODEL), f32) * D_EXPERT ** -0.5 * BETA
    ln2_g = 1.0 + 0.02 * jax.random.normal(ks[13], (DEPTH, D_MODEL), f32)
    ln2_b = 0.02 * jax.random.normal(ks[14], (DEPTH, D_MODEL), f32)
    return {"x": x, "w_in": w_in, "attn_out_gain": attn_out_gain, "rel_bias_table": rel_bias_table,
            "w_out": w_out, "ln1_g": ln1_g, "ln1_b": ln1_b, "w_router_group": w_router_group,
            "b_router_group": b_router_group, "w_router_expert": w_router_expert,
            "b_router_expert": b_router_expert, "w_gate_up": w_gate_up, "w_down": w_down,
            "ln2_g": ln2_g, "ln2_b": ln2_b}

def reference(x, w_in, attn_out_gain, rel_bias_table, w_out, ln1_g, ln1_b, w_router_group,
              b_router_group, w_router_expert, b_router_expert, w_gate_up, w_down, ln2_g, ln2_b):
    B, S, D = x.shape
    h = x
    for l in range(DEPTH):
        mix = hybrid_mixer(h, w_in[l], attn_out_gain[l], rel_bias_table, w_out[l])
        h = layer_norm(ALPHA * h + mix, ln1_g[l], ln1_b[l])
        ffn = hierarchical_moe(h.reshape(B * S, D), w_router_group[l], b_router_group[l],
                               w_router_expert[l], b_router_expert[l], w_gate_up[l], w_down[l]).reshape(B, S, D)
        h = layer_norm(ALPHA * h + ffn, ln2_g[l], ln2_b[l])
    return h


_drawn_inputs = setup_inputs


def setup_inputs(seed=0):
    import zlib

    import numpy as np

    out = dict(_drawn_inputs(seed))
    spreads = {}
    factors = {'attn_out_gain': 23.628,
     'ln1_b': 2.678,
     'b_router_group': 63.271,
     'b_router_expert': 56.269,
     'ln2_g': 7.446,
     'ln2_b': 7.87}
    for name, (base, spread) in spreads.items():
        noise = np.random.default_rng([zlib.crc32(name.encode()), seed]).standard_normal(out[name].shape)
        drawn = base * np.exp(spread * noise) if base else spread * noise
        out[name] = __import__('jax').numpy.asarray(drawn.astype(out[name].dtype))
    for name, factor in factors.items():
        out[name] = (out[name] * factor).astype(out[name].dtype)
    return out
```

```python
import math
from contextlib import ExitStack

import numpy as np

import concourse.bass as bass
from concourse import mybir

F32 = mybir.dt.float32
F32R = mybir.dt.float32r
U32 = mybir.dt.uint32
I32 = mybir.dt.int32
ALU = mybir.AluOpType
ACT = mybir.ActivationFunctionType
AX = mybir.AxisListType.X

P = 128
SEQ, D = 512, 1024
NT = SEQ // P
KC = D // P
HALF = 512
SLICES = 7
HA, DA = 8, 64
HR, DR = 4, 128
BUCKETS, MAX_DIST = 32, 128
NG, EPG = 4, 8
NE = NG * EPG
DE = 512
ALPHA = 2.0 ** 0.25
EPS = 1e-5
NEG = -1e30

IN_UNITS = SLICES * KC // 2
OUT_UNITS = KC
FRONT = IN_UNITS + OUT_UNITS
TU = KC + DE // P
RAW = TU
RAW_FRONT = 6
SPLIT = 4
MAXT = 40
SKIP = 1 << 20

RQ, RK, RV, RG, AQ, AK, AV = 3, 4, 5, 6, 0, 1, 2
ORDER = [RQ, RK, RV, RG, AQ, AK, AV]

LINE = 3 * P


def shape_constants():
    f = np.float32
    half = DR // 2
    inv = f(10000.0) ** (-np.arange(half, dtype=f) / f(half))
    ang = np.arange(SEQ, dtype=f)[:, None] * inv[None, :]
    rope = np.stack([np.cos(ang), np.sin(ang)], 1).astype(f)
    gam = f(1) - np.exp(np.linspace(math.log(1 / 32), math.log(1 / 512), HR).astype(f))
    log_g = np.log(gam).astype(f)
    dist = (np.arange(SEQ)[None, :] - np.arange(P)[:, None])[:, None, :]
    decay = np.where(dist >= 0, np.exp(np.maximum(dist, 0).astype(f) * log_g[None, :, None]), 0)
    decay = (decay * DR ** -0.5).astype(f)
    n = 2 * P - 1 - np.arange(LINE)
    nf = np.maximum(n, 1).astype(f)
    ex = BUCKETS // 2
    large = ex + (np.log(nf / f(ex)) / f(math.log(MAX_DIST / ex)) * f(BUCKETS - ex)).astype(np.int32)
    bucket = np.where(n < ex, np.maximum(n, 0), np.minimum(large, BUCKETS - 1))
    pick = np.zeros((BUCKETS + 1, LINE + P), f)
    pick[bucket, np.arange(LINE)] = 1
    pick[:BUCKETS, :LINE][:, n < 0] = 0
    pick[BUCKETS, :LINE][n < 0] = NEG
    pick[BUCKETS - 1, LINE:] = 1
    r = np.arange(P)
    mats = np.zeros((P, 4 * P + 2 * NE + MAXT + NT), f)
    mats[:, 0:P] = np.eye(P)
    mats[:, P:2 * P] = r[:, None] < r[None, :]
    mats[:, 2 * P:3 * P] = 1
    e = np.arange(NE)
    mats[:NE, 3 * P:3 * P + NE] = e[:, None] < e[None, :]
    mats[:NE, 3 * P + NE:3 * P + 2 * NE] = e[:, None] <= e[None, :]
    mats[:, 3 * P + 2 * NE:-NT - P] = np.arange(MAXT)[None, :]
    mats[:, -NT - P:-NT] = np.eye(P)[::-1]
    mats[:, -NT:] = r[:, None] + P * np.arange(NT)[None, :]
    return {"c_rope": rope, "c_decay": decay, "c_pick": pick, "c_mats": mats}


def layer_kernel(nc, x, w_in, gain, rel, w_out, ln1_g, ln1_b, w_rg, b_rg, w_re, b_re, w_gu, w_dn,
                 ln2_g, ln2_b, c_rope, c_decay, c_pick, c_mats, out):
    x_d = x[0].rearrange("(i p) d -> i p d", p=P)
    out_d = out[0].rearrange("(i p) d -> i p d", p=P)
    win_d = w_in[0].rearrange("(m c p) (s n) -> s m p c n", c=2, p=P, n=HALF)
    wout_d = w_out[0].rearrange("(c p) n -> c p n", p=P)
    gu_d = w_gu[0].rearrange("e (c p) n -> e c p n", p=P)
    dn_d = w_dn[0].rearrange("e (c p) n -> e c p n", p=P)

    line_d = nc.dram_tensor("bias_line", (HA, LINE), F32).ap()
    h_d = nc.dram_tensor("h_rows", (SEQ, D), F32).ap()
    list_d = nc.dram_tensor("tile_list", (P * MAXT, 4), U32).ap()
    y_d = nc.dram_tensor("y_rows", (2 * SEQ, D), F32).ap()

    with ExitStack() as ctx:
        def sb(name, shape, dt=F32):
            return ctx.enter_context(nc.sbuf_tensor(name, shape, dt))

        def sem(name):
            return ctx.enter_context(nc.semaphore(name))

        bank = [ctx.enter_context(nc.psum_tensor(f"bank{i}", [P, HALF], F32)) for i in range(8)]

        h_sb = sb("h_sb", [P, NT, D])
        raw = sb("raw", [P, RAW, D])
        w_hi = sb("w_hi", [P, SPLIT, D], F32R)
        w_lo = sb("w_lo", [P, SPLIT, D], F32R)
        act_hi = sb("act_hi", [P, KC, SEQ], F32R)
        act_lo = sb("act_lo", [P, KC, SEQ], F32R)
        mats = sb("mats", [P, 4 * P + 2 * NE + MAXT + NT])
        ident, before, ones = mats[:, 0:P], mats[:, P:2 * P], mats[:, 2 * P:3 * P]
        e_before = mats[0:NE, 3 * P:3 * P + NE]
        e_upto = mats[0:NE, 3 * P + NE:3 * P + 2 * NE]
        iota = mats[:, 3 * P + 2 * NE:3 * P + 2 * NE + MAXT]
        flip = mats[:, 3 * P + 2 * NE + MAXT:3 * P + 2 * NE + MAXT + P]
        token = mats[:, 3 * P + 2 * NE + MAXT + P:]
        qT = sb("qT", [P, 2, HA // 2, SEQ])
        v_sb = sb("v_sb", [P, NT, HALF])
        rT = sb("rT", [P, 2, HR, SEQ])
        rv_sb = sb("rv_sb", [P, NT, HALF])
        cat = sb("cat", [P, NT, D])
        work = sb("work", [P, 4, HALF])
        gain_b = sb("gain_b", [P, HALF])
        small = sb("small", [P, 128])
        rope = raw[:, 11, 0:NT * DR].rearrange("p (i a n) -> p i a n", i=NT, a=2)
        bias_t = raw[:, 6:8, :].rearrange("p a (b n) -> p (a b) n", n=2 * P)
        decay_t = raw[:, 8:10, :].rearrange("p a (b n) -> p (a b) n", n=SEQ)
        pick = raw[0:BUCKETS + 1, 10, 0:LINE + P]
        tab = raw[0:BUCKETS + 1, 10, 512:512 + HA]
        line_s = raw[0:HA, 11, 512:512 + LINE]
        turned_t = raw[:, 10:12, :].rearrange("p a (b n) -> p (a b) n", n=2 * P)
        far = small[:, 0:HA]
        hT = qT[:, :, :, :].rearrange("p a b n -> p (a b) n")
        ln1 = rT[:, 1, :, :].rearrange("p (a b) n -> p a (b n)", a=2)
        ln2 = rT[:, 0, :, :].rearrange("p (a b) n -> p a (b n)", a=2)
        xg = v_sb[:, 0:2, :].rearrange("p a n -> p (a n)")
        y_sb = v_sb[:, 2:4, :].rearrange("p a n -> p (a n)")
        hid = rv_sb[:, 0, :]
        sig = rv_sb[:, 1, :]
        xgT_hi, xgT_lo = act_hi[:, 0:2, :], act_lo[:, 0:2, :]
        hidT_hi, hidT_lo = act_hi[:, 2, :], act_lo[:, 2, :]
        NL = NG + NE
        wr = rv_sb[:, 2, 0:KC * NL].rearrange("p (c n) -> p c n", c=KC)
        br = rv_sb[:, 3, 0:NL]
        room = cat[:, :, :].rearrange("p i n -> p (i n)")

        def by_expert(k):
            return room[:, k * NT * NE:(k + 1) * NT * NE].rearrange("p (i e) -> p i e", i=NT)

        logit = room[:, 0:NT * NL].rearrange("p (i e) -> p i e", i=NT)
        g_prob, g_mask, member, n_tl = by_expert(2), by_expert(3), by_expert(4), by_expert(5)
        ends = room[0:NE, 6 * NT * NE:6 * NT * NE + MAXT]
        e_log, e_prob, pick1, pick2 = by_expert(7), by_expert(8), by_expert(9), by_expert(10)
        rank, tmp_a, tmp_b = by_expert(11), by_expert(12), by_expert(13)
        col = room[:, 14 * NT * NE:15 * NT * NE].rearrange("p (k i) -> p k i", i=NT)
        top = room[:, 15 * NT * NE:15 * NT * NE + 2 * NT * 8].rearrange("p (k i e) -> p k i e", k=2, i=NT)
        topi = room[:, 16 * NT * NE:16 * NT * NE + 2 * NT * 8].bitcast(U32).rearrange(
            "p (k i e) -> p k i e", k=2, i=NT)
        entry = room[:, 17 * NT * NE:17 * NT * NE + 8 * NT].bitcast(U32).rearrange(
            "p (i j w) -> p i j w", i=NT, j=2)
        entry_w = room[:, 17 * NT * NE:17 * NT * NE + 8 * NT].rearrange("p (i j w) -> p i j w", i=NT, j=2)
        place = room[:, 18 * NT * NE:18 * NT * NE + 2 * NT].bitcast(U32).rearrange("p (j i) -> p j i", j=2)
        tiles = room[:, 19 * NT * NE:19 * NT * NE + 4 * MAXT].bitcast(U32).rearrange("p (t w) -> p t w", w=4)
        stats = sb("stats", [P, NT, 2, 6])
        mv = sb("mv", [P, NT, 2])
        tlist = sb("tlist", [1, MAXT + 2], I32)
        g_idx = sb("g_idx", [P, 1], U32)
        s_ent = sb("s_ent", [P, 4], U32)

        x_in, mats_in, pick_in, rope_in, decay_in, bias_in, gain_in, router_in, ln1_in, ln2_in = [
            sem(n) for n in ("x_in", "mats_in", "pick_in", "rope_in", "decay_in", "bias_in",
                             "gain_in", "router_in", "ln1_in", "ln2_in")]
        raw_in = [sem(f"raw_in{i}") for i in range(RAW)]
        hi_done, lo_done, split_used = sem("hi_done"), sem("lo_done"), sem("split_used")
        xT_ps, act_hi_ok, act_lo_ok = sem("xT_ps"), sem("act_hi_ok"), sem("act_lo_ok")
        proj_done, proj_out = sem("proj_done"), sem("proj_out")
        roped, rope_ps, rT_ok = sem("roped"), sem("rope_ps"), sem("rT_ok")
        line_ps, line_ok, line_out, far_ok = sem("line_ps"), sem("line_ok"), sem("line_out"), sem("far_ok")
        rs_ps, rs_ok, ro_ps, ro_ok, r_sqrt = (sem(n) for n in ("rs_ps", "rs_ok", "ro_ps", "ro_ok", "r_sqrt"))
        r_var = sem("r_var")
        sc_ps, max_ok, exp_ok, pT_ps, pT_ok, o_ps, o_ok = (
            sem(n) for n in ("sc_ps", "max_ok", "exp_ok", "pT_ps", "pT_ok", "o_ps", "o_ok"))
        rms_var, rms_sqrt, cat_ok, catT_ps = (sem(n) for n in ("rms_var", "rms_sqrt", "cat_ok", "catT_ps"))
        mix_ps, ln_var, ln_sqrt, h_ok, h_out, hT_ps, hT_ok = (
            sem(n) for n in ("mix_ps", "ln_var", "ln_sqrt", "h_ok", "h_out", "hT_ps", "hT_ok"))
        rl_ps, rl_ok, r_exp, m_ok, rank_ps, nt_ok, tb_ps, le_ok, ent_ok, fill_ok, fill_out, ents_out = (
            sem(n) for n in ("rl_ps", "rl_ok", "r_exp", "m_ok", "rank_ps", "nt_ok", "tb_ps", "le_ok",
                             "ent_ok", "fill_ok", "fill_out", "ents_out"))
        el_ps, tlist_ok, tiles_in, pool_id = sem("el_ps"), sem("tlist_ok"), sem("tiles_in"), sem("pool_id")
        g_idx_ok, xg_in, xg_ps, xg_hi, xg_ok = (sem(n) for n in ("g_idx_ok", "xg_in", "xg_ps", "xg_hi", "xg_ok"))
        gu_ps, sig_ok, hid_ok, hidT_ps, hidT_hi_ok, hidT_ok = (
            sem(n) for n in ("gu_ps", "sig_ok", "hid_ok", "hidT_ps", "hidT_hi_ok", "hidT_ok"))
        y_ps, y_ok, ent_cur, y_out = sem("y_ps"), sem("y_ok"), sem("ent_cur"), sem("y_out")
        xg_zero, g_idx_first = sem("xg_zero"), sem("g_idx_first")
        y_in = [sem(f"y_in{i}") for i in range(2)]
        f_sum, f_var, f_sqrt, f_norm, f_gain, f_ok, out_sem = (
            sem(n) for n in ("f_sum", "f_var", "f_sqrt", "f_norm", "f_gain", "f_ok", "out_sem"))
        dve_seq = sem("dve_seq")
        bias_ps, bias_ok = sem("bias_ps"), sem("bias_ok")

        block = ctx.enter_context(nc.Block())

        def raw_slot(u):
            return u % RAW_FRONT

        def unit_view(ring, slot, u):
            v = ring[:, slot, :]
            return v.rearrange("p (c n) -> p c n", c=2) if u < IN_UNITS else v

        @block.sync
        def _(sp):
            for i in range(NT):
                sp.dma_start(h_sb[:, i, :], x_d[i]).then_inc(x_in, 16)
            for u in range(FRONT):
                if u >= RAW_FRONT:
                    sp.wait_ge(lo_done, u - RAW_FRONT + 1)
                s = raw_slot(u)
                src = win_d[ORDER[u // 4], u % 4] if u < IN_UNITS else wout_d[u - IN_UNITS]
                sp.dma_start(unit_view(raw, s, u), src).then_inc(raw_in[s], 16)
            for c in range(TU):
                if c < RAW_FRONT:
                    sp.wait_ge(lo_done, FRONT - RAW_FRONT + c + 1)
                elif c == RAW_FRONT:
                    sp.wait_ge(max_ok, NT * HA)
                src = gu_d[0, c] if c < KC else dn_d[0, c - KC]
                sp.dma_start(raw[:, c, :], src).then_inc(raw_in[c], 16)
            sp.wait_ge(tlist_ok, 1)
            n_tiles = sp.value_load(tlist[0:1, MAXT:MAXT + 1], min_val=2, max_val=MAXT - 1)
            with sp.Fori(1, n_tiles) as t:
                e = sp.value_load(tlist[0:1, bass.ds(t, 1)], min_val=0, max_val=NE - 1)
                for c in range(TU):
                    sp.wait_ge(lo_done, t * TU + FRONT - TU + c + 1)
                    src = gu_d[bass.ds(e, 1), c] if c < KC else dn_d[bass.ds(e, 1), c - KC]
                    sp.dma_start(raw[:, c, :], src.rearrange("e p n -> (e p) n")).then_inc(raw_in[c], 16)

            sp.wait_ge(y_out, n_tiles * 16)
            y_rows = y_d.rearrange("(i p j) n -> i p (j n)", p=P, j=2)
            for i in range(NT):
                if i >= 2:
                    sp.wait_ge(f_sum, i - 1)
                sp.dma_start(raw[:, 2 * (i % 2):2 * (i % 2) + 2, :].rearrange("p a n -> p (a n)"),
                             y_rows[i]).then_inc(y_in[i % 2], 16)
            for i in range(NT):
                sp.wait_ge(f_ok, i + 1)
                sp.dma_start(out_d[i], h_sb[:, i, :]).then_inc(out_sem, 16)
            sp.wait_ge(out_sem, NT * 16)

        @block.tensor
        def _(pe):
            def passes(o, l_hi, l_lo, r_hi, r_lo, start, stop):
                pe.matmul(o, l_hi, r_hi, start=start, stop=False)
                pe.matmul(o, l_lo, r_hi, start=False, stop=False)
                return pe.matmul(o, l_hi, r_lo, start=False, stop=stop)

            pe.wait_ge(mats_in, 16)
            pe.wait_ge(x_in, NT * 16)
            for c in range(KC):
                if c >= 4:
                    pe.wait_ge(act_lo_ok, c - 3)
                for i in range(NT):
                    mm = pe.transpose(bank[4 + c % 4][:, i * P:(i + 1) * P],
                                      h_sb[:, i, c * P:(c + 1) * P], ident)
                mm.then_inc(xT_ps, 1)

            pe.wait_ge(act_lo_ok, KC)
            pe.wait_ge(pick_in, 32)
            pe.wait_ge(line_ok, 1)
            pe.matmul(bank[4][0:HA, 0:LINE], tab, pick[:, 0:LINE], start=True, stop=True)
            pe.matmul(bank[5][:, 0:HA], pick[:, LINE:LINE + P], tab, start=True, stop=True).then_inc(line_ps, 1)

            def rope_transposes(q, i):
                n = NT * q + i
                pe.wait_ge(roped, n + 1)
                if n == 0:
                    pe.wait_ge(far_ok, 1)
                if n >= 2:
                    pe.wait_ge(rT_ok, n - 1)
                for h in range(HR):
                    mm = pe.transpose(bank[4 + n % 2][:, h * P:(h + 1) * P],
                                      work[:, i, h * P:(h + 1) * P], ident)
                mm.then_inc(rope_ps, 1)

            for s, name in enumerate(ORDER):
                for m in range(4):
                    u = 4 * s + m
                    pe.wait_ge(lo_done, u + 1)
                    if u == 0:
                        pe.wait_ge(act_lo_ok, KC)
                    wh, wl = unit_view(w_hi, u % SPLIT, u), unit_view(w_lo, u % SPLIT, u)
                    for b in range(4):
                        if m == 0 and s:
                            pe.wait_ge(proj_out, 4 * (s - 1) + b + 1)
                        cut = slice(b * P, (b + 1) * P)
                        for cc in range(2):
                            k = 2 * m + cc
                            first, last = k == 0, k == KC - 1
                            if name in (AQ, AK):
                                mm = passes(bank[b][:, :], wh[:, cc, cut], wl[:, cc, cut],
                                            act_hi[:, k, :], act_lo[:, k, :], first, last)
                            else:
                                mm = passes(bank[b][:, :], act_hi[:, k, cut], act_lo[:, k, cut],
                                            wh[:, cc, :], wl[:, cc, :], first, last)
                        if m == 3 and b < 3:
                            mm.then_inc(proj_done, 1)
                    mm.then_inc(split_used, 1)
                    if s in (1, 2):
                        rope_transposes(s - 1, m)

            pe.wait_ge(rT_ok, 2 * NT)
            pe.wait_ge(bias_in, 16)
            for k in range(4):
                pe.matmul(bank[4 + k][:, :], flip, turned_t[:, 2 * k:2 * k + 2, :], start=True,
                          stop=True).then_inc(bias_ps, 1)
            pe.wait_ge(bias_ok, 4)

            pe.wait_ge(proj_out, 4 * SLICES)
            for h in range(HR):
                for j in range(NT):
                    n = NT * h + j
                    if n >= 2:
                        pe.wait_ge(rs_ok, n - 1)
                    pe.matmul(bank[4 + n % 2][:, 0:SEQ - j * P], rT[:, 1, h, j * P:(j + 1) * P],
                              rT[:, 0, h, j * P:SEQ], start=True, stop=True).then_inc(rs_ps, 1)
                if h >= 2:
                    pe.wait_ge(ro_ok, h - 1)
                for i in range(NT):
                    for j in range(i + 1):
                        if i == 0 or j == i:
                            pe.wait_ge(rs_ok, NT * h + j + 1)
                        mm = pe.matmul(bank[6 + h % 2][:, i * P:(i + 1) * P],
                                       work[:, j, (i - j) * P:(i - j + 1) * P],
                                       rv_sb[:, j, h * P:(h + 1) * P], start=(j == 0), stop=(j == i))
                mm.then_inc(ro_ps, 1)

            pe.wait_ge(ro_ok, HR)

            def scores(n):
                i, h = divmod(n, HA)
                if n >= 2:
                    pe.wait_ge(max_ok, n - 1)
                a = DA * (h % 2)
                pe.matmul(bank[4 + n % 2][:, 0:(i + 1) * P], qT[a:a + DA, 0, h // 2, i * P:(i + 1) * P],
                          qT[a:a + DA, 1, h // 2, 0:(i + 1) * P], start=True, stop=True).then_inc(sc_ps, 1)

            def turn(n):
                i = n // HA
                pe.wait_ge(exp_ok, n + 1)
                if n >= 1:
                    pe.wait_ge(pT_ok, n)
                for j in range(i + 1):
                    mm = pe.transpose(bank[6][:, j * P:(j + 1) * P], work[:, n % 2, j * P:(j + 1) * P], ident)
                mm.then_inc(pT_ps, 1)

            def values(n):
                i, h = divmod(n, HA)
                pe.wait_ge(pT_ok, n + 1)
                if h == 0 and i:
                    pe.wait_ge(o_ok, i)
                for j in range(i + 1):
                    mm = pe.matmul(bank[7][:, h * DA:(h + 1) * DA], work[:, 2 + n % 2, j * P:(j + 1) * P],
                                   v_sb[:, j, h * DA:(h + 1) * DA], start=(j == 0), stop=(j == i))
                mm.then_inc(o_ps, 1)

            steps = NT * HA
            for n in range(steps + 2):
                if n < steps:
                    scores(n)
                if 1 <= n <= steps:
                    turn(n - 1)
                if n >= 2:
                    values(n - 2)

            pe.wait_ge(cat_ok, NT)
            for c in range(KC):
                if c >= 4:
                    pe.wait_ge(act_lo_ok, KC + c - 3)
                for i in range(NT):
                    mm = pe.transpose(bank[4 + c % 4][:, i * P:(i + 1) * P], cat[:, i, c * P:(c + 1) * P], ident)
                mm.then_inc(xT_ps, 1)
            pe.wait_ge(act_lo_ok, 2 * KC)
            for c in range(KC):
                u = IN_UNITS + c
                pe.wait_ge(lo_done, u + 1)
                wh, wl = w_hi[:, u % SPLIT, :], w_lo[:, u % SPLIT, :]
                for i in range(NT):
                    cut = slice(i * P, (i + 1) * P)
                    for a in range(2):
                        cols = slice(a * HALF, (a + 1) * HALF)
                        mm = passes(bank[2 * i + a][:, :], act_hi[:, c, cut], act_lo[:, c, cut],
                                    wh[:, cols], wl[:, cols], c == 0, c == KC - 1)
                    if c == KC - 1 and i < NT - 1:
                        mm.then_inc(mix_ps, 1)
                mm.then_inc(split_used, 1)

            for i in range(NT):
                pe.wait_ge(h_ok, i + 1)
                for a in range(2):
                    n = 2 * i + a
                    if n >= 2:
                        pe.wait_ge(hT_ok, n - 1)
                    for c in range(4):
                        mm = pe.transpose(bank[n % 2][:, c * P:(c + 1) * P],
                                          h_sb[:, i, (4 * a + c) * P:(4 * a + c + 1) * P], ident)
                    mm.then_inc(hT_ps, 1)
            pe.wait_ge(router_in, 64)
            for i in range(NT):
                pe.wait_ge(hT_ok, 2 * i + 2)
                for c in range(KC):
                    mm = pe.matmul(bank[2][:, i * NL:(i + 1) * NL], hT[:, c, i * P:(i + 1) * P],
                                   wr[:, c, :], start=(c == 0), stop=(c == KC - 1))
            mm.then_inc(rl_ps, 1)

            pe.wait_ge(m_ok, 1)
            M = member
            for i in range(NT):
                for k in range(i + 1):
                    pe.matmul(bank[3][:, i * NE:(i + 1) * NE], before if k == i else ones, M[:, k, :],
                              start=(k == 0), stop=(k == i))
            for k in range(NT):
                mm = pe.matmul(bank[4][0:NE, 0:P], M[:, k, :], ones, start=(k == 0), stop=(k == NT - 1))
            mm.then_inc(rank_ps, 1)
            pe.wait_ge(nt_ok, 1)
            ntl = n_tl[0:NE].rearrange("p i e -> p (i e)")
            pe.matmul(bank[5][:, 0:NE], ntl, e_before, start=True, stop=True)
            pe.matmul(bank[6][0:NE, 0:P], e_upto, ntl, start=True, stop=True)
            pe.matmul(bank[7][0:1, MAXT:MAXT + 1], ones[0:NE, 0:1], ntl[:, 0:1], start=True,
                      stop=True).then_inc(tb_ps, 1)
            pe.wait_ge(le_ok, 1)
            pe.matmul(bank[7][0:1, 0:MAXT], ones[0:NE, 0:1], ends, start=True, stop=True).then_inc(el_ps, 1)

            def gathered(t):
                pe.wait_ge(xg_in, t * 16 + 16)
                for c in range(KC):
                    mm = pe.transpose(bank[4 + c // 4][:, (c % 4) * P:(c % 4 + 1) * P],
                                      xg[:, c * P:(c + 1) * P], ident)
                mm.then_inc(xg_ps, 1)

            pe.wait_ge(tlist_ok, 1)
            n_tiles = pe.value_load(tlist[0:1, MAXT:MAXT + 1], min_val=2, max_val=MAXT - 1)
            gathered(0)
            with pe.Fori(0, n_tiles) as t:
                pe.wait_ge(xg_ok, t * 2 + 2)
                pe.wait_ge(hid_ok, t * 2)
                for c in range(KC):
                    pe.wait_ge(lo_done, t * TU + FRONT + c + 1)
                    slot = (FRONT + c) % SPLIT
                    cut = slice((c % 4) * P, (c % 4 + 1) * P)
                    for a in range(2):
                        cols = [w[:, slot, :].rearrange("p (g n) -> p g n", g=2)[:, :, a * 256:(a + 1) * 256]
                                for w in (w_hi, w_lo)]
                        o = bank[a][:, :].rearrange("p (g n) -> p g n", g=2)
                        mm = passes(o, xgT_hi[:, c // 4, cut], xgT_lo[:, c // 4, cut],
                                    cols[0], cols[1], c == 0, c == KC - 1)
                        if a == 0 and c == KC - 1:
                            mm.then_inc(gu_ps, 1)
                    mm.then_inc(split_used, 1)
                gathered(t + 1)

                def turn_hidden(a):
                    pe.wait_ge(hid_ok, t * 2 + a + 1)
                    for k in range(2):
                        mm = pe.transpose(bank[6 + a][:, k * P:(k + 1) * P],
                                          hid[:, (2 * a + k) * P:(2 * a + k + 1) * P], ident)
                    mm.then_inc(hidT_ps, 1)

                turn_hidden(0)
                pe.wait_ge(y_ok, t)
                for k in range(4):
                    if k == 1:
                        turn_hidden(1)
                    if k % 2 == 0:
                        pe.wait_ge(hidT_ok, t * 2 + k // 2 + 1)
                    pe.wait_ge(lo_done, t * TU + FRONT + KC + k + 1)
                    slot = (FRONT + KC + k) % SPLIT
                    cut = slice(k * P, (k + 1) * P)
                    for a in range(2):
                        cols = slice(a * HALF, (a + 1) * HALF)
                        mm = passes(bank[2 + a][:, :], hidT_hi[:, cut], hidT_lo[:, cut],
                                    w_hi[:, slot, cols], w_lo[:, slot, cols], k == 0, k == 3)
                    mm.then_inc(split_used, 1)

        @block.vector
        def _(dve):
            seq = [0]

            def step(ins):
                seq[0] += 1
                ins.then_inc(dve_seq, 1)
                dve.wait_ge(dve_seq, seq[0])

            def split_lo(u):
                dve.wait_ge(hi_done, u + 1)
                dve.tensor_tensor(w_lo[:, u % SPLIT, :], raw[:, raw_slot(u), :],
                                  w_hi[:, u % SPLIT, :].bitcast(F32), ALU.subtract).then_inc(lo_done, 1)

            def act_lo_of(n):
                c = n % KC
                dve.wait_ge(act_hi_ok, n + 1)
                dve.tensor_tensor(act_lo[:, c, :], bank[4 + c % 4][:, :], act_hi[:, c, :].bitcast(F32),
                                  ALU.subtract).then_inc(act_lo_ok, 1)

            dve.memset(tab[:, :], 1.0).then_inc(line_ok, 1)
            for n in range(KC):
                act_lo_of(n)
                if n % 2 and n < 2 * RAW_FRONT - 6:
                    split_lo(n // 2)
            dve.wait_ge(line_ps, 1)
            dve.tensor_copy(line_s, bank[4][0:HA, 0:LINE]).then_inc(line_ok, 1)
            dve.tensor_copy(far, bank[5][:, 0:HA]).then_inc(far_ok, 1)
            dve.wait_ge(rope_in, 16)

            def bank_done(s, b):
                if b < 3:
                    dve.wait_ge(proj_done, 3 * s + b + 1)
                else:
                    dve.wait_ge(split_used, 4 * s + 4)

            def rope_rows(s, i):
                n = NT * s + i
                bank_done(s, i)
                if n >= NT:
                    dve.wait_ge(rope_ps, n - NT + 1)
                t = bank[i][:, :].rearrange("p (h a n) -> p h a n", h=HR, a=2)
                o = work[:, i, :].rearrange("p (h a n) -> p h a n", h=HR, a=2)
                x1 = rv_sb[:, 0, :].rearrange("p (h a n) -> p h a n", h=HR, a=2)
                cos = rope[:, i, 0:1, :].to_broadcast([P, HR, DR // 2])
                sin = rope[:, i, 1:2, :].to_broadcast([P, HR, DR // 2])
                dve.tensor_tensor(o[:, :, 0, :], t[:, :, 0, :], cos, ALU.mult)
                dve.tensor_tensor(o[:, :, 1, :], t[:, :, 1, :], cos, ALU.mult)
                dve.tensor_tensor(x1[:, :, 0, :], t[:, :, 1, :], sin, ALU.mult)
                step(dve.tensor_tensor(x1[:, :, 1, :], t[:, :, 0, :], sin, ALU.mult))
                dve.tensor_tensor(o[:, :, 0, :], o[:, :, 0, :], x1[:, :, 0, :],
                                  ALU.subtract).then_inc(proj_out, 1)
                dve.tensor_tensor(o[:, :, 1, :], o[:, :, 1, :], x1[:, :, 1, :], ALU.add).then_inc(roped, 1)
                dve.wait_ge(roped, n + 1)

            for u in range(3, IN_UNITS + 4):
                if u % 4 == 3 and u > 4 and ORDER[u // 4 - 1] in (RQ, RK):
                    for i in range(NT):
                        rope_rows(u // 4 - 1, i)
                split_lo(u)

            dve.wait_ge(decay_in, 16)
            rcol = small[:, 32:32 + 4]
            for h in range(HR):
                for j in range(NT):
                    n = NT * h + j
                    dve.wait_ge(rs_ps, n + 1)
                    if j == 0 and h:
                        dve.wait_ge(ro_ps, h)
                    dve.tensor_tensor(work[:, j, 0:SEQ - j * P], bank[4 + n % 2][:, 0:SEQ - j * P],
                                      decay_t[:, h, 0:SEQ - j * P], ALU.mult).then_inc(rs_ok, 1)
                dve.wait_ge(ro_ps, h + 1)
                o = bank[6 + h % 2][:, :].rearrange("p (i n) -> p i n", i=NT)
                for i in range(NT):
                    ins = dve.bn_stats(stats[:, i, 0, :], o[:, i, :])
                step(ins)
                for i in range(NT):
                    ins = dve.bn_aggr(mv[:, i, :], stats[:, i, 0, :])
                step(ins)
                if h:
                    dve.wait_ge(r_sqrt, h)
                dve.tensor_scalar(small[:, 16:20], mv[:, :, 1], EPS, None, ALU.add).then_inc(r_var, 1)
                dve.wait_ge(r_sqrt, h + 1)
                step(dve.reciprocal(rcol, small[:, 20:24]))
                gate = cat[:, :, HALF + h * P:HALF + (h + 1) * P]
                dve.wait_ge(proj_out, NT * (ORDER.index(RG) + 1))
                for i in range(NT):
                    ins = dve.scalar_tensor_tensor(out=gate[:, i, :], in0=o[:, i, :], scalar=mv[:, i, 0:1],
                                                   in1=gate[:, i, :], op0=ALU.subtract, op1=ALU.mult)
                ins.then_inc(ro_ok, 1)
                dve.wait_ge(ro_ok, h + 1)
                step(dve.tensor_tensor(gate, gate, rcol.unsqueeze(2).to_broadcast([P, NT, P]), ALU.mult))

            dve.wait_ge(bias_ok, 4)
            scale = DA ** -0.5
            for n in range(NT * HA + 1):
                if n < NT * HA:
                    i, h = divmod(n, HA)
                    dve.wait_ge(sc_ps, n + 1)
                    if n >= 2:
                        dve.wait_ge(pT_ps, n - 1)
                    lg, s_b = work[:, n % 2, :], bank[4 + n % 2]
                    near = max(0, (i - 1) * P)
                    if near:
                        dve.tensor_scalar(lg[:, 0:near], s_b[:, 0:near], scale, far[:, h:h + 1],
                                          ALU.mult, ALU.add)
                    step(dve.scalar_tensor_tensor(
                        out=lg[:, near:(i + 1) * P], in0=s_b[:, near:(i + 1) * P], scalar=scale,
                        in1=bias_t[:, h, P if i == 0 else 0:2 * P], op0=ALU.mult, op1=ALU.add))
                    step(dve.tensor_reduce(small[:, 40 + n % 2:41 + n % 2], lg[:, 0:(i + 1) * P], AX, ALU.max))
                    dve.tensor_scalar(small[:, 44 + n % 2:45 + n % 2], small[:, 40 + n % 2:41 + n % 2], -1.0,
                                      None, ALU.mult).then_inc(max_ok, 1)
                if n >= HA and n % HA == 0:
                    i = n // HA - 1
                    dve.wait_ge(o_ps, NT and n)
                    inv = small[:, 48:48 + HA]
                    step(dve.reciprocal(inv, small[:, 56 + HA * (i % 2):56 + HA * (i % 2) + HA]))
                    a_o = cat[:, i, 0:HALF].rearrange("p (h n) -> p h n", h=HA)
                    dve.tensor_tensor(a_o, bank[7][:, :].rearrange("p (h n) -> p h n", h=HA),
                                      inv.unsqueeze(2).to_broadcast([P, HA, DA]), ALU.mult).then_inc(o_ok, 1)
                    dve.wait_ge(o_ok, i + 1)
            for i in range(NT):
                ins = dve.tensor_tensor_reduce(work[:, i, :], cat[:, i, 0:HALF], cat[:, i, 0:HALF], 1.0, 0.0,
                                               ALU.mult, ALU.add, small[:, 80 + i:81 + i])
            step(ins)
            dve.tensor_scalar(small[:, 84:88], small[:, 80:84], 1.0 / HALF, EPS, ALU.mult,
                              ALU.add).then_inc(rms_var, 1)
            dve.wait_ge(rms_sqrt, 1)
            step(dve.reciprocal(small[:, 92:96], small[:, 88:92]))
            dve.wait_ge(gain_in, 16)
            for i in range(NT):
                dve.scalar_tensor_tensor(out=cat[:, i, 0:HALF], in0=cat[:, i, 0:HALF],
                                         scalar=small[:, 92 + i:93 + i], in1=gain_b[:, :],
                                         op0=ALU.mult, op1=ALU.mult).then_inc(cat_ok, 1)
            for n in range(KC, 2 * KC):
                act_lo_of(n)
            for u in range(IN_UNITS + 4, FRONT):
                split_lo(u)

            def norm_sums(i, done):
                for a in range(2):
                    ins = dve.bn_stats(stats[:, i, a, :], h_sb[:, i, a * HALF:(a + 1) * HALF])
                step(ins)
                step(dve.bn_aggr(mv[:, i, :], stats[:, i, :, :]))
                dve.tensor_scalar(small[:, 100 + i:101 + i], mv[:, i, 1:2], EPS, None, ALU.add).then_inc(done, 1)

            def normed(i, g_b, root, done, n):
                dve.wait_ge(root, i + 1)
                step(dve.reciprocal(small[:, 108 + i:109 + i], small[:, 104 + i:105 + i]))
                step(dve.tensor_scalar(h_sb[:, i, :], h_sb[:, i, :], mv[:, i, 0:1], small[:, 108 + i:109 + i],
                                       ALU.subtract, ALU.mult))
                step(dve.tensor_tensor(h_sb[:, i, :], h_sb[:, i, :], g_b[:, 0, :], ALU.mult))
                dve.tensor_tensor(h_sb[:, i, :], h_sb[:, i, :], g_b[:, 1, :], ALU.add).then_inc(done, 1)

            for i in range(NT):
                if i < NT - 1:
                    dve.wait_ge(mix_ps, i + 1)
                else:
                    dve.wait_ge(split_used, FRONT)
                for a in range(2):
                    cols = slice(a * HALF, (a + 1) * HALF)
                    ins = dve.scalar_tensor_tensor(out=h_sb[:, i, cols], in0=h_sb[:, i, cols], scalar=ALPHA,
                                                   in1=bank[2 * i + a][:, :], op0=ALU.mult, op1=ALU.add)
                step(ins)
                norm_sums(i, ln_var)
                if i == 0:
                    dve.wait_ge(ln1_in, 32)
                if i:
                    normed(i - 1, ln1, ln_sqrt, h_ok, i - 1)
            normed(NT - 1, ln1, ln_sqrt, h_ok, NT - 1)

            dve.wait_ge(rl_ps, 1)
            dve.wait_ge(router_in, 64)
            step(dve.tensor_tensor(logit, bank[2][:, 0:NT * NL].rearrange("p (i e) -> p i e", i=NT),
                                   br.unsqueeze(1).to_broadcast([P, NT, NL]), ALU.add))

            def over(c, n):
                return c.unsqueeze(2).to_broadcast([P, NT, n])

            dve.memset(g_prob[:, :, NG:8], -1.0)
            step(dve.tensor_reduce(col[:, 0, :], logit[:, :, 0:NG], AX, ALU.max))
            dve.tensor_tensor(tmp_a[:, :, 0:NG], logit[:, :, 0:NG], over(col[:, 0, :], NG),
                              ALU.subtract).then_inc(rl_ok, 1)
            dve.wait_ge(r_exp, 1)
            step(dve.tensor_reduce(col[:, 1, :], tmp_b[:, :, 0:NG], AX, ALU.add))
            step(dve.reciprocal(col[:, 2, :], col[:, 1, :]))
            step(dve.tensor_tensor(g_prob[:, :, 0:NG], tmp_b[:, :, 0:NG], over(col[:, 2, :], NG), ALU.mult))
            for i in range(NT):
                ins = dve.max(top[:, 0, i, :], g_prob[:, i, 0:8])
            step(ins)
            for i in range(NT):
                ins = dve.max_index(topi[:, 0, i, :], top[:, 0, i, :], g_prob[:, i, 0:8])
            step(ins)
            dve.tensor_copy(col[:, 3, :], top[:, 0, :, 0])
            step(dve.tensor_copy(col[:, 4, :], topi[:, 0, :, 0]))
            step(dve.tensor_tensor(tmp_a[:, :, 0:NG], iota[:, 0:NG].unsqueeze(1).to_broadcast([P, NT, NG]),
                                   over(col[:, 4, :], NG), ALU.is_equal))
            spread = tmp_a[:, :, 0:NG].unsqueeze(3).to_broadcast([P, NT, NG, EPG])
            step(dve.tensor_copy(g_mask.rearrange("p i (g e) -> p i g e", g=NG), spread))
            step(dve.tensor_scalar(tmp_b, g_mask, -NEG, NEG, ALU.mult, ALU.add))
            step(dve.tensor_tensor(e_log, logit[:, :, NG:NL], g_mask, ALU.mult))
            step(dve.tensor_tensor(e_log, e_log, tmp_b, ALU.add))
            step(dve.tensor_reduce(col[:, 5, :], e_log, AX, ALU.max))
            dve.tensor_tensor(e_log, e_log, over(col[:, 5, :], NE), ALU.subtract).then_inc(rl_ok, 1)
            dve.wait_ge(r_exp, 2)
            step(dve.tensor_reduce(col[:, 6, :], e_prob, AX, ALU.add))
            step(dve.reciprocal(col[:, 7, :], col[:, 6, :]))
            dve.tensor_scalar(tmp_b, g_mask, -1.0, None, ALU.add)
            step(dve.tensor_tensor(e_prob, e_prob, over(col[:, 7, :], NE), ALU.mult))
            step(dve.tensor_tensor(e_prob, e_prob, tmp_b, ALU.add))
            for i in range(NT):
                ins = dve.max(top[:, 1, i, :], e_prob[:, i, :])
            step(ins)
            for i in range(NT):
                ins = dve.max_index(topi[:, 1, i, :], top[:, 1, i, :], e_prob[:, i, :])
            step(ins)
            for j in range(2):
                ins = dve.tensor_copy(col[:, 8 + j, :], topi[:, 1, :, j])
            step(ins)
            for j, o in enumerate((pick1, pick2)):
                ins = dve.tensor_tensor(o, iota[:, 0:NE].unsqueeze(1).to_broadcast([P, NT, NE]),
                                        over(col[:, 8 + j, :], NE), ALU.is_equal)
            step(ins)
            dve.tensor_tensor(member, pick1, pick2, ALU.add).then_inc(m_ok, 1)
            step(dve.tensor_tensor(col[:, 10, :], top[:, 1, :, 0], top[:, 1, :, 1], ALU.add))
            step(dve.reciprocal(col[:, 11, :], col[:, 10, :]))
            for j in range(2):
                ins = dve.tensor_tensor(col[:, 12 + j, :], top[:, 1, :, j], col[:, 11, :], ALU.mult)
            step(ins)
            dve.memset(entry[:, :, :, 3], 0)
            for j in range(2):
                dve.tensor_tensor(entry_w[:, :, j, 2], col[:, 12 + j, :], col[:, 3, :], ALU.mult)
                dve.tensor_copy(entry[:, :, j, 0], token)
                ins = dve.tensor_scalar(entry[:, :, j, 1], token, 2.0, float(j), ALU.mult, ALU.add)
            step(ins)

            dve.wait_ge(rank_ps, 1)
            counts = bank[4][0:NE, 0:P]
            ntl = n_tl[0:NE].rearrange("p i e -> p (i e)")
            step(dve.tensor_scalar(ntl, counts, 0.0, None, ALU.is_gt))
            for k in range(1, NT):
                step(dve.scalar_tensor_tensor(out=ntl, in0=counts, scalar=float(k * P), in1=ntl,
                                              op0=ALU.is_gt, op1=ALU.add))
            dve.tensor_scalar(ntl[0:1, :], ntl[0:1, :], 1.0, None, ALU.max).then_inc(nt_ok, 1)
            step(dve.tensor_copy(rank, bank[3][:, 0:NT * NE].rearrange("p (i e) -> p i e", i=NT)))
            dve.wait_ge(tb_ps, 1)
            step(dve.tensor_copy(small[0:NE, 120:121], bank[6][0:NE, 0:1]))
            dve.tensor_scalar(ends, iota[0:NE, 0:MAXT], small[0:NE, 120:121], None, ALU.is_ge).then_inc(le_ok, 1)
            tb = bank[5][:, 0:NE].unsqueeze(1).to_broadcast([P, NT, NE])
            for j, pk in enumerate((pick1, pick2)):
                dve.tensor_tensor(tmp_a, pk, rank, ALU.mult)
                step(dve.tensor_tensor(tmp_b, pk, tb, ALU.mult))
                dve.tensor_reduce(col[:, 14, :], tmp_a, AX, ALU.add)
                step(dve.tensor_reduce(col[:, 15, :], tmp_b, AX, ALU.add))
                step(dve.tensor_scalar(col[:, 16, :], col[:, 14, :], float(P), None, ALU.is_ge))
                for k in range(2, NT):
                    step(dve.scalar_tensor_tensor(out=col[:, 16, :], in0=col[:, 14, :], scalar=float(k * P),
                                                  in1=col[:, 16, :], op0=ALU.is_ge, op1=ALU.add))
                step(dve.tensor_tensor(col[:, 15, :], col[:, 15, :], col[:, 16, :], ALU.add))
                step(dve.scalar_tensor_tensor(out=col[:, 14, :], in0=col[:, 16, :], scalar=-float(P),
                                              in1=col[:, 14, :], op0=ALU.mult, op1=ALU.add))
                step(dve.scalar_tensor_tensor(out=col[:, 17 + j, :], in0=col[:, 14, :], scalar=float(MAXT),
                                              in1=col[:, 15, :], op0=ALU.mult, op1=ALU.add))
                dve.tensor_copy(place[:, j, :], col[:, 17 + j, :]).then_inc(ent_ok, 1)
            dve.wait_ge(el_ps, 1)
            step(dve.tensor_scalar(tlist[0:1, 0:MAXT], bank[7][0:1, 0:MAXT], float(NE - 1), None, ALU.min))
            dve.tensor_copy(tlist[0:1, MAXT:MAXT + 1], bank[7][0:1, MAXT:MAXT + 1]).then_inc(tlist_ok, 1)
            dve.wait_ge(tlist_ok, 1)
            n_tiles = dve.value_load(tlist[0:1, MAXT:MAXT + 1], min_val=2, max_val=MAXT - 1)

            def tokens_lo(n):
                for a in range(2):
                    dve.wait_ge(xg_hi, n + a + 1)
                    dve.tensor_tensor(xgT_lo[:, a, :], bank[4 + a][:, :], xgT_hi[:, a, :].bitcast(F32),
                                      ALU.subtract).then_inc(xg_ok, 1)

            tokens_lo(0)
            with dve.Fori(0, n_tiles) as t:
                def weights_lo(c):
                    s = (FRONT + c) % SPLIT
                    dve.wait_ge(hi_done, t * TU + FRONT + c + 1)
                    dve.tensor_tensor(w_lo[:, s, :], raw[:, c, :], w_hi[:, s, :].bitcast(F32),
                                      ALU.subtract).then_inc(lo_done, 1)

                def hidden_lo(a):
                    dve.wait_ge(hidT_hi_ok, t * 2 + a + 1)
                    cut = slice(a * 256, (a + 1) * 256)
                    dve.tensor_tensor(hidT_lo[:, cut], bank[6 + a][:, 0:256], hidT_hi[:, cut].bitcast(F32),
                                      ALU.subtract).then_inc(hidT_ok, 1)

                for c in range(TU - 1):
                    weights_lo(c)
                for a in range(2):
                    dve.wait_ge(sig_ok, t * 2 + a + 1)
                    cut = slice(a * 256, (a + 1) * 256)
                    dve.tensor_tensor(hid[:, cut], sig[:, cut], bank[a][:, 256:512],
                                      ALU.mult).then_inc(hid_ok, 1)
                hidden_lo(0)
                weights_lo(TU - 1)
                hidden_lo(1)
                tokens_lo(t * 2 + 2)

            for i in range(NT):
                dve.wait_ge(y_in[i % 2], 16 * (i // 2 + 1))
                yr = raw[:, 2 * (i % 2):2 * (i % 2) + 2, :]
                step(dve.scalar_tensor_tensor(out=h_sb[:, i, :], in0=h_sb[:, i, :], scalar=ALPHA,
                                              in1=yr[:, 0, :], op0=ALU.mult, op1=ALU.add))
                dve.tensor_tensor(h_sb[:, i, :], h_sb[:, i, :], yr[:, 1, :], ALU.add).then_inc(f_sum, 1)
                dve.wait_ge(f_sum, i + 1)
                norm_sums(i, f_var)
                if i == 0:
                    dve.wait_ge(ln2_in, 32)
                if i:
                    normed(i - 1, ln2, f_sqrt, f_ok, i - 1)
            normed(NT - 1, ln2, f_sqrt, f_ok, NT - 1)

        @block.scalar
        def _(act):
            act.dma_start(mats[:, :], c_mats).then_inc(mats_in, 16)
            act.dma_start(pick, c_pick).then_inc(pick_in, 16)
            act.wait_ge(line_ok, 1)
            act.dma_start(tab[0:BUCKETS, :], rel).then_inc(pick_in, 16)
            act.dma_start(rope, c_rope.rearrange("(i p) a n -> p i a n", p=P)).then_inc(rope_in, 16)
            act.dma_start(decay_t, c_decay).then_inc(decay_in, 16)
            act.dma_start(gain_b[:, :], gain[0].partition_broadcast(P)).then_inc(gain_in, 16)

            def split_hi(u):
                s = raw_slot(u)
                act.wait_ge(raw_in[s], 16 * (u // RAW_FRONT + 1))
                if u >= SPLIT:
                    act.wait_ge(split_used, u - SPLIT + 1)
                act.activation(w_hi[:, u % SPLIT, :], raw[:, s, :], ACT.Copy).then_inc(hi_done, 1)

            def act_hi_of(n):
                c = n % KC
                act.wait_ge(xT_ps, n + 1)
                act.activation(act_hi[:, c, :], bank[4 + c % 4][:, :], ACT.Copy).then_inc(act_hi_ok, 1)

            for n in range(KC):
                act_hi_of(n)
                if n % 2 and n < 2 * RAW_FRONT - 6:
                    split_hi(n // 2)
            act.wait_ge(line_ok, 2)
            act.dma_start(line_d, line_s).then_inc(line_out, 16)

            def turned_rows(n):
                act.wait_ge(rope_ps, n + 1)
                q, i = divmod(n, NT)
                act.activation(rT[:, q, :, i * P:(i + 1) * P],
                               bank[4 + n % 2][:, :].rearrange("p (h n) -> p h n", h=HR),
                               ACT.Copy).then_inc(rT_ok, 1)

            def slice_out(s):
                name = ORDER[s]
                for b in range(4):
                    if b < 3:
                        act.wait_ge(proj_done, 3 * s + b + 1)
                    else:
                        act.wait_ge(split_used, 4 * s + 4)
                    o, f = {RV: (rv_sb[:, b, :], ACT.Copy), RG: (cat[:, b, HALF:D], ACT.Silu),
                            AQ: (qT[:, 0, b, :], ACT.Copy), AK: (qT[:, 1, b, :], ACT.Copy),
                            AV: (v_sb[:, b, :], ACT.Copy)}[name]
                    act.activation(o, bank[b][:, :], f).then_inc(proj_out, 1)

            for u in range(3, IN_UNITS + 4):
                if u % 4 == 3 and u > 4 and ORDER[u // 4 - 1] not in (RQ, RK):
                    slice_out(u // 4 - 1)
                split_hi(u)
                if u // 4 in (2, 3):
                    turned_rows(u - 8)
            act.wait_ge(line_out, 16)
            act.wait_ge(roped, 2 * NT)
            act.dma_start(turned_t, bass.AP(tensor=line_d.tensor, offset=line_d.offset,
                                            ap=[[1, P], [LINE, HA], [1, 2 * P]])).then_inc(bias_in, 16)
            for k in range(4):
                act.wait_ge(bias_ps, k + 1)
                act.activation(bias_t[:, 2 * k:2 * k + 2, :],
                               bank[4 + k][:, :].rearrange("p (h n) -> p h n", h=2), ACT.Copy).then_inc(bias_ok, 1)

            for h in range(HR):
                act.wait_ge(r_var, h + 1)
                act.activation(small[:, 20:24], small[:, 16:20], ACT.Sqrt).then_inc(r_sqrt, 1)
            act.wait_ge(ro_ok, HR)
            act.dma_start(wr[:, :, 0:NG], w_rg[0].rearrange("(c p) n -> p c n", p=P)).then_inc(router_in, 16)
            act.dma_start(wr[:, :, NG:NL], w_re[0].rearrange("(c p) n -> p c n", p=P)).then_inc(router_in, 16)
            act.dma_start(br[:, 0:NG], b_rg[0].partition_broadcast(P)).then_inc(router_in, 16)
            act.dma_start(br[:, NG:NL], b_re[0].partition_broadcast(P)).then_inc(router_in, 16)
            for to, g, b, done in ((ln1, ln1_g, ln1_b, ln1_in), (ln2, ln2_g, ln2_b, ln2_in)):
                act.dma_start(to[:, 0, :], g[0].partition_broadcast(P)).then_inc(done, 16)
                act.dma_start(to[:, 1, :], b[0].partition_broadcast(P)).then_inc(done, 16)

            def turned_probs(n):
                i = n // HA
                act.wait_ge(pT_ps, n + 1)
                if n >= 2:
                    act.wait_ge(o_ps, n - 1)
                act.activation(work[:, 2 + n % 2, 0:(i + 1) * P], bank[6][:, 0:(i + 1) * P],
                               ACT.Copy).then_inc(pT_ok, 1)

            for n in range(NT * HA):
                i, h = divmod(n, HA)
                act.wait_ge(max_ok, n + 1)
                if h == 0 and i >= 2:
                    act.wait_ge(o_ok, i - 1)
                a = 56 + HA * (i % 2) + h
                row = work[:, n % 2, 0:(i + 1) * P]
                act.activation(row, row, ACT.Exp, bias=small[:, 44 + n % 2:45 + n % 2],
                               accum_out=small[:, a:a + 1]).then_inc(exp_ok, 1)
                if n:
                    turned_probs(n - 1)
            turned_probs(NT * HA - 1)
            act.wait_ge(rms_var, 1)
            act.activation(small[:, 88:92], small[:, 84:88], ACT.Sqrt).then_inc(rms_sqrt, 1)
            for n in range(KC, 2 * KC):
                act_hi_of(n)
            for u in range(IN_UNITS + 4, FRONT):
                split_hi(u)

            def turned_h(n):
                i, a = divmod(n, 2)
                act.wait_ge(hT_ps, n + 1)
                act.activation(hT[:, 4 * a:4 * a + 4, i * P:(i + 1) * P],
                               bank[n % 2][:, :].rearrange("p (c n) -> p c n", c=4), ACT.Copy).then_inc(hT_ok, 1)

            for i in range(NT):
                act.wait_ge(ln_var, i + 1)
                act.activation(small[:, 104 + i:105 + i], small[:, 100 + i:101 + i], ACT.Sqrt).then_inc(ln_sqrt, 1)
                if i:
                    turned_h(2 * i - 2)
                    turned_h(2 * i - 1)
            turned_h(2 * NT - 2)
            turned_h(2 * NT - 1)
            act.wait_ge(rl_ok, 1)
            act.activation(tmp_b[:, :, 0:NG], tmp_a[:, :, 0:NG], ACT.Exp).then_inc(r_exp, 1)
            act.wait_ge(rl_ok, 2)
            act.activation(e_prob, e_log, ACT.Exp).then_inc(r_exp, 1)

            def tokens_hi(n, t):
                act.wait_ge(xg_ps, t + 1)
                for a in range(2):
                    act.activation(xgT_hi[:, a, :], bank[4 + a][:, :], ACT.Copy).then_inc(xg_hi, 1)

            def expert(t):
                def weights_hi(c):
                    s = (FRONT + c) % SPLIT
                    before_it = FRONT // RAW_FRONT if c < RAW_FRONT else 0
                    act.wait_ge(raw_in[c], t * 16 + 16 * (before_it + 1))
                    act.wait_ge(split_used, t * TU + FRONT + c - SPLIT + 1)
                    act.activation(w_hi[:, s, :], raw[:, c, :], ACT.Copy).then_inc(hi_done, 1)

                def hidden_hi(a):
                    act.wait_ge(hidT_ps, t * 2 + a + 1)
                    act.activation(hidT_hi[:, a * 256:(a + 1) * 256], bank[6 + a][:, 0:256],
                                   ACT.Copy).then_inc(hidT_hi_ok, 1)

                for c in range(TU - 1):
                    weights_hi(c)
                    if c == 3 and not isinstance(t, int):
                        rows_out(t)
                act.wait_ge(gu_ps, t + 1)
                act.activation(sig[:, 0:256], bank[0][:, 0:256], ACT.Silu).then_inc(sig_ok, 1)
                act.wait_ge(split_used, t * TU + FRONT + KC)
                act.activation(sig[:, 256:512], bank[1][:, 0:256], ACT.Silu).then_inc(sig_ok, 1)
                hidden_hi(0)
                weights_hi(TU - 1)
                hidden_hi(1)
                tokens_hi(None, t + 1)

            def rows_out(n):
                act.wait_ge(split_used, n * TU + FRONT)
                act.wait_ge(ent_cur, n)
                for a in range(2):
                    ins = act.activation(y_sb[:, a * HALF:(a + 1) * HALF], bank[2 + a][:, :], ACT.Copy,
                                         scale=s_ent[:, 2:3].bitcast(F32))
                ins.then_inc(y_ok, 1)

            act.wait_ge(tlist_ok, 1)
            n_tiles = act.value_load(tlist[0:1, MAXT:MAXT + 1], min_val=2, max_val=MAXT - 1)
            tokens_hi(None, 0)
            expert(0)
            with act.Fori(1, n_tiles) as t:
                expert(t)
            rows_out(n_tiles)
            for i in range(NT):
                act.wait_ge(f_var, i + 1)
                act.activation(small[:, 104 + i:105 + i], small[:, 100 + i:101 + i], ACT.Sqrt).then_inc(f_sqrt, 1)

        @block.gpsimd
        def _(pool):
            pool.wait_ge(xT_ps, 2 * KC)
            pool.memset(tiles, SKIP).then_inc(fill_ok, 1)
            pool.memset(xg, 0.0).then_inc(xg_zero, 1)
            pool.wait_ge(fill_ok, 1)
            rows = list_d.rearrange("(p t) w -> p t w", p=P)
            pool.dma_start(rows, tiles).then_inc(fill_out, 16)
            for i in range(NT):
                pool.wait_ge(h_ok, i + 1)
                pool.dma_start(h_d.rearrange("(i p) n -> i p n", p=P)[i], h_sb[:, i, :]).then_inc(h_out, 16)
            pool.wait_ge(fill_out, 16)
            for j in range(2):
                pool.wait_ge(ent_ok, j + 1)
                for i in range(NT):
                    pool.indirect_dma_start(
                        out=list_d, out_offset=bass.IndirectOffsetOnAxis(ap=place[:, j, i:i + 1], axis=0),
                        in_=entry[:, i, j, :], in_offset=None, bounds_check=P * MAXT - 1,
                        oob_is_err=False).then_inc(ents_out, 16)
            pool.wait_ge(ents_out, 2 * NT * 16)
            pool.dma_start(tiles, rows).then_inc(tiles_in, 16)
            pool.wait_ge(tiles_in, 16)
            pool.wait_ge(tlist_ok, 1)
            n_tiles = pool.value_load(tlist[0:1, MAXT:MAXT + 1], min_val=2, max_val=MAXT - 1)
            pool.wait_ge(h_out, NT * 16)
            pool.wait_ge(xg_zero, 1)

            def gather(t, index_ok, count):
                pool.tensor_copy(g_idx[:, :], tiles[:, bass.ds(t, 1), 0]).then_inc(index_ok, 1)
                pool.wait_ge(h_out, NT * 16)
                pool.wait_ge(index_ok, count)
                pool.indirect_dma_start(
                    out=xg, out_offset=None, in_=h_d,
                    in_offset=bass.IndirectOffsetOnAxis(ap=g_idx[:, 0:1], axis=0),
                    bounds_check=SEQ - 1, oob_is_err=False).then_inc(xg_in, 16)

            gather(0, g_idx_first, 1)
            with pool.Fori(0, n_tiles) as t:
                pool.wait_ge(xg_ps, t + 1)
                gather(t + 1, g_idx_ok, t + 1)
                pool.wait_ge(y_out, t * 16)
                pool.tensor_copy(s_ent[:, :], tiles[:, bass.ds(t, 1), :].rearrange("p a w -> p (a w)")
                                 ).then_inc(ent_cur, 1)
                pool.wait_ge(tiles_in, 16)
                pool.wait_ge(ent_cur, t + 1)
                pool.wait_ge(y_ok, t + 1)
                pool.indirect_dma_start(
                    out=y_d, out_offset=bass.IndirectOffsetOnAxis(ap=s_ent[:, 1:2], axis=0),
                    in_=y_sb, in_offset=None, bounds_check=2 * SEQ - 1, oob_is_err=False).then_inc(y_out, 16)


_INS = ["x", "w_in", "attn_out_gain", "rel_bias_table", "w_out", "ln1_g", "ln1_b", "w_router_group",
        "b_router_group", "w_router_expert", "b_router_expert", "w_gate_up", "w_down", "ln2_g", "ln2_b"]
_CONSTS = ["c_rope", "c_decay", "c_pick", "c_mats"]


def kernel(**inputs):
    import numpy as _np
    import concourse.bacc as _bacc
    from concourse import mybir as _mybir
    from concourse.bass_utils import run_bass_kernel_spmd as _run

    nc = _bacc.Bacc("TRN2", target_bir_lowering=False, num_devices=1)
    arrays, args = {}, []
    consts = shape_constants()
    for name in _INS + _CONSTS:
        a = _np.ascontiguousarray(inputs[name] if name in _INS else consts[name])
        arrays[f"in_{name}_dram"] = a
        args.append(nc.dram_tensor(f"in_{name}_dram", a.shape, _mybir.dt.from_np(a.dtype), kind="ExternalInput").ap())
    out = nc.dram_tensor("out_0_dram", (1, SEQ, D), _mybir.dt.float32, kind="ExternalOutput").ap()
    layer_kernel(nc, *args, out)
    r = _run(nc, [arrays], core_ids=[0])
    return r.results[0]["out_0_dram"]
```

```python
import math
from contextlib import ExitStack

import numpy as np

import concourse.bass as bass
from concourse import mybir

F32 = mybir.dt.float32
F32R = mybir.dt.float32r
U32 = mybir.dt.uint32
I32 = mybir.dt.int32
ALU = mybir.AluOpType
ACT = mybir.ActivationFunctionType
AX = mybir.AxisListType.X

P = 128
SEQ, D = 512, 1024
NT = SEQ // P
KC = D // P
HALF = 512
SLICES = 7
HA, DA = 8, 64
HR, DR = 4, 128
BUCKETS, MAX_DIST = 32, 128
NG, EPG = 4, 8
NE = NG * EPG
DE = 512
ALPHA = 2.0 ** 0.25
EPS = 1e-5
NEG = -1e30

IN_UNITS = SLICES * KC // 2
OUT_UNITS = 2 * KC // 2
FRONT = IN_UNITS + OUT_UNITS
TU = KC + DE // P
RAW = TU
RAW_FRONT = 6
SPLIT = 4
MAXT = 41
PIECE = 32
PIECES = P // PIECE
SKIP = 1 << 20

AQ, AK, AV, RQ, RK, RV, RG = range(SLICES)

STEPS = NT * HA
FIRST = 4 * RQ
ROPE_AT = {(16, 3): 0, (17, 3): 1, (18, 3): 2, (19, 3): 3, (20, 3): 4, (21, 1): 5, (21, 3): 6, (22, 3): 7}
BIAS_AT = 5
RET_FIRST = 4 * (4 * RV + 3) + 1


def attention_step(u, q):
    n = 3 * (u - FIRST) + q
    return n if q < 3 and 0 <= n < STEPS + 2 else None


def retention_scores(u, q):
    m = 4 * u + q - RET_FIRST
    return divmod(m, NT) if 0 <= m < HR * NT else None


def retention_sums(u, q):
    m = 4 * u + q - RET_FIRST - NT
    return m // NT if m % NT == 0 and 0 <= m < HR * NT else None

LINE = 3 * P


def shape_constants():
    f = np.float32
    half = DR // 2
    inv = f(10000.0) ** (-np.arange(half, dtype=f) / f(half))
    ang = np.arange(SEQ, dtype=f)[:, None] * inv[None, :]
    rope = np.stack([np.cos(ang), np.sin(ang)], 1).astype(f)
    gam = f(1) - np.exp(np.linspace(math.log(1 / 32), math.log(1 / 512), HR).astype(f))
    log_g = np.log(gam).astype(f)
    dist = (np.arange(SEQ)[None, :] - np.arange(P)[:, None])[:, None, :]
    decay = np.where(dist >= 0, np.exp(np.maximum(dist, 0).astype(f) * log_g[None, :, None]), 0)
    decay = (decay * DR ** -0.5).astype(f)
    n = 2 * P - 1 - np.arange(LINE)
    nf = np.maximum(n, 1).astype(f)
    ex = BUCKETS // 2
    large = ex + (np.log(nf / f(ex)) / f(math.log(MAX_DIST / ex)) * f(BUCKETS - ex)).astype(np.int32)
    bucket = np.where(n < ex, np.maximum(n, 0), np.minimum(large, BUCKETS - 1))
    pick = np.zeros((BUCKETS + 1, LINE + P), f)
    pick[bucket, np.arange(LINE)] = 1
    pick[:BUCKETS, :LINE][:, n < 0] = 0
    pick[BUCKETS, :LINE][n < 0] = NEG
    pick[BUCKETS - 1, LINE:] = 1
    r = np.arange(P)
    mats = np.zeros((P, 4 * P + 2 * NE + MAXT + NT), f)
    mats[:, 0:P] = np.eye(P)
    mats[:, P:2 * P] = r[:, None] < r[None, :]
    mats[:, 2 * P:3 * P] = 1
    e = np.arange(NE)
    mats[:NE, 3 * P:3 * P + NE] = e[:, None] < e[None, :]
    mats[:NE, 3 * P + NE:3 * P + 2 * NE] = e[:, None] <= e[None, :]
    mats[:, 3 * P + 2 * NE:-NT - P] = np.arange(MAXT)[None, :]
    mats[:, -NT - P:-NT] = np.eye(P)[::-1]
    mats[:, -NT:] = r[:, None] + P * np.arange(NT)[None, :]
    return {"c_rope": rope, "c_decay": decay, "c_pick": pick, "c_mats": mats}


def layer_kernel(nc, x, w_in, gain, rel, w_out, ln1_g, ln1_b, w_rg, b_rg, w_re, b_re, w_gu, w_dn,
                 ln2_g, ln2_b, c_rope, c_decay, c_pick, c_mats, out):
    x_d = x[0].rearrange("(i p) d -> i p d", p=P)
    out_d = out[0].rearrange("(i p) d -> i p d", p=P)
    win_d = w_in[0].rearrange("(m c p) (s n) -> s m p c n", c=2, p=P, n=HALF)
    wout_d = w_out[0].rearrange("(m c p) (a n) -> a m p c n", c=2, p=P, n=HALF)
    gu_d = w_gu[0].rearrange("e (c p) n -> e c p n", p=P)
    dn_d = w_dn[0].rearrange("e (c p) n -> e c p n", p=P)

    line_d = nc.dram_tensor("bias_line", (HA, LINE), F32).ap()
    h_d = nc.dram_tensor("h_rows", (SEQ, D), F32).ap()
    list_d = nc.dram_tensor("tile_list", (P * MAXT, 4), U32).ap()
    y_d = nc.dram_tensor("y_rows", (2 * SEQ, D), F32).ap()

    with ExitStack() as ctx:
        def sb(name, shape, dt=F32):
            return ctx.enter_context(nc.sbuf_tensor(name, shape, dt))

        def sem(name):
            return ctx.enter_context(nc.semaphore(name))

        bank = [ctx.enter_context(nc.psum_tensor(f"bank{i}", [P, HALF], F32)) for i in range(8)]

        h_sb = sb("h_sb", [P, NT, D])
        raw = sb("raw", [P, RAW, D])
        w_hi = sb("w_hi", [P, SPLIT, D], F32R)
        w_lo = sb("w_lo", [P, SPLIT, D], F32R)
        act_hi = sb("act_hi", [P, KC, SEQ], F32R)
        act_lo = sb("act_lo", [P, KC, SEQ], F32R)
        mats = sb("mats", [P, 4 * P + 2 * NE + MAXT + NT])
        ident, before, ones = mats[:, 0:P], mats[:, P:2 * P], mats[:, 2 * P:3 * P]
        e_before = mats[0:NE, 3 * P:3 * P + NE]
        e_upto = mats[0:NE, 3 * P + NE:3 * P + 2 * NE]
        iota = mats[:, 3 * P + 2 * NE:3 * P + 2 * NE + MAXT]
        flip = mats[:, 3 * P + 2 * NE + MAXT:3 * P + 2 * NE + MAXT + P]
        token = mats[:, 3 * P + 2 * NE + MAXT + P:]
        qT = sb("qT", [P, 2, HA // 2, SEQ])
        v_sb = sb("v_sb", [P, NT, HALF])
        rT = sb("rT", [P, 2, HR, SEQ])
        rv_sb = sb("rv_sb", [P, NT, HALF])
        cat = sb("cat", [P, NT, D])
        work = sb("work", [P, 4, HALF])
        gain_b = sb("gain_b", [P, HALF])
        small = sb("small", [P, 128])
        rope = gain_b[:, :].rearrange("p (i a n) -> p i a n", i=NT, a=2)
        bias_t = raw[:, 6:8, :].rearrange("p a (b n) -> p (a b) n", n=2 * P)
        decay_t = raw[:, 8:10, :].rearrange("p a (b n) -> p (a b) n", n=SEQ)
        pick = raw[0:BUCKETS + 1, 10, 0:LINE + P]
        tab = raw[0:BUCKETS + 1, 10, 512:512 + HA]
        line_s = raw[0:HA, 11, 512:512 + LINE]
        turned_t = raw[:, 10:12, :].rearrange("p a (b n) -> p (a b) n", n=2 * P)
        far = small[:, 0:HA]
        hT = qT[:, :, :, :].rearrange("p a b n -> p (a b) n")
        ln1 = rT[:, 1, :, :].rearrange("p (a b) n -> p a (b n)", a=2)
        ln2 = rT[:, 0, :, :].rearrange("p (a b) n -> p a (b n)", a=2)
        xg = v_sb[:, 0:2, :].rearrange("p a n -> p (a n)")
        y_sb = v_sb[:, 2:4, :].rearrange("p a n -> p (a n)")
        hid = rv_sb[:, 0, :]
        sig = rv_sb[:, 1, :]
        xgT_hi, xgT_lo = act_hi[:, 0:2, :], act_lo[:, 0:2, :]
        hidT_hi, hidT_lo = act_hi[:, 2, :], act_lo[:, 2, :]
        NL = NG + NE
        wr = rv_sb[:, 2, 0:KC * NL].rearrange("p (c n) -> p c n", c=KC)
        br = rv_sb[:, 3, 0:NL]
        room = cat[:, :, :].rearrange("p i n -> p (i n)")

        def by_expert(k):
            return room[:, k * NT * NE:(k + 1) * NT * NE].rearrange("p (i e) -> p i e", i=NT)

        logit = room[:, 0:NT * NL].rearrange("p (i e) -> p i e", i=NT)
        g_prob, g_mask, member, n_tl = by_expert(2), by_expert(3), by_expert(4), by_expert(5)
        ends = room[0:NE, 6 * NT * NE:6 * NT * NE + MAXT]
        e_log, e_prob, pick1, pick2 = by_expert(7), by_expert(8), by_expert(9), by_expert(10)
        rank, tmp_a, tmp_b = by_expert(11), by_expert(12), by_expert(13)
        col = room[:, 14 * NT * NE:15 * NT * NE].rearrange("p (k i) -> p k i", i=NT)
        top = room[:, 15 * NT * NE:15 * NT * NE + 2 * NT * 8].rearrange("p (k i e) -> p k i e", k=2, i=NT)
        topi = room[:, 16 * NT * NE:16 * NT * NE + 2 * NT * 8].bitcast(U32).rearrange(
            "p (k i e) -> p k i e", k=2, i=NT)
        entry = room[:, 17 * NT * NE:17 * NT * NE + 8 * NT].bitcast(U32).rearrange(
            "p (i j w) -> p i j w", i=NT, j=2)
        entry_w = room[:, 17 * NT * NE:17 * NT * NE + 8 * NT].rearrange("p (i j w) -> p i j w", i=NT, j=2)
        place = room[:, 18 * NT * NE:18 * NT * NE + 2 * NT].bitcast(U32).rearrange("p (j i) -> p j i", j=2)
        tiles = room[:, 19 * NT * NE:19 * NT * NE + 4 * MAXT].bitcast(U32).rearrange("p (t w) -> p t w", w=4)
        stats = sb("stats", [P, NT, 2, 6])
        mv = sb("mv", [P, NT, 2])
        valid = room[:, 21 * NT * NE:21 * NT * NE + MAXT]
        pieces = room[0:PIECE, 22 * NT * NE:22 * NT * NE + PIECES * MAXT * 4].bitcast(U32).rearrange(
            "p (q t w) -> p q t w", q=PIECES, w=4)
        tlist = sb("tlist", [1, MAXT + 2], I32)
        rows_of = sb("rows_of", [1, MAXT], I32)
        g_idx = sb("g_idx", [PIECE, PIECES], U32)
        s_idx = sb("s_idx", [PIECE, PIECES], U32)
        s_ent = sb("s_ent", [P, 4], U32)

        x_in, mats_in, pick_in, rope_in, decay_in, bias_in, gain_in, router_in, ln1_in, ln2_in = [
            sem(n) for n in ("x_in", "mats_in", "pick_in", "rope_in", "decay_in", "bias_in",
                             "gain_in", "router_in", "ln1_in", "ln2_in")]
        raw_in = [sem(f"raw_in{i}") for i in range(RAW)]
        hi_done, lo_done, split_used = sem("hi_done"), sem("lo_done"), sem("split_used")
        xT_ps, act_hi_ok, act_lo_ok = sem("xT_ps"), sem("act_hi_ok"), sem("act_lo_ok")
        proj_done, proj_out = sem("proj_done"), sem("proj_out")
        roped, rope_ps, rT_ok = sem("roped"), sem("rope_ps"), sem("rT_ok")
        line_ps, line_ok, line_out, far_ok = sem("line_ps"), sem("line_ok"), sem("line_out"), sem("far_ok")
        rs_ps, rs_ok, ro_ps, ro_ok, r_sqrt = (sem(n) for n in ("rs_ps", "rs_ok", "ro_ps", "ro_ok", "r_sqrt"))
        r_var = sem("r_var")
        sc_ps, max_ok, exp_ok, pT_ps, pT_ok, o_ps, o_ok = (
            sem(n) for n in ("sc_ps", "max_ok", "exp_ok", "pT_ps", "pT_ok", "o_ps", "o_ok"))
        rms_var, rms_sqrt, cat_ok, catT_ps = (sem(n) for n in ("rms_var", "rms_sqrt", "cat_ok", "catT_ps"))
        gated, ln_var, ln_sqrt, h_ok, h_out, hT_ps, hT_ok = (
            sem(n) for n in ("gated", "ln_var", "ln_sqrt", "h_ok", "h_out", "hT_ps", "hT_ok"))
        rl_ps, rl_ok, r_exp, m_ok, rank_ps, nt_ok, tb_ps, le_ok, ent_ok, fill_ok, fill_out, ents_out = (
            sem(n) for n in ("rl_ps", "rl_ok", "r_exp", "m_ok", "rank_ps", "nt_ok", "tb_ps", "le_ok",
                             "ent_ok", "fill_ok", "fill_out", "ents_out"))
        el_ps, tlist_ok, tiles_in, pool_id = sem("el_ps"), sem("tlist_ok"), sem("tiles_in"), sem("pool_id")
        g_idx_ok, xg_in, xg_ps, xg_hi, xg_ok = (sem(n) for n in ("g_idx_ok", "xg_in", "xg_ps", "xg_hi", "xg_ok"))
        gu_ps, sig_ok, hid_ok, hidT_ps, hidT_hi_ok, hidT_ok = (
            sem(n) for n in ("gu_ps", "sig_ok", "hid_ok", "hidT_ps", "hidT_hi_ok", "hidT_ok"))
        y_ps, y_ok, ent_cur, y_out = sem("y_ps"), sem("y_ok"), sem("ent_cur"), sem("y_out")
        xg_zero, g_idx_first = sem("xg_zero"), sem("g_idx_first")
        s_idx_ok = sem("s_idx_ok")
        y_in = [sem(f"y_in{i}") for i in range(2)]
        f_sum, f_var, f_sqrt, f_norm, f_gain, f_ok, out_sem = (
            sem(n) for n in ("f_sum", "f_var", "f_sqrt", "f_norm", "f_gain", "f_ok", "out_sem"))
        dve_seq = sem("dve_seq")
        valid_ok, valid_ps, rows_ok = sem("valid_ok"), sem("valid_ps"), sem("rows_ok")
        bias_ps, bias_ok = sem("bias_ps"), sem("bias_ok")

        block = ctx.enter_context(nc.Block())

        def catT_bank(c):
            return bank[6] if c < 4 else bank[c]

        def raw_slot(u):
            return u % RAW_FRONT

        def unit_view(ring, slot, u):
            return ring[:, slot, :].rearrange("p (c n) -> p c n", c=2)

        @block.sync
        def _(sp):
            for i in range(NT):
                sp.dma_start(h_sb[:, i, :], x_d[i]).then_inc(x_in, 16)
            for u in range(FRONT):
                if u >= RAW_FRONT:
                    sp.wait_ge(lo_done, u - RAW_FRONT + 1)
                s = raw_slot(u)
                src = win_d[u // 4, u % 4] if u < IN_UNITS else wout_d[(u - IN_UNITS) // 4, u % 4]
                sp.dma_start(unit_view(raw, s, u), src).then_inc(raw_in[s], 16)
            sp.wait_ge(ro_ok, HR)
            sp.dma_start(wr[:, :, 0:NG], w_rg[0].rearrange("(c p) n -> p c n", p=P)).then_inc(router_in, 16)
            sp.dma_start(wr[:, :, NG:NL], w_re[0].rearrange("(c p) n -> p c n", p=P)).then_inc(router_in, 16)
            sp.dma_start(br[:, 0:NG], b_rg[0].partition_broadcast(P)).then_inc(router_in, 16)
            sp.dma_start(br[:, NG:NL], b_re[0].partition_broadcast(P)).then_inc(router_in, 16)
            for to, g, b, done in ((ln1, ln1_g, ln1_b, ln1_in), (ln2, ln2_g, ln2_b, ln2_in)):
                sp.dma_start(to[:, 0, :], g[0].partition_broadcast(P)).then_inc(done, 16)
                sp.dma_start(to[:, 1, :], b[0].partition_broadcast(P)).then_inc(done, 16)
            for c in range(TU):
                if c < RAW_FRONT:
                    sp.wait_ge(lo_done, FRONT - RAW_FRONT + c + 1)
                elif c == RAW_FRONT:
                    sp.wait_ge(rs_ok, NT * HR)
                src = gu_d[0, c] if c < KC else dn_d[0, c - KC]
                sp.dma_start(raw[:, c, :], src).then_inc(raw_in[c], 16)
            sp.wait_ge(tlist_ok, 1)
            n_tiles = sp.value_load(tlist[0:1, MAXT:MAXT + 1], min_val=2, max_val=MAXT - 2)
            with sp.Fori(1, n_tiles) as t:
                e = sp.value_load(tlist[0:1, bass.ds(t, 1)], min_val=0, max_val=NE - 1)
                for c in range(TU):
                    sp.wait_ge(lo_done, t * TU + FRONT - TU + c + 1)
                    src = gu_d[bass.ds(e, 1), c] if c < KC else dn_d[bass.ds(e, 1), c - KC]
                    sp.dma_start(raw[:, c, :], src.rearrange("e p n -> (e p) n")).then_inc(raw_in[c], 16)

            sp.wait_ge(y_out, n_tiles * (16 * PIECES) + 16)
            y_rows = y_d.rearrange("(i p j) n -> i p (j n)", p=P, j=2)
            for i in range(NT):
                if i >= 2:
                    sp.wait_ge(f_sum, i - 1)
                sp.dma_start(raw[:, 2 * (i % 2):2 * (i % 2) + 2, :].rearrange("p a n -> p (a n)"),
                             y_rows[i]).then_inc(y_in[i % 2], 16)
            for i in range(NT):
                sp.wait_ge(f_ok, i + 1)
                sp.dma_start(out_d[i], h_sb[:, i, :]).then_inc(out_sem, 16)
            sp.wait_ge(out_sem, NT * 16)

        @block.tensor
        def _(pe):
            def passes(o, l_hi, l_lo, r_hi, r_lo, start, stop):
                pe.matmul(o, l_hi, r_hi, start=start, stop=False)
                pe.matmul(o, l_lo, r_hi, start=False, stop=False)
                return pe.matmul(o, l_hi, r_lo, start=False, stop=stop)

            pe.wait_ge(mats_in, 16)
            pe.wait_ge(x_in, NT * 16)
            for c in range(KC):
                if c >= 4:
                    pe.wait_ge(act_lo_ok, c - 3)
                for i in range(NT):
                    mm = pe.transpose(bank[4 + c % 4][:, i * P:(i + 1) * P],
                                      h_sb[:, i, c * P:(c + 1) * P], ident)
                mm.then_inc(xT_ps, 1)

            def line_products():
                pe.wait_ge(pick_in, 32)
                pe.wait_ge(line_ok, 1)
                pe.matmul(bank[4][0:HA, 0:LINE], tab, pick[:, 0:LINE], start=True, stop=True)
                pe.matmul(bank[5][:, 0:HA], pick[:, LINE:LINE + P], tab, start=True, stop=True).then_inc(line_ps, 1)

            def bias_tiles():
                pe.wait_ge(bias_in, 16)
                pe.wait_ge(far_ok, 1)
                for k in range(4):
                    pe.matmul(bank[4 + k][:, :], flip, turned_t[:, 2 * k:2 * k + 2, :], start=True,
                              stop=True).then_inc(bias_ps, 1)

            def bank6_free(turns, ropes):
                if turns:
                    pe.wait_ge(pT_ok, turns)
                if ropes:
                    pe.wait_ge(rT_ok, ropes)

            def rope_transposes(n, turns):
                pe.wait_ge(roped, n + 1)
                bank6_free(turns, n)
                for h in range(HR):
                    mm = pe.transpose(bank[6][:, h * P:(h + 1) * P],
                                      cat[:, n % NT, HALF + h * P:HALF + (h + 1) * P], ident)
                mm.then_inc(rope_ps, 1)

            def scores(n):
                i, h = divmod(n, HA)
                if n >= 2:
                    pe.wait_ge(max_ok, n - 1)
                a = DA * (h % 2)
                pe.matmul(bank[4 + n % 2][:, 0:(i + 1) * P], qT[a:a + DA, 0, h // 2, i * P:(i + 1) * P],
                          qT[a:a + DA, 1, h // 2, 0:(i + 1) * P], start=True, stop=True).then_inc(sc_ps, 1)

            def turn(n, ropes):
                i = n // HA
                pe.wait_ge(exp_ok, n + 1)
                bank6_free(n, ropes)
                for j in range(i + 1):
                    mm = pe.transpose(bank[6][:, j * P:(j + 1) * P], work[:, n % 2, j * P:(j + 1) * P], ident)
                mm.then_inc(pT_ps, 1)

            def values(n):
                i, h = divmod(n, HA)
                pe.wait_ge(pT_ok, n + 1)
                if h == 0 and i:
                    pe.wait_ge(o_ok, i)
                for j in range(i + 1):
                    mm = pe.matmul(bank[7][:, h * DA:(h + 1) * DA], work[:, 2 + n % 2, j * P:(j + 1) * P],
                                   v_sb[:, j, h * DA:(h + 1) * DA], start=(j == 0), stop=(j == i))
                mm.then_inc(o_ps, 1)

            def ret_scores(h, j):
                n = NT * h + j
                if n < 2:
                    pe.wait_ge(max_ok, STEPS - 1 + n)
                    pe.wait_ge(rT_ok, 2 * NT)
                else:
                    pe.wait_ge(rs_ok, n - 1)
                pe.matmul(bank[4 + n % 2][:, 0:SEQ - j * P], rT[:, 1, h, j * P:(j + 1) * P],
                          rT[:, 0, h, j * P:SEQ], start=True, stop=True).then_inc(rs_ps, 1)

            def ret_sums(h):
                if h:
                    pe.wait_ge(ro_ok, h)
                else:
                    pe.wait_ge(o_ok, NT)
                    pe.wait_ge(proj_out, 4 * RV + 4)
                pe.wait_ge(rs_ok, NT * h + NT)
                for i in range(NT):
                    for j in range(i + 1):
                        mm = pe.matmul(bank[7][:, i * P:(i + 1) * P],
                                       work[:, j, (i - j) * P:(i - j + 1) * P],
                                       rv_sb[:, j, h * P:(h + 1) * P], start=(j == 0), stop=(j == i))
                mm.then_inc(ro_ps, 1)

            def cat_transposes(c):
                for i in range(NT):
                    mm = pe.transpose(catT_bank(c)[:, i * P:(i + 1) * P], cat[:, i, c * P:(c + 1) * P], ident)
                mm.then_inc(xT_ps, 1)

            ropes = 0
            for u in range(FRONT):
                s, m = divmod(u, 4)
                pe.wait_ge(lo_done, u + 1)
                if u == 0:
                    pe.wait_ge(act_lo_ok, KC)
                if u == IN_UNITS:
                    pe.wait_ge(act_lo_ok, KC + 4)
                wh, wl = unit_view(w_hi, u % SPLIT, u), unit_view(w_lo, u % SPLIT, u)
                for q in range(4):
                    cut = slice(q * P, (q + 1) * P)
                    to = bank[4 + q] if s == SLICES + 1 else bank[q]
                    if m == 0 and s and s <= SLICES:
                        pe.wait_ge(proj_out, 4 * (s - 1) + q + 1)
                    for cc in range(2):
                        k = 2 * m + cc
                        first, last = k == 0, k == KC - 1
                        if s in (AQ, AK):
                            mm = passes(to[:, :], wh[:, cc, cut], wl[:, cc, cut],
                                        act_hi[:, k, :], act_lo[:, k, :], first, last)
                        else:
                            mm = passes(to[:, :], act_hi[:, k, cut], act_lo[:, k, cut],
                                        wh[:, cc, :], wl[:, cc, :], first, last)
                    if m == 3 and q < 3:
                        mm.then_inc(proj_done, 1)
                    if q == 3:
                        mm.then_inc(split_used, 1)
                    n = attention_step(u, q)
                    if n == 0:
                        pe.wait_ge(bias_ok, 4)
                        pe.wait_ge(proj_out, 4 * AV + 4)
                    if (u, q) in ROPE_AT:
                        rope_transposes(ROPE_AT[u, q], 3 * (u - FIRST) + min(q, 3) - 1)
                        ropes += 1
                    if n is not None:
                        if n < STEPS:
                            scores(n)
                        if 1 <= n <= STEPS:
                            turn(n - 1, ropes)
                        if n >= 2:
                            values(n - 2)
                    if retention_sums(u, q) is not None:
                        ret_sums(retention_sums(u, q))
                    if retention_scores(u, q) is not None:
                        ret_scores(*retention_scores(u, q))
                    if u == IN_UNITS - 2:
                        if q == 0:
                            pe.wait_ge(cat_ok, NT)
                        else:
                            pe.wait_ge(act_lo_ok, KC + q)
                        cat_transposes(q)
                if u == 0:
                    line_products()
                if u == BIAS_AT:
                    bias_tiles()
                if u == IN_UNITS + 1:
                    pe.wait_ge(gated, NT)
                    for c in range(4, KC):
                        cat_transposes(c)
                    pe.wait_ge(act_lo_ok, 2 * KC)

            for i in range(NT):
                pe.wait_ge(h_ok, i + 1)
                for a in range(2):
                    n = 2 * i + a
                    if n >= 2:
                        pe.wait_ge(hT_ok, n - 1)
                    for c in range(4):
                        mm = pe.transpose(bank[n % 2][:, c * P:(c + 1) * P],
                                          h_sb[:, i, (4 * a + c) * P:(4 * a + c + 1) * P], ident)
                    mm.then_inc(hT_ps, 1)
            pe.wait_ge(router_in, 64)
            for i in range(NT):
                pe.wait_ge(hT_ok, 2 * i + 2)
                for c in range(KC):
                    mm = pe.matmul(bank[2][:, i * NL:(i + 1) * NL], hT[:, c, i * P:(i + 1) * P],
                                   wr[:, c, :], start=(c == 0), stop=(c == KC - 1))
            mm.then_inc(rl_ps, 1)

            pe.wait_ge(m_ok, 1)
            M = member
            for i in range(NT):
                for k in range(i + 1):
                    pe.matmul(bank[3][:, i * NE:(i + 1) * NE], before if k == i else ones, M[:, k, :],
                              start=(k == 0), stop=(k == i))
            for k in range(NT):
                mm = pe.matmul(bank[4][0:NE, 0:P], M[:, k, :], ones, start=(k == 0), stop=(k == NT - 1))
            mm.then_inc(rank_ps, 1)
            pe.wait_ge(nt_ok, 1)
            ntl = n_tl[0:NE].rearrange("p i e -> p (i e)")
            pe.matmul(bank[5][:, 0:NE], ntl, e_before, start=True, stop=True)
            pe.matmul(bank[6][0:NE, 0:P], e_upto, ntl, start=True, stop=True)
            pe.matmul(bank[7][0:1, MAXT:MAXT + 1], ones[0:NE, 0:1], ntl[:, 0:1], start=True,
                      stop=True).then_inc(tb_ps, 1)
            pe.wait_ge(le_ok, 1)
            pe.matmul(bank[7][0:1, 0:MAXT], ones[0:NE, 0:1], ends, start=True, stop=True).then_inc(el_ps, 1)

            pe.wait_ge(valid_ok, 1)
            pe.matmul(bank[7][0:1, 0:MAXT], ones[:, 0:1], valid, start=True, stop=True).then_inc(valid_ps, 1)

            def gathered(t):
                pe.wait_ge(xg_in, t * 16 * PIECES + 16 * PIECES)
                for c in range(KC):
                    mm = pe.transpose(bank[4 + c // 4][:, (c % 4) * P:(c % 4 + 1) * P],
                                      xg[:, c * P:(c + 1) * P], ident)
                mm.then_inc(xg_ps, 1)

            pe.wait_ge(tlist_ok, 1)
            n_tiles = pe.value_load(tlist[0:1, MAXT:MAXT + 1], min_val=2, max_val=MAXT - 2)
            gathered(0)
            with pe.Fori(0, n_tiles) as t:
                pe.wait_ge(xg_ok, t * 2 + 2)
                pe.wait_ge(hid_ok, t * 2 + 2)

                def gate_up(c, a):
                    slot = (FRONT + c) % SPLIT
                    cut = slice((c % 4) * P, (c % 4 + 1) * P)
                    cols = [w[:, slot, :].rearrange("p (g n) -> p g n", g=2)[:, :, a * 256:(a + 1) * 256]
                            for w in (w_hi, w_lo)]
                    return passes(bank[a][:, :].rearrange("p (g n) -> p g n", g=2), xgT_hi[:, c // 4, cut],
                                  xgT_lo[:, c // 4, cut], cols[0], cols[1], c == 0, c == KC - 1)

                for c in range(KC - 2):
                    pe.wait_ge(lo_done, t * TU + FRONT + c + 1)
                    gate_up(c, 0)
                    gate_up(c, 1).then_inc(split_used, 1)
                pe.wait_ge(lo_done, t * TU + FRONT + KC)
                gate_up(KC - 2, 0)
                gate_up(KC - 1, 0).then_inc(gu_ps, 1)
                gate_up(KC - 2, 1).then_inc(split_used, 1)
                gate_up(KC - 1, 1).then_inc(split_used, 1)

                def turn_hidden(a):
                    pe.wait_ge(hid_ok, t * 2 + a + 3)
                    for k in range(2):
                        mm = pe.transpose(bank[6 + a][:, k * P:(k + 1) * P],
                                          hid[:, (2 * a + k) * P:(2 * a + k + 1) * P], ident)
                    mm.then_inc(hidT_ps, 1)

                turn_hidden(0)
                gathered(t + 1)
                pe.wait_ge(y_ok, t + 1)
                for k in range(4):
                    if k == 1:
                        turn_hidden(1)
                    if k % 2 == 0:
                        pe.wait_ge(hidT_ok, t * 2 + k // 2 + 1)
                    pe.wait_ge(lo_done, t * TU + FRONT + KC + k + 1)
                    slot = (FRONT + KC + k) % SPLIT
                    cut = slice(k * P, (k + 1) * P)
                    for a in range(2):
                        cols = slice(a * HALF, (a + 1) * HALF)
                        mm = passes(bank[2 + a][:, :], hidT_hi[:, cut], hidT_lo[:, cut],
                                    w_hi[:, slot, cols], w_lo[:, slot, cols], k == 0, k == 3)
                    mm.then_inc(split_used, 1)

        @block.vector
        def _(dve):
            seq = [0]

            def step(ins):
                seq[0] += 1
                ins.then_inc(dve_seq, 1)
                dve.wait_ge(dve_seq, seq[0])

            def split_lo(u):
                dve.wait_ge(hi_done, u + 1)
                dve.tensor_tensor(w_lo[:, u % SPLIT, :], raw[:, raw_slot(u), :],
                                  w_hi[:, u % SPLIT, :].bitcast(F32), ALU.subtract).then_inc(lo_done, 1)

            def act_lo_of(n):
                c = n % KC
                dve.wait_ge(act_hi_ok, n + 1)
                b = bank[4 + c % 4] if n < KC else catT_bank(c)
                dve.tensor_tensor(act_lo[:, c, :], b[:, :], act_hi[:, c, :].bitcast(F32),
                                  ALU.subtract).then_inc(act_lo_ok, 1)

            dve.memset(tab[:, :], 1.0).then_inc(line_ok, 1)
            for n in range(KC):
                act_lo_of(n)
                if n % 2 and n < 2 * RAW_FRONT - 6:
                    split_lo(n // 2)
            dve.wait_ge(line_ps, 1)
            dve.tensor_copy(line_s, bank[4][0:HA, 0:LINE]).then_inc(line_ok, 1)
            dve.tensor_copy(far, bank[5][:, 0:HA]).then_inc(far_ok, 1)

            def rope_rows(s, i):
                if i < 3:
                    dve.wait_ge(proj_done, 3 * s + i + 1)
                else:
                    dve.wait_ge(split_used, 4 * s + 4)
                if s == RK:
                    dve.wait_ge(rope_ps, i + 1)
                t = bank[i][:, :].rearrange("p (h a n) -> p h a n", h=HR, a=2)
                o = cat[:, i, HALF:D].rearrange("p (h a n) -> p h a n", h=HR, a=2)
                x1 = rv_sb[:, i, :].rearrange("p (h a n) -> p h a n", h=HR, a=2)
                cos = rope[:, i, 0:1, :].to_broadcast([P, HR, DR // 2])
                sin = rope[:, i, 1:2, :].to_broadcast([P, HR, DR // 2])
                dve.tensor_tensor(o[:, :, 0, :], t[:, :, 0, :], cos, ALU.mult)
                dve.tensor_tensor(o[:, :, 1, :], t[:, :, 1, :], cos, ALU.mult)
                dve.tensor_tensor(x1[:, :, 0, :], t[:, :, 1, :], sin, ALU.mult)
                dve.tensor_tensor(x1[:, :, 1, :], t[:, :, 0, :], sin, ALU.mult).then_inc(proj_out, 1)

            scale = DA ** -0.5

            def logits(n):
                i, h = divmod(n, HA)
                dve.wait_ge(sc_ps, n + 1)
                if n == 0:
                    dve.wait_ge(bias_ok, 4)
                if n >= 2:
                    dve.wait_ge(pT_ps, n - 1)
                lg, s_b = work[:, n % 2, :], bank[4 + n % 2]
                near = max(0, (i - 1) * P)
                if near:
                    dve.tensor_scalar(lg[:, 0:near], s_b[:, 0:near], scale, far[:, h:h + 1],
                                      ALU.mult, ALU.add)
                step(dve.scalar_tensor_tensor(
                    out=lg[:, near:(i + 1) * P], in0=s_b[:, near:(i + 1) * P], scalar=scale,
                    in1=bias_t[:, h, P if i == 0 else 0:2 * P], op0=ALU.mult, op1=ALU.add))
                step(dve.tensor_reduce(small[:, 40 + n % 2:41 + n % 2], lg[:, 0:(i + 1) * P], AX, ALU.max))
                dve.tensor_scalar(small[:, 44 + n % 2:45 + n % 2], small[:, 40 + n % 2:41 + n % 2], -1.0,
                                  None, ALU.mult).then_inc(max_ok, 1)

            def scaled_sums(i):
                dve.wait_ge(o_ps, HA * (i + 1))
                inv = small[:, 48:48 + HA]
                step(dve.reciprocal(inv, small[:, 56 + HA * (i % 2):56 + HA * (i % 2) + HA]))
                a_o = cat[:, i, 0:HALF].rearrange("p (h n) -> p h n", h=HA)
                dve.tensor_tensor(a_o, bank[7][:, :].rearrange("p (h n) -> p h n", h=HA),
                                  inv.unsqueeze(2).to_broadcast([P, HA, DA]), ALU.mult).then_inc(o_ok, 1)
                dve.wait_ge(o_ok, i + 1)

            def decayed(h, j):
                n = NT * h + j
                if n == 0:
                    dve.wait_ge(decay_in, 16)
                dve.wait_ge(rs_ps, n + 1)
                if j == 0 and h:
                    dve.wait_ge(ro_ps, h)
                dve.tensor_tensor(work[:, j, 0:SEQ - j * P], bank[4 + n % 2][:, 0:SEQ - j * P],
                                  decay_t[:, h, 0:SEQ - j * P], ALU.mult).then_inc(rs_ok, 1)

            rcol = small[:, 32:32 + 4]

            def group_norm(h):
                dve.wait_ge(ro_ps, h + 1)
                o = bank[7][:, :].rearrange("p (i n) -> p i n", i=NT)
                for i in range(NT):
                    ins = dve.bn_stats(stats[:, i, 0, :], o[:, i, :])
                step(ins)
                for i in range(NT):
                    ins = dve.bn_aggr(mv[:, i, :], stats[:, i, 0, :])
                step(ins)
                dve.tensor_scalar(small[:, 16:20], mv[:, :, 1], EPS, None, ALU.add).then_inc(r_var, 1)
                dve.wait_ge(r_sqrt, h + 1)
                step(dve.reciprocal(rcol, small[:, 20:24]))
                for i in range(NT):
                    ins = dve.tensor_scalar(cat[:, i, HALF + h * P:HALF + (h + 1) * P], o[:, i, :],
                                            mv[:, i, 0:1], rcol[:, i:i + 1], ALU.subtract, ALU.mult)
                ins.then_inc(ro_ok, 1)

            def rms_sums():
                for i in range(NT):
                    ins = dve.tensor_tensor_reduce(v_sb[:, i, :], cat[:, i, 0:HALF], cat[:, i, 0:HALF], 1.0, 0.0,
                                                   ALU.mult, ALU.add, small[:, 80 + i:81 + i])
                step(ins)
                dve.tensor_scalar(small[:, 84:88], small[:, 80:84], 1.0 / HALF, EPS, ALU.mult,
                                  ALU.add).then_inc(rms_var, 1)

            def rms_normed():
                dve.wait_ge(rms_sqrt, 1)
                step(dve.reciprocal(small[:, 92:96], small[:, 88:92]))
                dve.wait_ge(gain_in, 16)
                for i in range(NT):
                    dve.scalar_tensor_tensor(out=cat[:, i, 0:HALF], in0=cat[:, i, 0:HALF],
                                             scalar=small[:, 92 + i:93 + i], in1=gain_b[:, :],
                                             op0=ALU.mult, op1=ALU.mult).then_inc(cat_ok, 1)

            def mixed(a, i):
                s = SLICES + a
                if i < 3:
                    dve.wait_ge(proj_done, 3 * s + i + 1)
                else:
                    dve.wait_ge(split_used, 4 * s + 4)
                cols = slice(a * HALF, (a + 1) * HALF)
                return dve.scalar_tensor_tensor(out=h_sb[:, i, cols], in0=h_sb[:, i, cols], scalar=ALPHA,
                                                in1=bank[4 * a + i][:, :], op0=ALU.mult, op1=ALU.add)

            for u in range(FRONT):
                for q in range(4):
                    if q == 1 and 3 <= u + 3 < FRONT:
                        split_lo(u + 3)
                    n = attention_step(u, q)
                    if n is not None and n < STEPS:
                        logits(n)
                    if u // 4 in (RQ, RK) and u % 4 == 3:
                        if u == 4 * RQ + 3 and q == 0:
                            dve.wait_ge(rope_in, 16)
                        rope_rows(u // 4, q)
                    if n is not None and n >= HA + 1 and (n - 1) % HA == 0:
                        scaled_sums((n - 1) // HA - 1)
                    if retention_scores(u, q) is not None:
                        decayed(*retention_scores(u, q))
                    if retention_sums(u, q) is not None:
                        group_norm(retention_sums(u, q))
                    if (u, q) == (IN_UNITS - 4, 2):
                        rms_sums()
                    if (u, q) == (IN_UNITS - 3, 0):
                        rms_normed()
                    if u == IN_UNITS - 2:
                        act_lo_of(KC + q)
                    if u == IN_UNITS:
                        dve.wait_ge(ro_ok, HR)
                        dve.wait_ge(proj_out, 4 * RG + q + 1)
                        dve.tensor_tensor(cat[:, q, HALF:D], cat[:, q, HALF:D], v_sb[:, q, :],
                                          ALU.mult).then_inc(gated, 1)
                    if u == IN_UNITS + 4 + 1:
                        mixed(0, q)
                if u == IN_UNITS + 1:
                    for c in range(4, KC):
                        act_lo_of(KC + c)

            def norm_sums(i, done):
                for a in range(2):
                    ins = dve.bn_stats(stats[:, i, a, :], h_sb[:, i, a * HALF:(a + 1) * HALF])
                step(ins)
                step(dve.bn_aggr(mv[:, i, :], stats[:, i, :, :]))
                dve.tensor_scalar(small[:, 100 + i:101 + i], mv[:, i, 1:2], EPS, None, ALU.add).then_inc(done, 1)

            def normed(i, g_b, root, done, n):
                dve.wait_ge(root, i + 1)
                step(dve.reciprocal(small[:, 108 + i:109 + i], small[:, 104 + i:105 + i]))
                step(dve.tensor_scalar(h_sb[:, i, :], h_sb[:, i, :], mv[:, i, 0:1], small[:, 108 + i:109 + i],
                                       ALU.subtract, ALU.mult))
                step(dve.tensor_tensor(h_sb[:, i, :], h_sb[:, i, :], g_b[:, 0, :], ALU.mult))
                dve.tensor_tensor(h_sb[:, i, :], h_sb[:, i, :], g_b[:, 1, :], ALU.add).then_inc(done, 1)

            for i in range(NT):
                step(mixed(1, i))
                norm_sums(i, ln_var)
                if i == 0:
                    dve.wait_ge(ln1_in, 32)
                if i:
                    normed(i - 1, ln1, ln_sqrt, h_ok, i - 1)
            normed(NT - 1, ln1, ln_sqrt, h_ok, NT - 1)

            dve.wait_ge(rl_ps, 1)
            dve.wait_ge(router_in, 64)
            step(dve.tensor_tensor(logit, bank[2][:, 0:NT * NL].rearrange("p (i e) -> p i e", i=NT),
                                   br.unsqueeze(1).to_broadcast([P, NT, NL]), ALU.add))

            def over(c, n):
                return c.unsqueeze(2).to_broadcast([P, NT, n])

            dve.memset(g_prob[:, :, NG:8], -1.0)
            step(dve.tensor_reduce(col[:, 0, :], logit[:, :, 0:NG], AX, ALU.max))
            dve.tensor_tensor(tmp_a[:, :, 0:NG], logit[:, :, 0:NG], over(col[:, 0, :], NG),
                              ALU.subtract).then_inc(rl_ok, 1)
            dve.wait_ge(r_exp, 1)
            step(dve.tensor_reduce(col[:, 1, :], tmp_b[:, :, 0:NG], AX, ALU.add))
            step(dve.reciprocal(col[:, 2, :], col[:, 1, :]))
            step(dve.tensor_tensor(g_prob[:, :, 0:NG], tmp_b[:, :, 0:NG], over(col[:, 2, :], NG), ALU.mult))
            for i in range(NT):
                ins = dve.max(top[:, 0, i, :], g_prob[:, i, 0:8])
            step(ins)
            for i in range(NT):
                ins = dve.max_index(topi[:, 0, i, :], top[:, 0, i, :], g_prob[:, i, 0:8])
            step(ins)
            dve.tensor_copy(col[:, 3, :], top[:, 0, :, 0])
            step(dve.tensor_copy(col[:, 4, :], topi[:, 0, :, 0]))
            step(dve.tensor_tensor(tmp_a[:, :, 0:NG], iota[:, 0:NG].unsqueeze(1).to_broadcast([P, NT, NG]),
                                   over(col[:, 4, :], NG), ALU.is_equal))
            spread = tmp_a[:, :, 0:NG].unsqueeze(3).to_broadcast([P, NT, NG, EPG])
            step(dve.tensor_copy(g_mask.rearrange("p i (g e) -> p i g e", g=NG), spread))
            step(dve.tensor_scalar(tmp_b, g_mask, -NEG, NEG, ALU.mult, ALU.add))
            step(dve.tensor_tensor(e_log, logit[:, :, NG:NL], g_mask, ALU.mult))
            step(dve.tensor_tensor(e_log, e_log, tmp_b, ALU.add))
            step(dve.tensor_reduce(col[:, 5, :], e_log, AX, ALU.max))
            dve.tensor_tensor(e_log, e_log, over(col[:, 5, :], NE), ALU.subtract).then_inc(rl_ok, 1)
            dve.wait_ge(r_exp, 2)
            step(dve.tensor_reduce(col[:, 6, :], e_prob, AX, ALU.add))
            step(dve.reciprocal(col[:, 7, :], col[:, 6, :]))
            dve.tensor_scalar(tmp_b, g_mask, -1.0, None, ALU.add)
            step(dve.tensor_tensor(e_prob, e_prob, over(col[:, 7, :], NE), ALU.mult))
            step(dve.tensor_tensor(e_prob, e_prob, tmp_b, ALU.add))
            for i in range(NT):
                ins = dve.max(top[:, 1, i, :], e_prob[:, i, :])
            step(ins)
            for i in range(NT):
                ins = dve.max_index(topi[:, 1, i, :], top[:, 1, i, :], e_prob[:, i, :])
            step(ins)
            for j in range(2):
                ins = dve.tensor_copy(col[:, 8 + j, :], topi[:, 1, :, j])
            step(ins)
            for j, o in enumerate((pick1, pick2)):
                ins = dve.tensor_tensor(o, iota[:, 0:NE].unsqueeze(1).to_broadcast([P, NT, NE]),
                                        over(col[:, 8 + j, :], NE), ALU.is_equal)
            step(ins)
            dve.tensor_tensor(member, pick1, pick2, ALU.add).then_inc(m_ok, 1)
            step(dve.tensor_tensor(col[:, 10, :], top[:, 1, :, 0], top[:, 1, :, 1], ALU.add))
            step(dve.reciprocal(col[:, 11, :], col[:, 10, :]))
            for j in range(2):
                ins = dve.tensor_tensor(col[:, 12 + j, :], top[:, 1, :, j], col[:, 11, :], ALU.mult)
            step(ins)
            dve.memset(entry[:, :, :, 3], 0)
            for j in range(2):
                dve.tensor_tensor(entry_w[:, :, j, 2], col[:, 12 + j, :], col[:, 3, :], ALU.mult)
                dve.tensor_copy(entry[:, :, j, 0], token)
                ins = dve.tensor_scalar(entry[:, :, j, 1], token, 2.0, float(j), ALU.mult, ALU.add)
            step(ins)

            dve.wait_ge(rank_ps, 1)
            counts = bank[4][0:NE, 0:P]
            ntl = n_tl[0:NE].rearrange("p i e -> p (i e)")
            step(dve.tensor_scalar(ntl, counts, 0.0, None, ALU.is_gt))
            for k in range(1, NT):
                step(dve.scalar_tensor_tensor(out=ntl, in0=counts, scalar=float(k * P), in1=ntl,
                                              op0=ALU.is_gt, op1=ALU.add))
            dve.tensor_scalar(ntl[0:1, :], ntl[0:1, :], 1.0, None, ALU.max).then_inc(nt_ok, 1)
            step(dve.tensor_copy(rank, bank[3][:, 0:NT * NE].rearrange("p (i e) -> p i e", i=NT)))
            dve.wait_ge(tb_ps, 1)
            step(dve.tensor_copy(small[0:NE, 120:121], bank[6][0:NE, 0:1]))
            dve.tensor_scalar(ends, iota[0:NE, 0:MAXT], small[0:NE, 120:121], None, ALU.is_ge).then_inc(le_ok, 1)
            tb = bank[5][:, 0:NE].unsqueeze(1).to_broadcast([P, NT, NE])
            for j, pk in enumerate((pick1, pick2)):
                dve.tensor_tensor(tmp_a, pk, rank, ALU.mult)
                step(dve.tensor_tensor(tmp_b, pk, tb, ALU.mult))
                dve.tensor_reduce(col[:, 14, :], tmp_a, AX, ALU.add)
                step(dve.tensor_reduce(col[:, 15, :], tmp_b, AX, ALU.add))
                step(dve.tensor_scalar(col[:, 16, :], col[:, 14, :], float(P), None, ALU.is_ge))
                for k in range(2, NT):
                    step(dve.scalar_tensor_tensor(out=col[:, 16, :], in0=col[:, 14, :], scalar=float(k * P),
                                                  in1=col[:, 16, :], op0=ALU.is_ge, op1=ALU.add))
                step(dve.tensor_tensor(col[:, 15, :], col[:, 15, :], col[:, 16, :], ALU.add))
                step(dve.scalar_tensor_tensor(out=col[:, 14, :], in0=col[:, 16, :], scalar=-float(P),
                                              in1=col[:, 14, :], op0=ALU.mult, op1=ALU.add))
                step(dve.scalar_tensor_tensor(out=col[:, 17 + j, :], in0=col[:, 14, :], scalar=float(MAXT),
                                              in1=col[:, 15, :], op0=ALU.mult, op1=ALU.add))
                dve.tensor_copy(place[:, j, :], col[:, 17 + j, :]).then_inc(ent_ok, 1)
            dve.wait_ge(el_ps, 1)
            step(dve.tensor_scalar(tlist[0:1, 0:MAXT], bank[7][0:1, 0:MAXT], float(NE - 1), None, ALU.min))
            dve.tensor_copy(tlist[0:1, MAXT:MAXT + 1], bank[7][0:1, MAXT:MAXT + 1]).then_inc(tlist_ok, 1)
            dve.wait_ge(tlist_ok, 1)
            n_tiles = dve.value_load(tlist[0:1, MAXT:MAXT + 1], min_val=2, max_val=MAXT - 2)

            dve.wait_ge(tiles_in, 16 * (1 + PIECES))
            dve.tensor_scalar(valid, tiles[:, :, 0], float(SEQ), None, ALU.is_lt).then_inc(valid_ok, 1)
            dve.wait_ge(valid_ps, 1)
            dve.tensor_copy(rows_of[0:1, :], bank[7][0:1, 0:MAXT]).then_inc(rows_ok, 1)
            dve.memset(sig[:, 0:1], 0.0).then_inc(hid_ok, 2)
            dve.memset(hid[:, 0:1], 0.0).then_inc(y_ok, 1)

            def tokens_lo(n):
                for a in range(2):
                    dve.wait_ge(xg_hi, n + a + 1)
                    dve.tensor_tensor(xgT_lo[:, a, :], bank[4 + a][:, :], xgT_hi[:, a, :].bitcast(F32),
                                      ALU.subtract).then_inc(xg_ok, 1)

            tokens_lo(0)
            with dve.Fori(0, n_tiles) as t:
                def weights_lo(c):
                    s = (FRONT + c) % SPLIT
                    dve.wait_ge(hi_done, t * TU + FRONT + c + 1)
                    dve.tensor_tensor(w_lo[:, s, :], raw[:, c, :], w_hi[:, s, :].bitcast(F32),
                                      ALU.subtract).then_inc(lo_done, 1)

                def hidden_lo(a):
                    dve.wait_ge(hidT_hi_ok, t * 2 + a + 1)
                    cut = slice(a * 256, (a + 1) * 256)
                    dve.tensor_tensor(hidT_lo[:, cut], bank[6 + a][:, 0:256], hidT_hi[:, cut].bitcast(F32),
                                      ALU.subtract).then_inc(hidT_ok, 1)

                for c in range(TU - 2):
                    weights_lo(c)
                for a in range(2):
                    dve.wait_ge(sig_ok, t * 2 + a + 1)
                    cut = slice(a * 256, (a + 1) * 256)
                    dve.tensor_tensor(hid[:, cut], sig[:, cut], bank[a][:, 256:512],
                                      ALU.mult).then_inc(hid_ok, 1)
                hidden_lo(0)
                weights_lo(TU - 2)
                hidden_lo(1)
                weights_lo(TU - 1)
                tokens_lo(t * 2 + 2)

            for i in range(NT):
                dve.wait_ge(y_in[i % 2], 16 * (i // 2 + 1))
                yr = raw[:, 2 * (i % 2):2 * (i % 2) + 2, :]
                step(dve.scalar_tensor_tensor(out=h_sb[:, i, :], in0=h_sb[:, i, :], scalar=ALPHA,
                                              in1=yr[:, 0, :], op0=ALU.mult, op1=ALU.add))
                dve.tensor_tensor(h_sb[:, i, :], h_sb[:, i, :], yr[:, 1, :], ALU.add).then_inc(f_sum, 1)
                dve.wait_ge(f_sum, i + 1)
                norm_sums(i, f_var)
                if i == 0:
                    dve.wait_ge(ln2_in, 32)
                if i:
                    normed(i - 1, ln2, f_sqrt, f_ok, i - 1)
            normed(NT - 1, ln2, f_sqrt, f_ok, NT - 1)

        @block.scalar
        def _(act):
            act.dma_start(mats[:, :], c_mats).then_inc(mats_in, 16)
            act.dma_start(pick, c_pick).then_inc(pick_in, 16)
            act.wait_ge(line_ok, 1)
            act.dma_start(tab[0:BUCKETS, :], rel).then_inc(pick_in, 16)
            act.dma_start(rope, c_rope.rearrange("(i p) a n -> p i a n", p=P)).then_inc(rope_in, 16)
            act.dma_start(decay_t, c_decay).then_inc(decay_in, 16)

            def split_hi(u):
                s = raw_slot(u)
                act.wait_ge(raw_in[s], 16 * (u // RAW_FRONT + 1))
                if u >= SPLIT:
                    act.wait_ge(split_used, u - SPLIT + 1)
                act.activation(w_hi[:, u % SPLIT, :], raw[:, s, :], ACT.Copy).then_inc(hi_done, 1)

            def act_hi_of(n):
                c = n % KC
                act.wait_ge(xT_ps, n + 1)
                b = bank[4 + c % 4] if n < KC else catT_bank(c)
                act.activation(act_hi[:, c, :], b[:, :], ACT.Copy).then_inc(act_hi_ok, 1)

            for n in range(KC):
                act_hi_of(n)
                if n % 2 and n < 2 * RAW_FRONT - 6:
                    split_hi(n // 2)
            def rotated(n):
                act.wait_ge(rope_ps, n + 1)
                q, i = divmod(n, NT)
                act.activation(rT[:, q, :, i * P:(i + 1) * P], bank[6][:, :].rearrange("p (h n) -> p h n", h=HR),
                               ACT.Copy).then_inc(rT_ok, 1)

            def slice_out(s, b):
                if b < 3:
                    act.wait_ge(proj_done, 3 * s + b + 1)
                else:
                    act.wait_ge(split_used, 4 * s + 4)
                o, f = {AQ: (qT[:, 0, b, :], ACT.Copy), AK: (qT[:, 1, b, :], ACT.Copy),
                        AV: (v_sb[:, b, :], ACT.Copy), RV: (rv_sb[:, b, :], ACT.Copy),
                        RG: (v_sb[:, b, :], ACT.Silu)}[s]
                act.activation(o, bank[b][:, :], f).then_inc(proj_out, 1)

            def exponentials(n):
                i, h = divmod(n, HA)
                act.wait_ge(max_ok, n + 1)
                if h == 0 and i >= 2:
                    act.wait_ge(o_ok, i - 1)
                a = 56 + HA * (i % 2) + h
                row = work[:, n % 2, 0:(i + 1) * P]
                act.activation(row, row, ACT.Exp, bias=small[:, 44 + n % 2:45 + n % 2],
                               accum_out=small[:, a:a + 1]).then_inc(exp_ok, 1)

            def turned_probs(n):
                i = n // HA
                act.wait_ge(pT_ps, n + 1)
                if n >= 2:
                    act.wait_ge(o_ps, n - 1)
                act.activation(work[:, 2 + n % 2, 0:(i + 1) * P], bank[6][:, 0:(i + 1) * P],
                               ACT.Copy).then_inc(pT_ok, 1)

            for u in range(FRONT):
                for q in range(4):
                    if q == 0 and 3 <= u + 3 < FRONT:
                        split_hi(u + 3)
                    if (u, q) in ROPE_AT:
                        rotated(ROPE_AT[u, q])
                    n = attention_step(u, q)
                    if n is not None and n < STEPS:
                        exponentials(n)
                    if n is not None and 1 <= n <= STEPS:
                        turned_probs(n - 1)
                    if u % 4 == 3 and u // 4 in (AQ, AK, AV, RV, RG):
                        slice_out(u // 4, q)
                    if retention_sums(u, q) is not None:
                        act.wait_ge(r_var, retention_sums(u, q) + 1)
                        act.activation(small[:, 20:24], small[:, 16:20], ACT.Sqrt).then_inc(r_sqrt, 1)
                    if (u, q) == (IN_UNITS - 4, 2):
                        act.wait_ge(rms_var, 1)
                        act.activation(small[:, 88:92], small[:, 84:88], ACT.Sqrt).then_inc(rms_sqrt, 1)
                    if u == IN_UNITS - 2:
                        act_hi_of(KC + q)
                if u == 1:
                    act.wait_ge(line_ok, 2)
                    act.dma_start(line_d, line_s).then_inc(line_out, 16)
                if u == 2:
                    act.wait_ge(line_out, 16)
                    act.dma_start(turned_t, bass.AP(tensor=line_d.tensor, offset=line_d.offset,
                                                    ap=[[1, P], [LINE, HA], [1, 2 * P]])).then_inc(bias_in, 16)
                if u == BIAS_AT:
                    for k in range(4):
                        act.wait_ge(bias_ps, k + 1)
                        act.activation(bias_t[:, 2 * k:2 * k + 2, :],
                                       bank[4 + k][:, :].rearrange("p (h n) -> p h n", h=2),
                                       ACT.Copy).then_inc(bias_ok, 1)
                if u == 4 * RV:
                    act.wait_ge(roped, 2 * NT)
                    act.dma_start(gain_b[:, :], gain[0].partition_broadcast(P)).then_inc(gain_in, 16)
                if u == IN_UNITS + 1:
                    for c in range(4, KC):
                        act_hi_of(KC + c)

            def turned_h(n):
                i, a = divmod(n, 2)
                act.wait_ge(hT_ps, n + 1)
                act.activation(hT[:, 4 * a:4 * a + 4, i * P:(i + 1) * P],
                               bank[n % 2][:, :].rearrange("p (c n) -> p c n", c=4), ACT.Copy).then_inc(hT_ok, 1)

            for i in range(NT):
                act.wait_ge(ln_var, i + 1)
                act.activation(small[:, 104 + i:105 + i], small[:, 100 + i:101 + i], ACT.Sqrt).then_inc(ln_sqrt, 1)
                if i:
                    turned_h(2 * i - 2)
                    turned_h(2 * i - 1)
            turned_h(2 * NT - 2)
            turned_h(2 * NT - 1)
            act.wait_ge(rl_ok, 1)
            act.activation(tmp_b[:, :, 0:NG], tmp_a[:, :, 0:NG], ACT.Exp).then_inc(r_exp, 1)
            act.wait_ge(rl_ok, 2)
            act.activation(e_prob, e_log, ACT.Exp).then_inc(r_exp, 1)

            def tokens_hi(n, t):
                act.wait_ge(xg_ps, t + 1)
                for a in range(2):
                    act.activation(xgT_hi[:, a, :], bank[4 + a][:, :], ACT.Copy).then_inc(xg_hi, 1)

            def expert(t):
                def weights_hi(c):
                    s = (FRONT + c) % SPLIT
                    before_it = FRONT // RAW_FRONT if c < RAW_FRONT else 0
                    act.wait_ge(raw_in[c], t * 16 + 16 * (before_it + 1))
                    act.wait_ge(split_used, t * TU + FRONT + c - SPLIT + 1)
                    act.activation(w_hi[:, s, :], raw[:, c, :], ACT.Copy).then_inc(hi_done, 1)

                def hidden_hi(a):
                    act.wait_ge(hidT_ps, t * 2 + a + 1)
                    act.activation(hidT_hi[:, a * 256:(a + 1) * 256], bank[6 + a][:, 0:256],
                                   ACT.Copy).then_inc(hidT_hi_ok, 1)

                for c in range(TU - 2):
                    weights_hi(c)
                    if c == 3 and not isinstance(t, int):
                        rows_out(t)
                act.wait_ge(gu_ps, t + 1)
                act.activation(sig[:, 0:256], bank[0][:, 0:256], ACT.Silu).then_inc(sig_ok, 1)
                act.wait_ge(split_used, t * TU + FRONT + KC)
                act.activation(sig[:, 256:512], bank[1][:, 0:256], ACT.Silu).then_inc(sig_ok, 1)
                hidden_hi(0)
                weights_hi(TU - 2)
                hidden_hi(1)
                weights_hi(TU - 1)
                tokens_hi(None, t + 1)

            def rows_out(n):
                act.wait_ge(split_used, n * TU + FRONT)
                act.wait_ge(ent_cur, n)
                for a in range(2):
                    ins = act.activation(y_sb[:, a * HALF:(a + 1) * HALF], bank[2 + a][:, :], ACT.Copy,
                                         scale=s_ent[:, 2:3].bitcast(F32))
                ins.then_inc(y_ok, 1)

            act.wait_ge(tlist_ok, 1)
            n_tiles = act.value_load(tlist[0:1, MAXT:MAXT + 1], min_val=2, max_val=MAXT - 2)
            tokens_hi(None, 0)
            expert(0)
            with act.Fori(1, n_tiles) as t:
                expert(t)
            rows_out(n_tiles)
            for i in range(NT):
                act.wait_ge(f_var, i + 1)
                act.activation(small[:, 104 + i:105 + i], small[:, 100 + i:101 + i], ACT.Sqrt).then_inc(f_sqrt, 1)

        @block.gpsimd
        def _(pool):
            for n in range(2 * NT):
                s, i = RQ + n // NT, n % NT
                o = cat[:, i, HALF:D].rearrange("p (h a n) -> p h a n", h=HR, a=2)
                x1 = rv_sb[:, i, :].rearrange("p (h a n) -> p h a n", h=HR, a=2)
                pool.wait_ge(proj_out, 4 * s + i + 1)
                pool.tensor_tensor(o[:, :, 0, :], o[:, :, 0, :], x1[:, :, 0, :], ALU.subtract)
                pool.tensor_tensor(o[:, :, 1, :], o[:, :, 1, :], x1[:, :, 1, :], ALU.add).then_inc(roped, 1)
            pool.wait_ge(xT_ps, 2 * KC)
            pool.memset(tiles, SKIP).then_inc(fill_ok, 1)
            pool.memset(xg, 0.0).then_inc(xg_zero, 1)
            pool.wait_ge(fill_ok, 1)
            rows = list_d.rearrange("(p t) w -> p t w", p=P)
            pool.dma_start(rows, tiles).then_inc(y_out, 16)
            for i in range(NT):
                pool.wait_ge(h_ok, i + 1)
                pool.dma_start(h_d.rearrange("(i p) n -> i p n", p=P)[i], h_sb[:, i, :]).then_inc(h_out, 16)
            pool.wait_ge(y_out, 16)
            for j in range(2):
                pool.wait_ge(ent_ok, j + 1)
                for i in range(NT):
                    pool.indirect_dma_start(
                        out=list_d, out_offset=bass.IndirectOffsetOnAxis(ap=place[:, j, i:i + 1], axis=0),
                        in_=entry[:, i, j, :], in_offset=None, bounds_check=P * MAXT - 1,
                        oob_is_err=False).then_inc(ents_out, 16)
            pool.wait_ge(ents_out, 2 * NT * 16)
            pool.dma_start(tiles, rows).then_inc(tiles_in, 16)
            for q in range(PIECES):
                pool.dma_start(pieces[:, q, :, :], list_d.rearrange("(q p t) w -> q p t w", q=PIECES, p=PIECE)[q]
                               ).then_inc(tiles_in, 16)
            pool.wait_ge(tiles_in, 16 * (1 + PIECES))
            pool.wait_ge(tlist_ok, 1)
            n_tiles = pool.value_load(tlist[0:1, MAXT:MAXT + 1], min_val=2, max_val=MAXT - 2)
            pool.wait_ge(h_out, NT * 16)
            pool.wait_ge(rows_ok, 1)
            pool.wait_ge(xg_zero, 1)

            last_token, last_row = pool.alloc_register("last_token"), pool.alloc_register("last_row")
            pool.reg_mov(last_token, SEQ - 1)
            pool.reg_mov(last_row, 2 * SEQ - 1)

            def for_pieces(n_rows, copy, done):
                copy(0)
                for q in range(1, PIECES):
                    with pool.If(n_rows > q * PIECE):
                        copy(q)
                    with pool.Else():
                        pool.inc_swdge_sem([done], [16])

            def gather(t, index_ok, count):
                n_rows = pool.value_load(rows_of[0:1, bass.ds(t, 1)], min_val=0, max_val=P)
                pool.tensor_copy(g_idx[:, :], pieces[:, :, bass.ds(t, 1), 0].rearrange("p q t -> p (q t)")
                                 ).then_inc(index_ok, 1)
                pool.wait_ge(h_out, NT * 16)
                pool.wait_ge(index_ok, count)

                def copy(q):
                    pool.indirect_dma_start(
                        out=xg[q * PIECE:(q + 1) * PIECE, :], out_offset=None, in_=h_d,
                        in_offset=bass.IndirectOffsetOnAxis(ap=g_idx[:, q:q + 1], axis=0),
                        bounds_check=last_token, oob_is_err=False).then_inc(xg_in, 16)

                for_pieces(n_rows, copy, xg_in)

            pool.memset(s_idx[:, :], SKIP).then_inc(s_idx_ok, 1)
            gather(0, g_idx_first, 1)
            pool.wait_ge(xg_ps, 1)
            gather(1, g_idx_ok, 1)
            with pool.Fori(0, n_tiles) as t:
                pool.wait_ge(y_out, t * (16 * PIECES) + 16)
                pool.wait_ge(tiles_in, 16 * (1 + PIECES))
                n_rows = pool.value_load(rows_of[0:1, bass.ds(t, 1)], min_val=0, max_val=P)
                pool.tensor_copy(s_ent[:, :], tiles[:, bass.ds(t, 1), :].rearrange("p a w -> p (a w)")
                                 ).then_inc(ent_cur, 1)
                pool.wait_ge(xg_ps, t + 2)
                gather(t + 2, g_idx_ok, t + 2)
                pool.wait_ge(y_ok, t + 2)
                pool.tensor_copy(s_idx[:, :], pieces[:, :, bass.ds(t, 1), 1].rearrange("p q t -> p (q t)")
                                 ).then_inc(s_idx_ok, 1)
                pool.wait_ge(tiles_in, 16 * (1 + PIECES))
                pool.wait_ge(s_idx_ok, t + 2)

                def copy(q):
                    pool.indirect_dma_start(
                        out=y_d, out_offset=bass.IndirectOffsetOnAxis(ap=s_idx[:, q:q + 1], axis=0),
                        in_=y_sb[q * PIECE:(q + 1) * PIECE, :], in_offset=None, bounds_check=last_row,
                        oob_is_err=False).then_inc(y_out, 16)

                for_pieces(n_rows, copy, y_out)


_INS = ["x", "w_in", "attn_out_gain", "rel_bias_table", "w_out", "ln1_g", "ln1_b", "w_router_group",
        "b_router_group", "w_router_expert", "b_router_expert", "w_gate_up", "w_down", "ln2_g", "ln2_b"]
_CONSTS = ["c_rope", "c_decay", "c_pick", "c_mats"]


def kernel(**inputs):
    import numpy as _np
    import concourse.bacc as _bacc
    from concourse import mybir as _mybir
    from concourse.bass_utils import run_bass_kernel_spmd as _run

    nc = _bacc.Bacc("TRN2", target_bir_lowering=False, num_devices=1)
    arrays, args = {}, []
    consts = shape_constants()
    for name in _INS + _CONSTS:
        a = _np.ascontiguousarray(inputs[name] if name in _INS else consts[name])
        arrays[f"in_{name}_dram"] = a
        args.append(nc.dram_tensor(f"in_{name}_dram", a.shape, _mybir.dt.from_np(a.dtype), kind="ExternalInput").ap())
    out = nc.dram_tensor("out_0_dram", (1, SEQ, D), _mybir.dt.float32, kind="ExternalOutput").ap()
    layer_kernel(nc, *args, out)
    r = _run(nc, [arrays], core_ids=[0])
    return r.results[0]["out_0_dram"]
```

```python
import math
from contextlib import ExitStack

import numpy as np

import concourse.bass as bass
from concourse import mybir

F32 = mybir.dt.float32
F32R = mybir.dt.float32r
U32 = mybir.dt.uint32
I32 = mybir.dt.int32
ALU = mybir.AluOpType
ACT = mybir.ActivationFunctionType
AX = mybir.AxisListType.X

P = 128
SEQ, D = 512, 1024
NT = SEQ // P
KC = D // P
HALF = 512
SLICES = 7
HA, DA = 8, 64
HR, DR = 4, 128
BUCKETS, MAX_DIST = 32, 128
NG, EPG = 4, 8
NE = NG * EPG
DE = 512
ALPHA = 2.0 ** 0.25
EPS = 1e-5
NEG = -1e30

IN_UNITS = SLICES * KC // 2
OUT_UNITS = 2 * KC // 2
FRONT = IN_UNITS + OUT_UNITS
TU = KC + DE // P
RAW = TU
RAW_FRONT = 6
SPLIT = 4
MAXT = 41
PIECE = 32
PIECES = P // PIECE
SKIP = 1 << 20

AQ, AK, AV, RQ, RK, RV, RG = range(SLICES)

STEPS = NT * HA
FIRST = 4 * RQ
ROPE_AT = {(16, 3): 0, (17, 3): 1, (18, 3): 2, (19, 3): 3, (20, 3): 4, (21, 1): 5, (21, 3): 6, (22, 3): 7}
BIAS_AT = 6
RET_FIRST = 4 * (4 * RV + 3) + 1


def attention_step(u, q):
    n = 3 * (u - FIRST) + q
    return n if q < 3 and 0 <= n < STEPS + 2 else None


def retention_scores(u, q):
    m = 4 * u + q - RET_FIRST
    return divmod(m, NT) if 0 <= m < HR * NT else None


def retention_sums(u, q):
    m = 4 * u + q - RET_FIRST - NT
    return m // NT if m % NT == 0 and 0 <= m < HR * NT else None

LINE = 3 * P


def shape_constants():
    f = np.float32
    half = DR // 2
    inv = f(10000.0) ** (-np.arange(half, dtype=f) / f(half))
    ang = np.arange(SEQ, dtype=f)[:, None] * inv[None, :]
    rope = np.stack([np.cos(ang), np.sin(ang)], 1).astype(f)
    gam = f(1) - np.exp(np.linspace(math.log(1 / 32), math.log(1 / 512), HR).astype(f))
    log_g = np.log(gam).astype(f)
    dist = (np.arange(SEQ)[None, :] - np.arange(P)[:, None])[:, None, :]
    decay = np.where(dist >= 0, np.exp(np.maximum(dist, 0).astype(f) * log_g[None, :, None]), 0)
    decay = (decay * DR ** -0.5).astype(f)
    n = 2 * P - 1 - np.arange(LINE)
    nf = np.maximum(n, 1).astype(f)
    ex = BUCKETS // 2
    large = ex + (np.log(nf / f(ex)) / f(math.log(MAX_DIST / ex)) * f(BUCKETS - ex)).astype(np.int32)
    bucket = np.where(n < ex, np.maximum(n, 0), np.minimum(large, BUCKETS - 1))
    pick = np.zeros((BUCKETS + 1, LINE + P), f)
    pick[bucket, np.arange(LINE)] = 1
    pick[:BUCKETS, :LINE][:, n < 0] = 0
    pick[BUCKETS, :LINE][n < 0] = NEG
    pick[BUCKETS - 1, LINE:] = 1
    r = np.arange(P)
    mats = np.zeros((P, 5 * P + 2 * NE + 2 * NT), f)
    mats[:, 0:P] = np.eye(P)
    mats[:, P:2 * P] = r[:, None] < r[None, :]
    mats[:, 2 * P:3 * P] = 1
    e = np.arange(NE)
    mats[:NE, 3 * P:3 * P + NE] = e[:, None] < e[None, :]
    mats[:NE, 3 * P + NE:3 * P + 2 * NE] = e[:, None] <= e[None, :]
    mats[:, 3 * P + 2 * NE:4 * P + 2 * NE] = np.arange(P)[None, :]
    mats[:, 4 * P + 2 * NE:5 * P + 2 * NE] = np.eye(P)[::-1]
    mats[:, 5 * P + 2 * NE:-NT] = r[:, None] + P * np.arange(NT)[None, :]
    mats[:, -NT:] = P * np.arange(NT)[None, :]
    mats[0, -NT] = -1
    return {"c_rope": rope, "c_decay": decay, "c_pick": pick, "c_mats": mats}


def layer_kernel(nc, x, w_in, gain, rel, w_out, ln1_g, ln1_b, w_rg, b_rg, w_re, b_re, w_gu, w_dn,
                 ln2_g, ln2_b, c_rope, c_decay, c_pick, c_mats, out):
    x_d = x[0].rearrange("(i p) d -> i p d", p=P)
    out_d = out[0].rearrange("(i p) d -> i p d", p=P)
    win_d = w_in[0].rearrange("(m c p) (s n) -> s m p c n", c=2, p=P, n=HALF)
    wout_d = w_out[0].rearrange("(m c p) (a n) -> a m p c n", c=2, p=P, n=HALF)
    gu_d = w_gu[0].rearrange("e (c p) n -> e c p n", p=P)
    dn_d = w_dn[0].rearrange("e (c p) n -> e c p n", p=P)

    line_d = nc.dram_tensor("bias_line", (HA, LINE), F32).ap()
    h_d = nc.dram_tensor("h_rows", (SEQ, D), F32).ap()
    y_d = nc.dram_tensor("y_rows", (2 * SEQ, D), F32).ap()

    with ExitStack() as ctx:
        def sb(name, shape, dt=F32):
            return ctx.enter_context(nc.sbuf_tensor(name, shape, dt))

        def sem(name):
            return ctx.enter_context(nc.semaphore(name))

        bank = [ctx.enter_context(nc.psum_tensor(f"bank{i}", [P, HALF], F32)) for i in range(8)]

        h_sb = sb("h_sb", [P, NT, D])
        raw = sb("raw", [P, RAW, D])
        w_hi = sb("w_hi", [P, SPLIT, D], F32R)
        w_lo = sb("w_lo", [P, SPLIT, D], F32R)
        act_hi = sb("act_hi", [P, KC, SEQ], F32R)
        act_lo = sb("act_lo", [P, KC, SEQ], F32R)
        mats = sb("mats", [P, 5 * P + 2 * NE + 2 * NT])
        ident, before, ones = mats[:, 0:P], mats[:, P:2 * P], mats[:, 2 * P:3 * P]
        e_before = mats[0:NE, 3 * P:3 * P + NE]
        e_upto = mats[0:NE, 3 * P + NE:3 * P + 2 * NE]
        iota = mats[:, 3 * P + 2 * NE:4 * P + 2 * NE]
        flip = mats[:, 4 * P + 2 * NE:5 * P + 2 * NE]
        token = mats[:, 5 * P + 2 * NE:5 * P + 2 * NE + NT]
        thresholds = mats[:, 5 * P + 2 * NE + NT:]
        qT = sb("qT", [P, 2, HA // 2, SEQ])
        v_sb = sb("v_sb", [P, NT, HALF])
        rT = sb("rT", [P, 2, HR, SEQ])
        rv_sb = sb("rv_sb", [P, NT, HALF])
        cat = sb("cat", [P, NT, D])
        work = sb("work", [P, 4, HALF])
        gain_b = sb("gain_b", [P, HALF])
        small = sb("small", [P, 128])
        rope = gain_b[:, :].rearrange("p (i a n) -> p i a n", i=NT, a=2)
        bias_t = raw[:, 6:8, :].rearrange("p a (b n) -> p (a b) n", n=2 * P)
        decay_t = raw[:, 8:10, :].rearrange("p a (b n) -> p (a b) n", n=SEQ)
        pick = raw[0:BUCKETS + 1, 10, 0:LINE + P]
        tab = raw[0:BUCKETS + 1, 10, 512:512 + HA]
        line_s = raw[0:HA, 11, 512:512 + LINE]
        turned_t = raw[:, 10:12, :].rearrange("p a (b n) -> p (a b) n", n=2 * P)
        far = small[:, 0:HA]
        hT = qT[:, :, :, :].rearrange("p a b n -> p (a b) n")
        ln1 = rT[:, 1, :, :].rearrange("p (a b) n -> p a (b n)", a=2)
        ln2 = rT[:, 0, :, :].rearrange("p (a b) n -> p a (b n)", a=2)
        xg = v_sb[:, 0:2, :].rearrange("p a n -> p (a n)")
        y_sb = v_sb[:, 2:4, :].rearrange("p a n -> p (a n)")
        hid = rv_sb[:, 0, :]
        sig = rv_sb[:, 1, :]
        xgT_hi, xgT_lo = act_hi[:, 0:2, :], act_lo[:, 0:2, :]
        hidT_hi, hidT_lo = act_hi[:, 2, :], act_lo[:, 2, :]
        NL = NG + NE
        wr = rv_sb[:, 2, 0:KC * NL].rearrange("p (c n) -> p c n", c=KC)
        br = rv_sb[:, 3, 0:NL]
        room = cat[:, :, :].rearrange("p i n -> p (i n)")

        def by_expert(k):
            return room[:, k * NT * NE:(k + 1) * NT * NE].rearrange("p (i e) -> p i e", i=NT)

        logit = room[:, 0:NT * NL].rearrange("p (i e) -> p i e", i=NT)
        g_prob, g_mask, member, n_tl = by_expert(2), by_expert(3), by_expert(4), by_expert(5)
        ends = room[0:NE, 6 * NT * NE:6 * NT * NE + MAXT]
        e_log, e_prob, pick1, pick2 = by_expert(7), by_expert(8), by_expert(9), by_expert(10)
        rank, tmp_a, tmp_b = by_expert(11), by_expert(12), by_expert(13)
        col = room[:, 14 * NT * NE:15 * NT * NE].rearrange("p (k i) -> p k i", i=NT)
        top = room[:, 15 * NT * NE:15 * NT * NE + 2 * NT * 8].rearrange("p (k i e) -> p k i e", k=2, i=NT)
        topi = room[:, 16 * NT * NE:16 * NT * NE + 2 * NT * 8].bitcast(U32).rearrange(
            "p (k i e) -> p k i e", k=2, i=NT)
        earlier = by_expert(17)
        everyone = room[:, 18 * NT * NE:18 * NT * NE + NE]

        def by_pick(k):
            return room[:, k * NT * NE:(k + 2) * NT * NE].rearrange("p (j i e) -> p j i e", j=2, i=NT)

        picks, of_rank, of_tile = by_pick(9), by_pick(19), by_pick(21)
        entry = room[:, 23 * NT * NE:23 * NT * NE + 4 * NT].rearrange("p (n w) -> p n w", w=2)
        dest = room[:, 24 * NT * NE:24 * NT * NE + MAXT]
        weight = room[:, 25 * NT * NE:25 * NT * NE + MAXT]
        valid = room[:, 26 * NT * NE:26 * NT * NE + MAXT]
        piece_to = room[0:PIECE, 27 * NT * NE:27 * NT * NE + PIECES * MAXT].bitcast(U32).rearrange(
            "p (q t) -> p q t", q=PIECES)
        piece_from = room[0:PIECE, 29 * NT * NE:29 * NT * NE + PIECES * MAXT].bitcast(U32).rearrange(
            "p (q t) -> p q t", q=PIECES)
        row_hot = hT[:, 0:2, :].rearrange("p a (n r) -> p (a n) r", r=P)
        tile_hot = hT[:, 2:4, :].rearrange("p a n -> p (a n)")[:, 0:2 * NT * MAXT].rearrange(
            "p (n t) -> p n t", t=MAXT)
        tile_val = hT[:, 4:6, :].rearrange("p a n -> p (a n)")[:, 0:4 * NT * MAXT].rearrange(
            "p (n w t) -> p n w t", w=2, t=MAXT)
        stats = sb("stats", [P, NT, 2, 6])
        mv = sb("mv", [P, NT, 2])
        tlist = sb("tlist", [1, MAXT + 2], I32)
        rows_of = sb("rows_of", [1, MAXT], I32)
        g_idx = sb("g_idx", [PIECE, PIECES], U32)
        s_idx = sb("s_idx", [PIECE, PIECES], U32)
        s_weight = sb("s_weight", [P, 1])

        x_in = [sem(f"x_in{a}") for a in range(2)]
        mats_in, pick_in, rope_in, decay_in, bias_in, gain_in, router_in, ln1_in, ln2_in = [
            sem(n) for n in ("mats_in", "pick_in", "rope_in", "decay_in", "bias_in",
                             "gain_in", "router_in", "ln1_in", "ln2_in")]
        raw_in = [sem(f"raw_in{i}") for i in range(RAW)]
        hi_done, lo_done, split_used = sem("hi_done"), sem("lo_done"), sem("split_used")
        xT_ps, act_hi_ok, act_lo_ok = sem("xT_ps"), sem("act_hi_ok"), sem("act_lo_ok")
        proj_done, proj_out = sem("proj_done"), sem("proj_out")
        roped, rope_ps, rT_ok = sem("roped"), sem("rope_ps"), sem("rT_ok")
        line_ps, line_ok, line_out, far_ok = sem("line_ps"), sem("line_ok"), sem("line_out"), sem("far_ok")
        rs_ps, rs_ok, ro_ps, ro_ok, r_sqrt = (sem(n) for n in ("rs_ps", "rs_ok", "ro_ps", "ro_ok", "r_sqrt"))
        r_var = sem("r_var")
        sc_ps, max_ok, exp_ok, pT_ps, pT_ok, o_ps, o_ok = (
            sem(n) for n in ("sc_ps", "max_ok", "exp_ok", "pT_ps", "pT_ok", "o_ps", "o_ok"))
        rms_var, rms_sqrt, cat_ok = (sem(n) for n in ("rms_var", "rms_sqrt", "cat_ok"))
        gated, ln_var, ln_sqrt, h_ok, h_out, hT_ps, hT_ok = (
            sem(n) for n in ("gated", "ln_var", "ln_sqrt", "h_ok", "h_out", "hT_ps", "hT_ok"))
        rl_ps, rl_ok, r_exp, m_ok, count_ps, rank_ps, nt_ok, tb_ps, le_ok, hot_ok, list_ps = (
            sem(n) for n in ("rl_ps", "rl_ok", "r_exp", "m_ok", "count_ps", "rank_ps", "nt_ok", "tb_ps", "le_ok",
                             "hot_ok", "list_ps"))
        el_ps, tlist_ok, lists_ok = sem("el_ps"), sem("tlist_ok"), sem("lists_ok")
        g_idx_ok, xg_in, xg_ps, xg_hi, xg_ok = (sem(n) for n in ("g_idx_ok", "xg_in", "xg_ps", "xg_hi", "xg_ok"))
        gu_ps, sig_ok, hid_ok, hidT_ps, hidT_hi_ok, hidT_ok = (
            sem(n) for n in ("gu_ps", "sig_ok", "hid_ok", "hidT_ps", "hidT_hi_ok", "hidT_ok"))
        y_ok, weight_cur, y_out = sem("y_ok"), sem("weight_cur"), sem("y_out")
        xg_zero, g_idx_first = sem("xg_zero"), sem("g_idx_first")
        s_idx_ok = sem("s_idx_ok")
        y_in = [sem(f"y_in{i}") for i in range(NT)]
        f_sum, f_var, f_sqrt, f_norm, f_gain, f_ok, f_added, y_added, out_sem, f_mean, f_root, eps_ok = (
            sem(n) for n in ("f_sum", "f_var", "f_sqrt", "f_norm", "f_gain", "f_ok", "f_added", "y_added", "out_sem",
                             "f_mean", "f_root", "eps_ok"))
        dve_seq = sem("dve_seq")
        valid_ok, valid_ps, rows_ok = sem("valid_ok"), sem("valid_ps"), sem("rows_ok")
        bias_ps, bias_ok = sem("bias_ps"), sem("bias_ok")

        block = ctx.enter_context(nc.Block())

        def catT_bank(c):
            return bank[6] if c < 4 else bank[c]

        def raw_slot(u):
            return u % RAW_FRONT

        def unit_view(ring, slot, u):
            return ring[:, slot, :].rearrange("p (c n) -> p c n", c=2)

        @block.sync
        def _(sp):

            def x_half(a):
                for i in range(NT):
                    cols = slice(a * HALF, (a + 1) * HALF)
                    sp.dma_start(h_sb[:, i, cols], x_d[i][:, cols]).then_inc(x_in[a], 16)

            x_half(0)
            for u in range(FRONT):
                if u == 1:
                    x_half(1)
                if u >= RAW_FRONT:
                    sp.wait_ge(lo_done, u - RAW_FRONT + 1)
                s = raw_slot(u)
                src = win_d[u // 4, u % 4] if u < IN_UNITS else wout_d[(u - IN_UNITS) // 4, u % 4]
                sp.dma_start(unit_view(raw, s, u), src).then_inc(raw_in[s], 16)
            sp.wait_ge(ro_ok, HR)
            sp.dma_start(wr[:, :, 0:NG], w_rg[0].rearrange("(c p) n -> p c n", p=P)).then_inc(router_in, 16)
            sp.dma_start(wr[:, :, NG:NL], w_re[0].rearrange("(c p) n -> p c n", p=P)).then_inc(router_in, 16)
            sp.dma_start(br[:, 0:NG], b_rg[0].partition_broadcast(P)).then_inc(router_in, 16)
            sp.dma_start(br[:, NG:NL], b_re[0].partition_broadcast(P)).then_inc(router_in, 16)
            for to, g, b, done in ((ln1, ln1_g, ln1_b, ln1_in), (ln2, ln2_g, ln2_b, ln2_in)):
                sp.dma_start(to[:, 0, :], g[0].partition_broadcast(P)).then_inc(done, 16)
                sp.dma_start(to[:, 1, :], b[0].partition_broadcast(P)).then_inc(done, 16)
            for c in range(TU):
                if c < RAW_FRONT:
                    sp.wait_ge(lo_done, FRONT - RAW_FRONT + c + 1)
                elif c == RAW_FRONT:
                    sp.wait_ge(rs_ok, NT * HR)
                src = gu_d[0, c] if c < KC else dn_d[0, c - KC]
                sp.dma_start(raw[:, c, :], src).then_inc(raw_in[c], 16)
            sp.wait_ge(tlist_ok, 1)
            n_tiles = sp.value_load(tlist[0:1, MAXT:MAXT + 1], min_val=2, max_val=MAXT - 2)
            sp.wait_ge(xg_in, 16 * PIECES)
            with sp.Fori(1, n_tiles) as t:
                e = sp.value_load(tlist[0:1, bass.ds(t, 1)], min_val=0, max_val=NE - 1)
                last_e = sp.value_load(tlist[0:1, bass.ds(t - 1, 1)], min_val=0, max_val=NE - 1)
                with sp.If(e > last_e):
                    for c in range(TU):
                        sp.wait_ge(lo_done, t * TU + FRONT - TU + c + 1)
                        src = gu_d[bass.ds(e, 1), c] if c < KC else dn_d[bass.ds(e, 1), c - KC]
                        sp.dma_start(raw[:, c, :], src.rearrange("e p n -> (e p) n")).then_inc(raw_in[c], 16)
                with sp.Else():
                    for c in range(TU):
                        sp.wait_ge(lo_done, t * TU + FRONT - TU + c + 1)
                        sp.sem_inc(raw_in[c], 16)

            sp.wait_ge(y_out, n_tiles * (16 * PIECES) + 16)
            y_rows = y_d.rearrange("(i p j) n -> i p (j n)", p=P, j=2)
            for i in range(NT):
                sp.dma_start(raw[:, 2 * i:2 * i + 2, :].rearrange("p a n -> p (a n)"),
                             y_rows[i]).then_inc(y_in[i], 16)
            for i in range(NT):
                sp.wait_ge(f_added, i + 1)
                if i >= 2:
                    sp.wait_ge(f_ok, i - 1)
                sp.dma_start(out_d[i], h_sb[:, i, :]).then_inc(out_sem, 16)
            sp.wait_ge(out_sem, NT * 16)

        @block.tensor
        def _(pe):
            def passes(o, l_hi, l_lo, r_hi, r_lo, start, stop):
                pe.matmul(o, l_hi, r_hi, start=start, stop=False)
                pe.matmul(o, l_lo, r_hi, start=False, stop=False)
                return pe.matmul(o, l_hi, r_lo, start=False, stop=stop)

            pe.wait_ge(mats_in, 16)
            pe.wait_ge(x_in[0], NT * 16)

            def x_transposes(c):
                if c == 4:
                    pe.wait_ge(x_in[1], NT * 16)
                if c >= 4:
                    pe.wait_ge(act_lo_ok, c - 3)
                for i in range(NT):
                    mm = pe.transpose(bank[4 + c % 4][:, i * P:(i + 1) * P],
                                      h_sb[:, i, c * P:(c + 1) * P], ident)
                mm.then_inc(xT_ps, 1)

            for c in range(4):
                x_transposes(c)

            def line_products():
                pe.wait_ge(pick_in, 32)
                pe.wait_ge(line_ok, 1)
                pe.matmul(bank[4][0:HA, 0:LINE], tab, pick[:, 0:LINE], start=True, stop=True)
                pe.matmul(bank[5][:, 0:HA], pick[:, LINE:LINE + P], tab, start=True, stop=True).then_inc(line_ps, 1)

            def bias_tiles():
                pe.wait_ge(bias_in, 16)
                pe.wait_ge(far_ok, 1)
                for k in range(4):
                    pe.matmul(bank[4 + k][:, :], flip, turned_t[:, 2 * k:2 * k + 2, :], start=True,
                              stop=True).then_inc(bias_ps, 1)

            def bank6_free(turns, ropes):
                if turns:
                    pe.wait_ge(pT_ok, turns)
                if ropes:
                    pe.wait_ge(rT_ok, ropes)

            def rope_transposes(n, turns):
                pe.wait_ge(roped, n + 1)
                bank6_free(turns, n)
                for h in range(HR):
                    mm = pe.transpose(bank[6][:, h * P:(h + 1) * P],
                                      cat[:, n % NT, HALF + h * P:HALF + (h + 1) * P], ident)
                mm.then_inc(rope_ps, 1)

            def scores(n):
                i, h = divmod(n, HA)
                if n >= 2:
                    pe.wait_ge(max_ok, n - 1)
                a = DA * (h % 2)
                pe.matmul(bank[4 + n % 2][:, 0:(i + 1) * P], qT[a:a + DA, 0, h // 2, i * P:(i + 1) * P],
                          qT[a:a + DA, 1, h // 2, 0:(i + 1) * P], start=True, stop=True).then_inc(sc_ps, 1)

            def turn(n, ropes):
                i = n // HA
                pe.wait_ge(exp_ok, n + 1)
                bank6_free(n, ropes)
                for j in range(i + 1):
                    mm = pe.transpose(bank[6][:, j * P:(j + 1) * P], work[:, n % 2, j * P:(j + 1) * P], ident)
                mm.then_inc(pT_ps, 1)

            def values(n):
                i, h = divmod(n, HA)
                pe.wait_ge(pT_ok, n + 1)
                if h == 0 and i:
                    pe.wait_ge(o_ok, i)
                for j in range(i + 1):
                    mm = pe.matmul(bank[7][:, h * DA:(h + 1) * DA], work[:, 2 + n % 2, j * P:(j + 1) * P],
                                   v_sb[:, j, h * DA:(h + 1) * DA], start=(j == 0), stop=(j == i))
                mm.then_inc(o_ps, 1)

            def ret_scores(h, j):
                n = NT * h + j
                if n < 2:
                    pe.wait_ge(max_ok, STEPS - 1 + n)
                    pe.wait_ge(rT_ok, 2 * NT)
                else:
                    pe.wait_ge(rs_ok, n - 1)
                pe.matmul(bank[4 + n % 2][:, 0:SEQ - j * P], rT[:, 1, h, j * P:(j + 1) * P],
                          rT[:, 0, h, j * P:SEQ], start=True, stop=True).then_inc(rs_ps, 1)

            def ret_sums(h):
                if h:
                    pe.wait_ge(ro_ok, h)
                else:
                    pe.wait_ge(o_ok, NT)
                    pe.wait_ge(proj_out, 4 * RV + 4)
                pe.wait_ge(rs_ok, NT * h + NT)
                for i in range(NT):
                    for j in range(i + 1):
                        mm = pe.matmul(bank[7][:, i * P:(i + 1) * P],
                                       work[:, j, (i - j) * P:(i - j + 1) * P],
                                       rv_sb[:, j, h * P:(h + 1) * P], start=(j == 0), stop=(j == i))
                mm.then_inc(ro_ps, 1)

            def cat_transposes(c):
                for i in range(NT):
                    mm = pe.transpose(catT_bank(c)[:, i * P:(i + 1) * P], cat[:, i, c * P:(c + 1) * P], ident)
                mm.then_inc(xT_ps, 1)

            ropes = 0
            for u in range(FRONT - 4):
                s, m = divmod(u, 4)
                pe.wait_ge(lo_done, u + 1)
                if u < 4:
                    pe.wait_ge(act_lo_ok, 2 * u + 2)
                if u == IN_UNITS:
                    pe.wait_ge(act_lo_ok, KC + 4)
                wh, wl = unit_view(w_hi, u % SPLIT, u), unit_view(w_lo, u % SPLIT, u)
                for q in range(4):
                    cut = slice(q * P, (q + 1) * P)
                    to = bank[q]
                    if m == 0 and s:
                        pe.wait_ge(proj_out, 4 * (s - 1) + q + 1)
                    for cc in range(2):
                        k = 2 * m + cc
                        first, last = k == 0, k == KC - 1
                        if s in (AQ, AK):
                            mm = passes(to[:, :], wh[:, cc, cut], wl[:, cc, cut],
                                        act_hi[:, k, :], act_lo[:, k, :], first, last)
                        else:
                            mm = passes(to[:, :], act_hi[:, k, cut], act_lo[:, k, cut],
                                        wh[:, cc, :], wl[:, cc, :], first, last)
                    if m == 3 and q < 3:
                        mm.then_inc(proj_done, 1)
                    if q == 3:
                        mm.then_inc(split_used, 1)
                    n = attention_step(u, q)
                    if n == 0:
                        pe.wait_ge(bias_ok, 4)
                        pe.wait_ge(proj_out, 4 * AV + 4)
                    if (u, q) in ROPE_AT:
                        rope_transposes(ROPE_AT[u, q], 3 * (u - FIRST) + min(q, 3) - 1)
                        ropes += 1
                    if n is not None:
                        if n < STEPS:
                            scores(n)
                        if 1 <= n <= STEPS:
                            turn(n - 1, ropes)
                        if n >= 2:
                            values(n - 2)
                    if retention_sums(u, q) is not None:
                        ret_sums(retention_sums(u, q))
                    if retention_scores(u, q) is not None:
                        ret_scores(*retention_scores(u, q))
                    if u == IN_UNITS - 2:
                        if q == 0:
                            pe.wait_ge(cat_ok, NT)
                        else:
                            pe.wait_ge(act_lo_ok, KC + q)
                        cat_transposes(q)
                if u < 2:
                    for c in range(4 + 2 * u, 6 + 2 * u):
                        x_transposes(c)
                if u == 2:
                    pe.wait_ge(act_lo_ok, KC)
                    line_products()
                if u == BIAS_AT:
                    bias_tiles()
                if u == IN_UNITS + 1:
                    pe.wait_ge(gated, NT)
                    for c in range(4, KC):
                        cat_transposes(c)
                    pe.wait_ge(act_lo_ok, 2 * KC)

            def h_transposes(i):
                pe.wait_ge(h_ok, i + 1)
                for n in (2 * i, 2 * i + 1):
                    if n >= 4:
                        pe.wait_ge(hT_ok, n - 3)
                    for c in range(4):
                        mm = pe.transpose(bank[n % 4][:, c * P:(c + 1) * P],
                                          h_sb[:, i, (4 * (n % 2) + c) * P:(4 * (n % 2) + c + 1) * P], ident)
                    mm.then_inc(hT_ps, 1)

            def logits(i):
                if i == 0:
                    pe.wait_ge(router_in, 64)
                pe.wait_ge(hT_ok, 2 * i + 2)
                for c in range(KC):
                    mm = pe.matmul(bank[4][:, i * NL:(i + 1) * NL], hT[:, c, i * P:(i + 1) * P],
                                   wr[:, c, :], start=(c == 0), stop=(c == KC - 1))
                if i == NT - 1:
                    mm.then_inc(rl_ps, 1)

            for i in range(NT):
                cut = slice(i * P, (i + 1) * P)
                for m in range(4):
                    u = FRONT - 4 + m
                    if i == 0:
                        pe.wait_ge(lo_done, u + 1)
                    wh, wl = unit_view(w_hi, u % SPLIT, u), unit_view(w_lo, u % SPLIT, u)
                    for cc in range(2):
                        k = 2 * m + cc
                        mm = passes(bank[4 + i][:, :], act_hi[:, k, cut], act_lo[:, k, cut],
                                    wh[:, cc, :], wl[:, cc, :], k == 0, k == KC - 1)
                    if i == NT - 1:
                        mm.then_inc(split_used, 1)
                if i < NT - 1:
                    mm.then_inc(proj_done, 1)
                if i == 2:
                    h_transposes(0)
            logits(0)
            h_transposes(1)
            h_transposes(2)
            logits(1)
            logits(2)
            h_transposes(3)
            logits(3)

            pe.wait_ge(m_ok, 2)
            pe.matmul(bank[4][0:NE, 0:1], everyone, ones[:, 0:1], start=True, stop=True).then_inc(count_ps, 1)
            pe.matmul(bank[3][:, 0:NT * NE], before, member.rearrange("p i e -> p (i e)"), start=True, stop=False)
            pe.matmul(bank[3][:, 0:NT * NE], ones, earlier.rearrange("p i e -> p (i e)"), start=False,
                      stop=True).then_inc(rank_ps, 1)
            pe.wait_ge(nt_ok, 1)
            ntl = n_tl[0:NE].rearrange("p i e -> p (i e)")
            pe.matmul(bank[5][:, 0:NE], ntl, e_before, start=True, stop=True)
            pe.matmul(bank[6][0:NE, 0:P], e_upto, ntl, start=True, stop=True)
            pe.matmul(bank[7][0:1, MAXT:MAXT + 1], ones[0:NE, 0:1], ntl[:, 0:1], start=True,
                      stop=True).then_inc(tb_ps, 1)
            pe.wait_ge(le_ok, 1)
            pe.matmul(bank[7][0:1, 0:MAXT], ones[0:NE, 0:1], ends, start=True, stop=True).then_inc(el_ps, 1)

            pe.wait_ge(hot_ok, 1)
            for n in range(2 * NT):
                mm = pe.matmul(bank[2][:, 0:2 * MAXT], row_hot[:, n, :],
                               tile_val[:, n, :, :].rearrange("p w t -> p (w t)"),
                               start=(n == 0), stop=(n == 2 * NT - 1))
            mm.then_inc(list_ps, 1)
            pe.wait_ge(valid_ok, 1)
            pe.matmul(bank[7][0:1, 0:MAXT], ones[:, 0:1], valid, start=True, stop=True)
            for q in range(PIECES):
                mm = pe.matmul(bank[3][0:PIECE, q * MAXT:(q + 1) * MAXT], ident[:, q * PIECE:(q + 1) * PIECE],
                               dest, start=True, stop=True)
            mm.then_inc(valid_ps, 1)

            def gathered(t):
                pe.wait_ge(xg_in, t * 16 * PIECES + 16 * PIECES)
                for c in range(KC):
                    mm = pe.transpose(bank[4 + c // 4][:, (c % 4) * P:(c % 4 + 1) * P],
                                      xg[:, c * P:(c + 1) * P], ident)
                mm.then_inc(xg_ps, 1)

            pe.wait_ge(tlist_ok, 1)
            n_tiles = pe.value_load(tlist[0:1, MAXT:MAXT + 1], min_val=2, max_val=MAXT - 2)
            gathered(0)
            with pe.Fori(0, n_tiles) as t:
                pe.wait_ge(xg_ok, t * 2 + 2)
                pe.wait_ge(hid_ok, t * 2 + 2)

                def gate_up(c, a):
                    slot = (FRONT + c) % SPLIT
                    cut = slice((c % 4) * P, (c % 4 + 1) * P)
                    cols = [w[:, slot, :].rearrange("p (g n) -> p g n", g=2)[:, :, a * 256:(a + 1) * 256]
                            for w in (w_hi, w_lo)]
                    return passes(bank[a][:, :].rearrange("p (g n) -> p g n", g=2), xgT_hi[:, c // 4, cut],
                                  xgT_lo[:, c // 4, cut], cols[0], cols[1], c == 0, c == KC - 1)

                for c in range(KC - 2):
                    pe.wait_ge(lo_done, t * TU + FRONT + c + 1)
                    gate_up(c, 0)
                    gate_up(c, 1).then_inc(split_used, 1)
                pe.wait_ge(lo_done, t * TU + FRONT + KC)
                gate_up(KC - 2, 0)
                gate_up(KC - 1, 0).then_inc(gu_ps, 1)
                gate_up(KC - 2, 1).then_inc(split_used, 1)
                gate_up(KC - 1, 1).then_inc(split_used, 1)

                def turn_hidden(a):
                    pe.wait_ge(hid_ok, t * 2 + a + 3)
                    for k in range(2):
                        mm = pe.transpose(bank[6 + a][:, k * P:(k + 1) * P],
                                          hid[:, (2 * a + k) * P:(2 * a + k + 1) * P], ident)
                    mm.then_inc(hidT_ps, 1)

                turn_hidden(0)
                gathered(t + 1)
                turn_hidden(1)
                pe.wait_ge(y_ok, t + 1)
                for k in range(4):
                    if k % 2 == 0:
                        pe.wait_ge(hidT_ok, t * 2 + k // 2 + 1)
                    pe.wait_ge(lo_done, t * TU + FRONT + KC + k + 1)
                    slot = (FRONT + KC + k) % SPLIT
                    cut = slice(k * P, (k + 1) * P)
                    for a in range(2):
                        cols = slice(a * HALF, (a + 1) * HALF)
                        mm = passes(bank[2 + a][:, :], hidT_hi[:, cut], hidT_lo[:, cut],
                                    w_hi[:, slot, cols], w_lo[:, slot, cols], k == 0, k == 3)
                    mm.then_inc(split_used, 1)

        @block.vector
        def _(dve):
            seq = [0]

            def step(ins):
                seq[0] += 1
                ins.then_inc(dve_seq, 1)
                dve.wait_ge(dve_seq, seq[0])

            def split_lo(u):
                dve.wait_ge(hi_done, u + 1)
                dve.tensor_tensor(w_lo[:, u % SPLIT, :], raw[:, raw_slot(u), :],
                                  w_hi[:, u % SPLIT, :].bitcast(F32), ALU.subtract).then_inc(lo_done, 1)

            def act_lo_of(n):
                c = n % KC
                dve.wait_ge(act_hi_ok, n + 1)
                b = bank[4 + c % 4] if n < KC else catT_bank(c)
                dve.tensor_tensor(act_lo[:, c, :], b[:, :], act_hi[:, c, :].bitcast(F32),
                                  ALU.subtract).then_inc(act_lo_ok, 1)

            dve.memset(tab[:, :], 1.0).then_inc(line_ok, 1)
            for n in range(KC):
                act_lo_of(n)
                if n % 2 and n < 2 * RAW_FRONT - 6:
                    split_lo(n // 2)

            def rope_rows(s, i):
                if i < 3:
                    dve.wait_ge(proj_done, 3 * s + i + 1)
                else:
                    dve.wait_ge(split_used, 4 * s + 4)
                if s == RK:
                    dve.wait_ge(rope_ps, i + 1)
                t = bank[i][:, :].rearrange("p (h a n) -> p h a n", h=HR, a=2)
                o = cat[:, i, HALF:D].rearrange("p (h a n) -> p h a n", h=HR, a=2)
                x1 = rv_sb[:, i, :].rearrange("p (h a n) -> p h a n", h=HR, a=2)
                cos = rope[:, i, 0:1, :].to_broadcast([P, HR, DR // 2])
                sin = rope[:, i, 1:2, :].to_broadcast([P, HR, DR // 2])
                dve.tensor_tensor(o[:, :, 0, :], t[:, :, 0, :], cos, ALU.mult)
                dve.tensor_tensor(o[:, :, 1, :], t[:, :, 1, :], cos, ALU.mult)
                dve.tensor_tensor(x1[:, :, 0, :], t[:, :, 1, :], sin, ALU.mult)
                dve.tensor_tensor(x1[:, :, 1, :], t[:, :, 0, :], sin, ALU.mult).then_inc(proj_out, 1)

            scale = DA ** -0.5

            def logits(n):
                i, h = divmod(n, HA)
                dve.wait_ge(sc_ps, n + 1)
                if n == 0:
                    dve.wait_ge(bias_ok, 4)
                if n >= 2:
                    dve.wait_ge(pT_ps, n - 1)
                lg, s_b = work[:, n % 2, :], bank[4 + n % 2]
                near = max(0, (i - 1) * P)
                if near:
                    dve.tensor_scalar(lg[:, 0:near], s_b[:, 0:near], scale, far[:, h:h + 1],
                                      ALU.mult, ALU.add)
                step(dve.scalar_tensor_tensor(
                    out=lg[:, near:(i + 1) * P], in0=s_b[:, near:(i + 1) * P], scalar=scale,
                    in1=bias_t[:, h, P if i == 0 else 0:2 * P], op0=ALU.mult, op1=ALU.add))
                step(dve.tensor_reduce(small[:, 40 + n % 2:41 + n % 2], lg[:, 0:(i + 1) * P], AX, ALU.max))
                dve.tensor_scalar(small[:, 44 + n % 2:45 + n % 2], small[:, 40 + n % 2:41 + n % 2], -1.0,
                                  None, ALU.mult).then_inc(max_ok, 1)

            def scaled_sums(i):
                dve.wait_ge(o_ps, HA * (i + 1))
                inv = small[:, 48:48 + HA]
                step(dve.reciprocal(inv, small[:, 56 + HA * (i % 2):56 + HA * (i % 2) + HA]))
                a_o = cat[:, i, 0:HALF].rearrange("p (h n) -> p h n", h=HA)
                dve.tensor_tensor(a_o, bank[7][:, :].rearrange("p (h n) -> p h n", h=HA),
                                  inv.unsqueeze(2).to_broadcast([P, HA, DA]), ALU.mult).then_inc(o_ok, 1)
                dve.wait_ge(o_ok, i + 1)

            def decayed(h, j):
                n = NT * h + j
                if n == 0:
                    dve.wait_ge(decay_in, 16)
                dve.wait_ge(rs_ps, n + 1)
                if j == 0 and h:
                    dve.wait_ge(ro_ps, h)
                dve.tensor_tensor(work[:, j, 0:SEQ - j * P], bank[4 + n % 2][:, 0:SEQ - j * P],
                                  decay_t[:, h, 0:SEQ - j * P], ALU.mult).then_inc(rs_ok, 1)

            rcol = small[:, 32:32 + 4]

            def group_norm(h):
                dve.wait_ge(ro_ps, h + 1)
                o = bank[7][:, :].rearrange("p (i n) -> p i n", i=NT)
                for i in range(NT):
                    ins = dve.bn_stats(stats[:, i, 0, :], o[:, i, :])
                step(ins)
                for i in range(NT):
                    ins = dve.bn_aggr(mv[:, i, :], stats[:, i, 0, :])
                step(ins)
                dve.tensor_scalar(small[:, 16:20], mv[:, :, 1], EPS, None, ALU.add).then_inc(r_var, 1)
                dve.wait_ge(r_sqrt, h + 1)
                step(dve.reciprocal(rcol, small[:, 20:24]))
                for i in range(NT):
                    ins = dve.tensor_scalar(cat[:, i, HALF + h * P:HALF + (h + 1) * P], o[:, i, :],
                                            mv[:, i, 0:1], rcol[:, i:i + 1], ALU.subtract, ALU.mult)
                ins.then_inc(ro_ok, 1)

            def rms_sums():
                for i in range(NT):
                    ins = dve.tensor_tensor_reduce(v_sb[:, i, :], cat[:, i, 0:HALF], cat[:, i, 0:HALF], 1.0, 0.0,
                                                   ALU.mult, ALU.add, small[:, 80 + i:81 + i])
                step(ins)
                dve.tensor_scalar(small[:, 84:88], small[:, 80:84], 1.0 / HALF, EPS, ALU.mult,
                                  ALU.add).then_inc(rms_var, 1)

            def rms_normed():
                dve.wait_ge(rms_sqrt, 1)
                step(dve.reciprocal(small[:, 92:96], small[:, 88:92]))
                dve.wait_ge(gain_in, 16)
                for i in range(NT):
                    dve.scalar_tensor_tensor(out=cat[:, i, 0:HALF], in0=cat[:, i, 0:HALF],
                                             scalar=small[:, 92 + i:93 + i], in1=gain_b[:, :],
                                             op0=ALU.mult, op1=ALU.mult).then_inc(cat_ok, 1)

            def half_sums(i, a):
                return dve.bn_stats(stats[:, i, a, :], h_sb[:, i, a * HALF:(a + 1) * HALF])

            def mixed(a, i):
                s = SLICES + a
                if i < 3:
                    dve.wait_ge(proj_done, 3 * s + i + 1)
                else:
                    dve.wait_ge(split_used, 4 * s + 4)
                cols = slice(a * HALF, (a + 1) * HALF)
                return dve.scalar_tensor_tensor(out=h_sb[:, i, cols], in0=h_sb[:, i, cols], scalar=ALPHA,
                                                in1=bank[4 * a + i][:, :], op0=ALU.mult, op1=ALU.add)

            for u in range(FRONT):
                for q in range(4):
                    if q == 1 and 3 <= u + 3 < FRONT:
                        split_lo(u + 3)
                    n = attention_step(u, q)
                    if n is not None and n < STEPS:
                        logits(n)
                    if u // 4 in (RQ, RK) and u % 4 == 3:
                        if u == 4 * RQ + 3 and q == 0:
                            dve.wait_ge(rope_in, 16)
                        rope_rows(u // 4, q)
                    if n is not None and n >= HA + 1 and (n - 1) % HA == 0:
                        scaled_sums((n - 1) // HA - 1)
                    if retention_scores(u, q) is not None:
                        decayed(*retention_scores(u, q))
                    if retention_sums(u, q) is not None:
                        group_norm(retention_sums(u, q))
                    if (u, q) == (2, 3):
                        dve.wait_ge(line_ps, 1)
                        dve.tensor_copy(line_s, bank[4][0:HA, 0:LINE]).then_inc(line_ok, 1)
                        dve.tensor_copy(far, bank[5][:, 0:HA]).then_inc(far_ok, 1)
                    if (u, q) == (IN_UNITS - 4, 2):
                        rms_sums()
                    if (u, q) == (IN_UNITS - 3, 0):
                        rms_normed()
                    if u == IN_UNITS - 2:
                        act_lo_of(KC + q)
                    if u == IN_UNITS:
                        dve.wait_ge(ro_ok, HR)
                        dve.wait_ge(proj_out, 4 * RG + q + 1)
                        dve.tensor_tensor(cat[:, q, HALF:D], cat[:, q, HALF:D], v_sb[:, q, :],
                                          ALU.mult).then_inc(gated, 1)
                    if u == IN_UNITS + 4 + 1:
                        step(mixed(0, q))
                        half_sums(q, 0)
                if u == IN_UNITS + 1:
                    for c in range(4, KC):
                        act_lo_of(KC + c)

            def variance(i, done):
                step(dve.bn_aggr(mv[:, i, :], stats[:, i, :, :]))
                dve.tensor_scalar(small[:, 100 + i:101 + i], mv[:, i, 1:2], EPS, None, ALU.add).then_inc(done, 1)

            def normed(i, g_b, root, done):
                step(dve.scalar_tensor_tensor(out=h_sb[:, i, :], in0=h_sb[:, i, :], scalar=mv[:, i, 0:1],
                                              in1=g_b[:, 0, :], op0=ALU.subtract, op1=ALU.mult))
                dve.wait_ge(root, i + 1)
                step(dve.reciprocal(small[:, 108 + i:109 + i], small[:, 104 + i:105 + i]))
                dve.scalar_tensor_tensor(out=h_sb[:, i, :], in0=h_sb[:, i, :], scalar=small[:, 108 + i:109 + i],
                                         in1=g_b[:, 1, :], op0=ALU.mult, op1=ALU.add).then_inc(done, 1)

            dve.wait_ge(ln1_in, 32)
            for i in range(NT):
                step(mixed(1, i))
                step(half_sums(i, 1))
                variance(i, ln_var)
                normed(i, ln1, ln_sqrt, h_ok)

            def weights_lo(c, t):
                s = (FRONT + c) % SPLIT
                dve.wait_ge(hi_done, t * TU + FRONT + c + 1)
                dve.tensor_tensor(w_lo[:, s, :], raw[:, c, :], w_hi[:, s, :].bitcast(F32),
                                  ALU.subtract).then_inc(lo_done, 1)

            for c in range(SPLIT):
                weights_lo(c, 0)

            dve.wait_ge(rl_ps, 1)
            dve.wait_ge(router_in, 64)
            step(dve.tensor_tensor(logit, bank[4][:, 0:NT * NL].rearrange("p (i e) -> p i e", i=NT),
                                   br.unsqueeze(1).to_broadcast([P, NT, NL]), ALU.add))

            def over(c, n):
                return c.unsqueeze(2).to_broadcast([P, NT, n])

            dve.memset(g_prob[:, :, NG:8], -1.0)
            step(dve.tensor_reduce(col[:, 0, :], logit[:, :, 0:NG], AX, ALU.max))
            dve.tensor_tensor(tmp_a[:, :, 0:NG], logit[:, :, 0:NG], over(col[:, 0, :], NG),
                              ALU.subtract).then_inc(rl_ok, 1)
            dve.wait_ge(r_exp, 1)
            step(dve.tensor_reduce(col[:, 1, :], tmp_b[:, :, 0:NG], AX, ALU.add))
            step(dve.reciprocal(col[:, 2, :], col[:, 1, :]))
            step(dve.tensor_tensor(g_prob[:, :, 0:NG], tmp_b[:, :, 0:NG], over(col[:, 2, :], NG), ALU.mult))
            for i in range(NT):
                ins = dve.max(top[:, 0, i, :], g_prob[:, i, 0:8])
            step(ins)
            for i in range(NT):
                ins = dve.max_index(topi[:, 0, i, :], top[:, 0, i, :], g_prob[:, i, 0:8])
            step(ins)
            dve.tensor_copy(col[:, 3, :], top[:, 0, :, 0])
            step(dve.tensor_copy(col[:, 4, :], topi[:, 0, :, 0]))
            step(dve.tensor_tensor(tmp_a[:, :, 0:NG], iota[:, 0:NG].unsqueeze(1).to_broadcast([P, NT, NG]),
                                   over(col[:, 4, :], NG), ALU.is_equal))
            mask = tmp_a[:, :, 0:NG].unsqueeze(3).to_broadcast([P, NT, NG, EPG])
            step(dve.tensor_tensor(g_mask.rearrange("p i (g e) -> p i g e", g=NG),
                                   logit[:, :, NG:NL].rearrange("p i (g e) -> p i g e", g=NG), mask, ALU.mult))
            eg_log, eg_prob = e_log[:, :, 0:EPG], e_prob[:, :, 0:EPG]
            step(dve.tensor_reduce(eg_log, g_mask.rearrange("p i (g e) -> p i e g", g=NG), AX, ALU.add))
            step(dve.tensor_reduce(col[:, 5, :], eg_log, AX, ALU.max))
            dve.tensor_tensor(eg_log, eg_log, over(col[:, 5, :], EPG), ALU.subtract).then_inc(rl_ok, 1)
            dve.wait_ge(r_exp, 2)
            step(dve.tensor_reduce(col[:, 6, :], eg_prob, AX, ALU.add))
            step(dve.reciprocal(col[:, 7, :], col[:, 6, :]))
            step(dve.tensor_tensor(eg_prob, eg_prob, over(col[:, 7, :], EPG), ALU.mult))
            for i in range(NT):
                ins = dve.max(top[:, 1, i, :], eg_prob[:, i, :])
            step(ins)
            for i in range(NT):
                ins = dve.max_index(topi[:, 1, i, :], top[:, 1, i, :], eg_prob[:, i, :])
            step(ins)
            for j in range(2):
                ins = dve.tensor_copy(col[:, 8 + j, :], topi[:, 1, :, j])
            step(ins)
            for j in range(2):
                ins = dve.scalar_tensor_tensor(out=col[:, 8 + j, :], in0=col[:, 4, :], scalar=float(EPG),
                                               in1=col[:, 8 + j, :], op0=ALU.mult, op1=ALU.add)
            step(ins)
            for j, o in enumerate((pick1, pick2)):
                ins = dve.tensor_tensor(o, iota[:, 0:NE].unsqueeze(1).to_broadcast([P, NT, NE]),
                                        over(col[:, 8 + j, :], NE), ALU.is_equal)
            step(ins)
            step(dve.tensor_tensor(member, pick1, pick2, ALU.add))
            dve.memset(earlier[:, 0, :], 0.0)
            dve.tensor_copy(earlier[:, 1, :], member[:, 0, :])
            step(dve.tensor_tensor(earlier[:, 2, :], member[:, 0, :], member[:, 1, :], ALU.add))
            step(dve.tensor_tensor(earlier[:, 3, :], earlier[:, 2, :], member[:, 2, :], ALU.add))
            dve.tensor_tensor(everyone, earlier[:, 3, :], member[:, 3, :], ALU.add).then_inc(m_ok, 2)
            step(dve.tensor_tensor(col[:, 10, :], top[:, 1, :, 0], top[:, 1, :, 1], ALU.add))
            step(dve.reciprocal(col[:, 11, :], col[:, 10, :]))
            for j in range(2):
                ins = dve.tensor_tensor(col[:, 12 + j, :], top[:, 1, :, j], col[:, 11, :], ALU.mult)
            step(ins)
            for j in range(2):
                ej = entry[:, j * NT:(j + 1) * NT, :]
                dve.tensor_scalar(ej[:, :, 0], token, 2.0, float(j + 1), ALU.mult, ALU.add)
                ins = dve.tensor_tensor(ej[:, :, 1], col[:, 12 + j, :], col[:, 3, :], ALU.mult)
            step(ins)

            dve.wait_ge(count_ps, 1)
            ntl = n_tl[0:NE].rearrange("p i e -> p (i e)")
            over_it, n_col = small[0:NE, 116:116 + NT], small[0:NE, 122:123]
            step(dve.tensor_copy(n_col, bank[4][0:NE, 0:1]))
            step(dve.tensor_scalar(over_it, thresholds[0:NE], n_col, None, ALU.is_lt))
            step(dve.tensor_reduce(n_col, over_it, AX, ALU.add))
            dve.tensor_copy(ntl, n_col.to_broadcast([NE, P])).then_inc(nt_ok, 1)
            dve.wait_ge(rank_ps, 1)
            step(dve.tensor_copy(rank, bank[3][:, 0:NT * NE].rearrange("p (i e) -> p i e", i=NT)))

            def both(a):
                return a.unsqueeze(1).to_broadcast([P, 2, NT, NE])

            step(dve.tensor_tensor(of_rank, picks, both(rank), ALU.mult))
            e_rank, e_tile, e_nth, e_row = (col[:, k:k + 2, :] for k in (14, 16, 18, 20))
            step(dve.tensor_reduce(e_rank, of_rank, AX, ALU.add))
            step(dve.tensor_scalar(e_nth, e_rank, float(P), None, ALU.is_ge))
            for k in range(2, NT):
                step(dve.scalar_tensor_tensor(out=e_nth, in0=e_rank, scalar=float(k * P), in1=e_nth,
                                              op0=ALU.is_ge, op1=ALU.add))
            step(dve.scalar_tensor_tensor(out=e_row, in0=e_nth, scalar=-float(P), in1=e_rank,
                                          op0=ALU.mult, op1=ALU.add))
            dve.tensor_tensor(row_hot, iota.unsqueeze(1).to_broadcast([P, 2 * NT, P]),
                              e_row.rearrange("p j i -> p (j i)").unsqueeze(2).to_broadcast([P, 2 * NT, P]),
                              ALU.is_equal)
            dve.wait_ge(tb_ps, 1)
            dve.tensor_copy(small[0:NE, 120:121], bank[6][0:NE, 0:1])
            step(dve.tensor_copy(rank[:, 0, :], bank[5][:, 0:NE]))
            dve.tensor_scalar(ends, iota[0:NE, 0:MAXT], small[0:NE, 120:121], None, ALU.is_ge).then_inc(le_ok, 1)
            step(dve.tensor_tensor(of_tile, picks, both(rank[:, 0:1, :].to_broadcast([P, NT, NE])), ALU.mult))
            step(dve.tensor_reduce(e_tile, of_tile, AX, ALU.add))
            step(dve.tensor_tensor(e_tile, e_tile, e_nth, ALU.add))
            step(dve.tensor_tensor(tile_hot, iota[:, 0:MAXT].unsqueeze(1).to_broadcast([P, 2 * NT, MAXT]),
                                   e_tile.rearrange("p j i -> p (j i)").unsqueeze(2).to_broadcast([P, 2 * NT, MAXT]),
                                   ALU.is_equal))
            dve.tensor_tensor(tile_val, tile_hot.unsqueeze(2).to_broadcast([P, 2 * NT, 2, MAXT]),
                              entry.unsqueeze(3).to_broadcast([P, 2 * NT, 2, MAXT]), ALU.mult).then_inc(hot_ok, 1)
            dve.wait_ge(el_ps, 1)
            step(dve.tensor_scalar(tlist[0:1, 0:MAXT], bank[7][0:1, 0:MAXT], float(NE - 1), None, ALU.min))
            dve.tensor_copy(tlist[0:1, MAXT:MAXT + 1], bank[7][0:1, MAXT:MAXT + 1]).then_inc(tlist_ok, 1)
            dve.wait_ge(tlist_ok, 1)
            n_tiles = dve.value_load(tlist[0:1, MAXT:MAXT + 1], min_val=2, max_val=MAXT - 2)

            dve.wait_ge(list_ps, 1)
            step(dve.tensor_scalar(valid, bank[2][:, 0:MAXT], 0.0, None, ALU.is_gt))
            step(dve.scalar_tensor_tensor(out=dest, in0=valid, scalar=-float(SKIP), in1=bank[2][:, 0:MAXT],
                                          op0=ALU.mult, op1=ALU.add))
            dve.tensor_scalar(dest, dest, float(SKIP - 1), None, ALU.add).then_inc(valid_ok, 1)
            dve.tensor_copy(weight, bank[2][:, MAXT:2 * MAXT])
            dve.wait_ge(valid_ps, 1)
            dve.tensor_copy(rows_of[0:1, :], bank[7][0:1, 0:MAXT]).then_inc(rows_ok, 1)
            step(dve.tensor_copy(piece_to, bank[3][0:PIECE, 0:PIECES * MAXT].rearrange("p (q t) -> p q t", q=PIECES)))
            dve.tensor_scalar(piece_from, piece_to, 1, None, ALU.logical_shift_right).then_inc(lists_ok, 1)
            dve.memset(sig[:, 0:1], 0.0).then_inc(hid_ok, 2)
            dve.memset(hid[:, 0:1], 0.0).then_inc(y_ok, 1)

            def tokens_lo(n):
                for a in range(2):
                    dve.wait_ge(xg_hi, n + a + 1)
                    dve.tensor_tensor(xgT_lo[:, a, :], bank[4 + a][:, :], xgT_hi[:, a, :].bitcast(F32),
                                      ALU.subtract).then_inc(xg_ok, 1)

            tokens_lo(0)

            def expert(t, first):
                def hidden_lo(a):
                    dve.wait_ge(hidT_hi_ok, t * 2 + a + 1)
                    cut = slice(a * 256, (a + 1) * 256)
                    dve.tensor_tensor(hidT_lo[:, cut], bank[6 + a][:, 0:256], hidT_hi[:, cut].bitcast(F32),
                                      ALU.subtract).then_inc(hidT_ok, 1)

                for c in range(first, TU - 2):
                    weights_lo(c, t)
                for a in range(2):
                    dve.wait_ge(sig_ok, t * 2 + a + 1)
                    cut = slice(a * 256, (a + 1) * 256)
                    dve.tensor_tensor(hid[:, cut], sig[:, cut], bank[a][:, 256:512],
                                      ALU.mult).then_inc(hid_ok, 1)
                hidden_lo(0)
                weights_lo(TU - 2, t)
                hidden_lo(1)
                weights_lo(TU - 1, t)
                tokens_lo(t * 2 + 2)

            expert(0, SPLIT)
            with dve.Fori(1, n_tiles) as t:
                expert(t, 0)

            def summed(i):
                dve.wait_ge(y_in[i], 16)
                yr = raw[:, 2 * i:2 * i + 2, :]
                step(dve.scalar_tensor_tensor(out=h_sb[:, i, 0:HALF], in0=h_sb[:, i, 0:HALF], scalar=ALPHA,
                                              in1=yr[:, 0, 0:HALF], op0=ALU.mult, op1=ALU.add))
                dve.tensor_tensor(h_sb[:, i, 0:HALF], h_sb[:, i, 0:HALF], yr[:, 1, 0:HALF],
                                  ALU.add).then_inc(f_sum, 1)
                dve.wait_ge(y_added, i + 1)
                dve.scalar_tensor_tensor(out=h_sb[:, i, HALF:D], in0=h_sb[:, i, HALF:D], scalar=ALPHA,
                                         in1=yr[:, 0, HALF:D], op0=ALU.mult, op1=ALU.add).then_inc(f_sum, 1)

            def root_and_shift(i):
                dve.wait_ge(f_sqrt, i + 1)
                step(dve.reciprocal(small[:, 108 + i:109 + i], small[:, 104 + i:105 + i]))
                dve.tensor_tensor(small[:, 112 + i:113 + i], small[:, 96 + i:97 + i], small[:, 108 + i:109 + i],
                                  ALU.mult).then_inc(f_root, 1)

            def scaled(i):
                dve.wait_ge(f_norm, i + 1)
                dve.tensor_tensor(h_sb[:, i, :], h_sb[:, i, :], ln2[:, 0, :], ALU.mult).then_inc(f_gain, 1)
                if i >= 2:
                    dve.wait_ge(f_gain, i + 1)
                    dve.tensor_tensor(h_sb[:, i, 0:HALF], h_sb[:, i, 0:HALF], ln2[:, 1, 0:HALF],
                                      ALU.add).then_inc(f_ok, 1)

            dve.memset(small[:, 121:122], EPS).then_inc(eps_ok, 1)
            dve.wait_ge(ln2_in, 32)
            summed(0)
            for i in range(NT):
                if i < NT - 1:
                    summed(i + 1)
                root_and_shift(i)
                if i:
                    scaled(i - 1)
            scaled(NT - 1)

        @block.scalar
        def _(act):
            act.dma_start(mats[:, :], c_mats).then_inc(mats_in, 16)
            act.dma_start(pick, c_pick).then_inc(pick_in, 16)
            act.wait_ge(line_ok, 1)
            act.dma_start(tab[0:BUCKETS, :], rel).then_inc(pick_in, 16)

            def split_hi(u):
                s = raw_slot(u)
                act.wait_ge(raw_in[s], 16 * (u // RAW_FRONT + 1))
                if u >= SPLIT:
                    act.wait_ge(split_used, u - SPLIT + 1)
                act.activation(w_hi[:, u % SPLIT, :], raw[:, s, :], ACT.Copy).then_inc(hi_done, 1)

            def act_hi_of(n):
                c = n % KC
                act.wait_ge(xT_ps, n + 1)
                b = bank[4 + c % 4] if n < KC else catT_bank(c)
                act.activation(act_hi[:, c, :], b[:, :], ACT.Copy).then_inc(act_hi_ok, 1)

            for n in range(KC):
                act_hi_of(n)
                if n % 2 and n < 2 * RAW_FRONT - 6:
                    split_hi(n // 2)
            def rotated(n):
                act.wait_ge(rope_ps, n + 1)
                q, i = divmod(n, NT)
                act.activation(rT[:, q, :, i * P:(i + 1) * P], bank[6][:, :].rearrange("p (h n) -> p h n", h=HR),
                               ACT.Copy).then_inc(rT_ok, 1)

            def slice_out(s, b):
                if b < 3:
                    act.wait_ge(proj_done, 3 * s + b + 1)
                else:
                    act.wait_ge(split_used, 4 * s + 4)
                o, f = {AQ: (qT[:, 0, b, :], ACT.Copy), AK: (qT[:, 1, b, :], ACT.Copy),
                        AV: (v_sb[:, b, :], ACT.Copy), RV: (rv_sb[:, b, :], ACT.Copy),
                        RG: (v_sb[:, b, :], ACT.Silu)}[s]
                act.activation(o, bank[b][:, :], f).then_inc(proj_out, 1)

            def exponentials(n):
                i, h = divmod(n, HA)
                act.wait_ge(max_ok, n + 1)
                if h == 0 and i >= 2:
                    act.wait_ge(o_ok, i - 1)
                a = 56 + HA * (i % 2) + h
                row = work[:, n % 2, 0:(i + 1) * P]
                act.activation(row, row, ACT.Exp, bias=small[:, 44 + n % 2:45 + n % 2],
                               accum_out=small[:, a:a + 1]).then_inc(exp_ok, 1)

            def turned_probs(n):
                i = n // HA
                act.wait_ge(pT_ps, n + 1)
                if n >= 2:
                    act.wait_ge(o_ps, n - 1)
                act.activation(work[:, 2 + n % 2, 0:(i + 1) * P], bank[6][:, 0:(i + 1) * P],
                               ACT.Copy).then_inc(pT_ok, 1)

            for u in range(FRONT):
                for q in range(4):
                    if q == 0 and 3 <= u + 3 < FRONT:
                        split_hi(u + 3)
                    if (u, q) in ROPE_AT:
                        rotated(ROPE_AT[u, q])
                    n = attention_step(u, q)
                    if n is not None and 1 <= n <= STEPS:
                        turned_probs(n - 1)
                    if n is not None and n < STEPS:
                        exponentials(n)
                    if u % 4 == 3 and u // 4 in (AQ, AK, AV, RV, RG):
                        slice_out(u // 4, q)
                    if retention_sums(u, q) is not None:
                        act.wait_ge(r_var, retention_sums(u, q) + 1)
                        act.activation(small[:, 20:24], small[:, 16:20], ACT.Sqrt).then_inc(r_sqrt, 1)
                    if (u, q) == (IN_UNITS - 4, 2):
                        act.wait_ge(rms_var, 1)
                        act.activation(small[:, 88:92], small[:, 84:88], ACT.Sqrt).then_inc(rms_sqrt, 1)
                    if u == IN_UNITS - 2:
                        act_hi_of(KC + q)
                if u == 8:
                    act.dma_start(rope, c_rope.rearrange("(i p) a n -> p i a n", p=P)).then_inc(rope_in, 16)
                    act.dma_start(decay_t, c_decay).then_inc(decay_in, 16)
                if u == 3:
                    act.wait_ge(line_ok, 2)
                    act.dma_start(line_d, line_s).then_inc(line_out, 16)
                if u == 4:
                    act.wait_ge(line_out, 16)
                    act.dma_start(turned_t, bass.AP(tensor=line_d.tensor, offset=line_d.offset,
                                                    ap=[[1, P], [LINE, HA], [1, 2 * P]])).then_inc(bias_in, 16)
                if u == BIAS_AT:
                    for k in range(4):
                        act.wait_ge(bias_ps, k + 1)
                        act.activation(bias_t[:, 2 * k:2 * k + 2, :],
                                       bank[4 + k][:, :].rearrange("p (h n) -> p h n", h=2),
                                       ACT.Copy).then_inc(bias_ok, 1)
                if u == 4 * RV:
                    act.wait_ge(roped, 2 * NT)
                    act.dma_start(gain_b[:, :], gain[0].partition_broadcast(P)).then_inc(gain_in, 16)
                if u == IN_UNITS + 1:
                    for c in range(4, KC):
                        act_hi_of(KC + c)

            def turned_h(n):
                i, a = divmod(n, 2)
                act.wait_ge(hT_ps, n + 1)
                act.activation(hT[:, 4 * a:4 * a + 4, i * P:(i + 1) * P],
                               bank[n % 4][:, :].rearrange("p (c n) -> p c n", c=4), ACT.Copy).then_inc(hT_ok, 1)

            def weights_hi(c, t):
                s = (FRONT + c) % SPLIT
                before_it = FRONT // RAW_FRONT if c < RAW_FRONT else 0
                act.wait_ge(raw_in[c], t * 16 + 16 * (before_it + 1))
                act.wait_ge(split_used, t * TU + FRONT + c - SPLIT + 1)
                act.activation(w_hi[:, s, :], raw[:, c, :], ACT.Copy).then_inc(hi_done, 1)

            for i in range(NT):
                if i == NT - 1:
                    for c in range(SPLIT):
                        weights_hi(c, 0)
                act.wait_ge(ln_var, i + 1)
                act.activation(small[:, 104 + i:105 + i], small[:, 100 + i:101 + i], ACT.Sqrt).then_inc(ln_sqrt, 1)
                if i == 1:
                    turned_h(0)
                    turned_h(1)
            for n in range(2, 2 * NT):
                turned_h(n)
            act.wait_ge(rl_ok, 1)
            act.activation(tmp_b[:, :, 0:NG], tmp_a[:, :, 0:NG], ACT.Exp).then_inc(r_exp, 1)
            act.wait_ge(rl_ok, 2)
            act.activation(e_prob[:, :, 0:EPG], e_log[:, :, 0:EPG], ACT.Exp).then_inc(r_exp, 1)

            def tokens_hi(n, t):
                act.wait_ge(xg_ps, t + 1)
                for a in range(2):
                    act.activation(xgT_hi[:, a, :], bank[4 + a][:, :], ACT.Copy).then_inc(xg_hi, 1)

            def expert(t, first):
                def hidden_hi(a):
                    act.wait_ge(hidT_ps, t * 2 + a + 1)
                    act.activation(hidT_hi[:, a * 256:(a + 1) * 256], bank[6 + a][:, 0:256],
                                   ACT.Copy).then_inc(hidT_hi_ok, 1)

                for c in range(first, TU - 2):
                    weights_hi(c, t)
                    if c == 3:
                        rows_out(t)
                act.wait_ge(gu_ps, t + 1)
                act.activation(sig[:, 0:256], bank[0][:, 0:256], ACT.Silu).then_inc(sig_ok, 1)
                act.wait_ge(split_used, t * TU + FRONT + KC)
                act.activation(sig[:, 256:512], bank[1][:, 0:256], ACT.Silu).then_inc(sig_ok, 1)
                hidden_hi(0)
                weights_hi(TU - 2, t)
                hidden_hi(1)
                weights_hi(TU - 1, t)
                tokens_hi(None, t + 1)

            def rows_out(n):
                act.wait_ge(split_used, n * TU + FRONT)
                act.wait_ge(weight_cur, n)
                for a in range(2):
                    ins = act.activation(y_sb[:, a * HALF:(a + 1) * HALF], bank[2 + a][:, :], ACT.Copy,
                                         scale=s_weight[:, 0:1])
                ins.then_inc(y_ok, 1)

            act.wait_ge(tlist_ok, 1)
            n_tiles = act.value_load(tlist[0:1, MAXT:MAXT + 1], min_val=2, max_val=MAXT - 2)
            tokens_hi(None, 0)
            expert(0, SPLIT)
            with act.Fori(1, n_tiles) as t:
                expert(t, 0)
            rows_out(n_tiles)

            def row_root(i):
                row, used, minus_mean = h_sb[:, i, :], raw[:, 2 * i, :], small[:, 96 + i:97 + i]
                act.wait_ge(f_sum, 2 * i + 2)
                act.activation(used, row, ACT.Copy, scale=-1.0 / D, accum_out=minus_mean).then_inc(f_mean, 1)
                act.wait_ge(f_mean, i + 1)
                act.activation(used, row, ACT.Square, bias=minus_mean,
                               accum_out=small[:, 100 + i:101 + i]).then_inc(f_var, 1)
                act.wait_ge(f_var, i + 1)
                act.activation(small[:, 104 + i:105 + i], small[:, 100 + i:101 + i], ACT.Sqrt, scale=1.0 / D,
                               bias=small[:, 121:122]).then_inc(f_sqrt, 1)

            def row_norm(i):
                act.wait_ge(f_root, i + 1)
                act.activation(h_sb[:, i, :], h_sb[:, i, :], ACT.Identity, bias=small[:, 112 + i:113 + i],
                               scale=small[:, 108 + i:109 + i]).then_inc(f_norm, 1)

            act.wait_ge(eps_ok, 1)
            act.activation(small[:, 123:124], small[:, 121:122], ACT.Sqrt)
            for i in range(NT):
                row_root(i)
                if i:
                    row_norm(i - 1)
            row_norm(NT - 1)

        @block.gpsimd
        def _(pool):
            for n in range(2 * NT):
                s, i = RQ + n // NT, n % NT
                o = cat[:, i, HALF:D].rearrange("p (h a n) -> p h a n", h=HR, a=2)
                x1 = rv_sb[:, i, :].rearrange("p (h a n) -> p h a n", h=HR, a=2)
                pool.wait_ge(proj_out, 4 * s + i + 1)
                pool.tensor_tensor(o[:, :, 0, :], o[:, :, 0, :], x1[:, :, 0, :], ALU.subtract)
                pool.tensor_tensor(o[:, :, 1, :], o[:, :, 1, :], x1[:, :, 1, :], ALU.add).then_inc(roped, 1)
            pool.wait_ge(xT_ps, 2 * KC)
            pool.memset(xg, 0.0).then_inc(xg_zero, 1)
            for i in range(NT):
                pool.wait_ge(h_ok, i + 1)
                pool.dma_start(h_d.rearrange("(i p) n -> i p n", p=P)[i], h_sb[:, i, :]).then_inc(h_out, 16)
            pool.wait_ge(tlist_ok, 1)
            n_tiles = pool.value_load(tlist[0:1, MAXT:MAXT + 1], min_val=2, max_val=MAXT - 2)
            pool.wait_ge(h_out, NT * 16)
            pool.wait_ge(xg_zero, 1)
            pool.memset(s_idx[:, :], SKIP).then_inc(s_idx_ok, 1)
            pool.inc_swdge_sem([y_out], [16])

            last_token, last_row = pool.alloc_register("last_token"), pool.alloc_register("last_row")
            pool.reg_mov(last_token, SEQ - 1)
            pool.reg_mov(last_row, 2 * SEQ - 1)

            def for_pieces(n_rows, copy, done):
                copy(0)
                for q in range(1, PIECES):
                    with pool.If(n_rows > q * PIECE):
                        copy(q)
                    with pool.Else():
                        pool.inc_swdge_sem([done], [16])

            def gather(t, index_ok, count):
                n_rows = pool.value_load(rows_of[0:1, bass.ds(t, 1)], min_val=0, max_val=P)
                pool.wait_ge(lists_ok, 1)
                pool.tensor_copy(g_idx[:, :], piece_from[:, :, bass.ds(t, 1)].rearrange("p q t -> p (q t)")
                                 ).then_inc(index_ok, 1)
                pool.wait_ge(h_out, NT * 16)
                pool.wait_ge(index_ok, count)

                def copy(q):
                    pool.indirect_dma_start(
                        out=xg[q * PIECE:(q + 1) * PIECE, :], out_offset=None, in_=h_d,
                        in_offset=bass.IndirectOffsetOnAxis(ap=g_idx[:, q:q + 1], axis=0),
                        bounds_check=last_token, oob_is_err=False).then_inc(xg_in, 16)

                for_pieces(n_rows, copy, xg_in)

            pool.wait_ge(rows_ok, 1)
            gather(0, g_idx_first, 1)
            pool.wait_ge(xg_ps, 1)
            gather(1, g_idx_ok, 1)
            with pool.Fori(0, n_tiles) as t:
                pool.wait_ge(y_out, t * (16 * PIECES) + 16)
                pool.wait_ge(lists_ok, 1)
                n_rows = pool.value_load(rows_of[0:1, bass.ds(t, 1)], min_val=0, max_val=P)
                pool.tensor_copy(s_weight[:, :], weight[:, bass.ds(t, 1)]
                                 ).then_inc(weight_cur, 1)
                pool.wait_ge(xg_ps, t + 2)
                gather(t + 2, g_idx_ok, t + 2)
                pool.wait_ge(y_ok, t + 2)
                pool.tensor_copy(s_idx[:, :], piece_to[:, :, bass.ds(t, 1)].rearrange("p q t -> p (q t)")
                                 ).then_inc(s_idx_ok, 1)
                pool.wait_ge(lists_ok, 1)
                pool.wait_ge(s_idx_ok, t + 2)

                def copy(q):
                    pool.indirect_dma_start(
                        out=y_d, out_offset=bass.IndirectOffsetOnAxis(ap=s_idx[:, q:q + 1], axis=0),
                        in_=y_sb[q * PIECE:(q + 1) * PIECE, :], in_offset=None, bounds_check=last_row,
                        oob_is_err=False).then_inc(y_out, 16)

                for_pieces(n_rows, copy, y_out)

            def y_sum(i):
                yr = raw[:, 2 * i:2 * i + 2, HALF:D]
                pool.wait_ge(y_in[i], 16)
                pool.tensor_tensor(yr[:, 0, :], yr[:, 0, :], yr[:, 1, :], ALU.add).then_inc(y_added, 1)

            for i in range(NT):
                y_sum(i)
            for i in range(NT):
                pool.wait_ge(f_gain, i + 1)
                cols = slice(0 if i < 2 else HALF, D)
                pool.tensor_tensor(h_sb[:, i, cols], h_sb[:, i, cols], ln2[:, 1, cols],
                                   ALU.add).then_inc(f_added, 1)


_INS = ["x", "w_in", "attn_out_gain", "rel_bias_table", "w_out", "ln1_g", "ln1_b", "w_router_group",
        "b_router_group", "w_router_expert", "b_router_expert", "w_gate_up", "w_down", "ln2_g", "ln2_b"]
_CONSTS = ["c_rope", "c_decay", "c_pick", "c_mats"]


def kernel(**inputs):
    import numpy as _np
    import concourse.bacc as _bacc
    from concourse import mybir as _mybir
    from concourse.bass_utils import run_bass_kernel_spmd as _run

    nc = _bacc.Bacc("TRN2", target_bir_lowering=False, num_devices=1)
    arrays, args = {}, []
    consts = shape_constants()
    for name in _INS + _CONSTS:
        a = _np.ascontiguousarray(inputs[name] if name in _INS else consts[name])
        arrays[f"in_{name}_dram"] = a
        args.append(nc.dram_tensor(f"in_{name}_dram", a.shape, _mybir.dt.from_np(a.dtype), kind="ExternalInput").ap())
    out = nc.dram_tensor("out_0_dram", (1, SEQ, D), _mybir.dt.float32, kind="ExternalOutput").ap()
    layer_kernel(nc, *args, out)
    r = _run(nc, [arrays], core_ids=[0])
    return r.results[0]["out_0_dram"]
```
